# Optimizing a Trainium2 kernel written in Bass

```python
import math
import jax
import jax.numpy as jnp
from jax import lax
import numpy as np

D_MODEL = 2048
BATCH = 1
SEQ = 1024
DEPTH = 1
DEC_BATCH = 8
DEC_SEQ = 16
PAST_LEN = 2048

CHUNK = 64
D_MIX = D_MODEL
D_GROUP = D_MIX // 4
ATT_HEADS = 8
ATT_DH = D_GROUP // ATT_HEADS
BAND = 8
REL_CLIP = 128
ML_HEADS = 4
ML_DH = D_GROUP // ML_HEADS
CONV_W = 3
S5_GROUP_CH = 16
S5_GROUPS = D_GROUP // S5_GROUP_CH
S5_STATE = 64
NORM_EPS = 1e-6
SPLITS = (D_GROUP,) * 4 + (D_GROUP,) * 5 + (2 * ML_HEADS,) + (D_GROUP,) * 4 + (D_GROUP,) * 2
D_IN = 15 * D_GROUP + 2 * ML_HEADS

kernel_name = "hybrid_streaming_encoder_step"

def _rmsnorm(x, g):
    x32 = x.astype(jnp.float32)
    y = x32 * lax.rsqrt(jnp.mean(x32 * x32, axis=-1, keepdims=True) + NORM_EPS)
    return (y * g.astype(jnp.float32)).astype(x.dtype)

def _split(u):
    idx = np.cumsum(np.array(SPLITS))[:-1].tolist()
    return jnp.split(u, idx, axis=-1)

def _rel_bias(rel_bias, n_q, n_k, offset):
    rel = jnp.arange(n_q)[:, None] + offset - jnp.arange(n_k)[None, :]
    idx = jnp.clip(rel, -REL_CLIP, REL_CLIP) + REL_CLIP
    return rel_bias[:, idx].astype(jnp.float32)

def _band_attention_prompt(q, k, v, rel_bias):
    B, S, H, Dh = q.shape
    nc = S // CHUNK
    pad = BAND * CHUNK
    nk = (BAND + 1) * CHUNK
    qc = q.reshape(B, nc, CHUNK, H, Dh)
    kp = jnp.pad(k, ((0, 0), (pad, 0), (0, 0), (0, 0))).reshape(B, nc + BAND, CHUNK, H, Dh)
    vp = jnp.pad(v, ((0, 0), (pad, 0), (0, 0), (0, 0))).reshape(B, nc + BAND, CHUNK, H, Dh)
    kb = jnp.concatenate([kp[:, j:j + nc] for j in range(BAND + 1)], axis=2)
    vb = jnp.concatenate([vp[:, j:j + nc] for j in range(BAND + 1)], axis=2)
    s = jnp.einsum('bcqhd,bckhd->bchqk', qc, kb).astype(jnp.float32) * (Dh ** -0.5)
    s = s + _rel_bias(rel_bias, CHUNK, nk, pad)[None, None]
    kpos = (jnp.arange(nc)[:, None] - BAND) * CHUNK + jnp.arange(nk)[None, :]
    s = jnp.where((kpos >= 0)[None, :, None, None, :], s, -jnp.inf)
    p = jax.nn.softmax(s, axis=-1).astype(v.dtype)
    o = jnp.einsum('bchqk,bckhd->bcqhd', p, vb)
    return o.reshape(B, S, H * Dh)

def _band_attention_sample(q, k, v, k_cache, v_cache, rel_bias):
    B, T, H, Dh = q.shape
    W = k_cache.shape[1]
    k_all = jnp.concatenate([k_cache, k.astype(k_cache.dtype)], axis=1)
    v_all = jnp.concatenate([v_cache, v.astype(v_cache.dtype)], axis=1)
    s = jnp.einsum('bqhd,bkhd->bhqk', q, k_all).astype(jnp.float32) * (Dh ** -0.5)
    s = s + _rel_bias(rel_bias, T, W + T, W)[None]
    p = jax.nn.softmax(s, axis=-1).astype(v_all.dtype)
    o = jnp.einsum('bhqk,bkhd->bqhd', p, v_all).reshape(B, T, H * Dh)
    return o, k_all[:, T:], v_all[:, T:]

def _mlstm_chunk(carry, inp):
    C, n, m = carry
    q, k, v, ig, lf = inp
    L = q.shape[2]
    b = jnp.cumsum(lf, axis=-1)
    causal = jnp.tril(jnp.ones((L, L), dtype=bool))
    d = jnp.where(causal, b[..., :, None] - b[..., None, :] + ig[..., None, :], -jnp.inf)
    m_inter = b + m[..., None]
    m_t = jnp.maximum(m_inter, jnp.max(d, axis=-1))
    w_intra = jnp.exp(d - m_t[..., None]) * jnp.einsum('bhtd,bhsd->bhts', q, k)
    w_inter = jnp.exp(m_inter - m_t)
    num = w_inter[..., None] * jnp.einsum('bhvk,bhtk->bhtv', C, q) + jnp.einsum('bhts,bhsv->bhtv', w_intra, v)
    den = w_inter * jnp.einsum('bhk,bhtk->bht', n, q) + jnp.sum(w_intra, axis=-1)
    h = num / jnp.maximum(jnp.abs(den), jnp.exp(-m_t))[..., None]
    b_last = b[..., -1]
    m_new = jnp.maximum(b_last + m, jnp.max(b_last[..., None] - b + ig, axis=-1))
    ws = jnp.exp(b_last[..., None] - b + ig - m_new[..., None])
    decay = jnp.exp(b_last + m - m_new)
    C_new = decay[..., None, None] * C + jnp.einsum('bhs,bhsv,bhsk->bhvk', ws, v, k)
    n_new = decay[..., None] * n + jnp.einsum('bhs,bhsk->bhk', ws, k)
    return (C_new, n_new, m_new), h

def _mlstm(q, k, v, ig, lf, state):
    B, S, H, Dh = q.shape
    L = CHUNK if S % CHUNK == 0 else S
    nc = S // L

    def chunks(t):
        t = t.astype(jnp.float32).reshape((B, nc, L, H) + t.shape[3:])
        return jnp.moveaxis(t, (1, 3), (0, 2))

    state = tuple(s.astype(jnp.float32) for s in state)
    xs = (chunks(q), chunks(k) * (Dh ** -0.5), chunks(v), chunks(ig), chunks(lf))
    state, h = lax.scan(_mlstm_chunk, state, xs)
    h = jnp.moveaxis(h, (0, 2), (1, 3)).reshape(B, S, H * Dh)
    return h, state

def _short_conv(bg, cg, xin, buf, w):
    S = xin.shape[1]
    u = jnp.concatenate([buf.astype(xin.dtype), cg * xin], axis=1)
    y = sum(w[j] * u[:, j:j + S] for j in range(CONV_W))
    return bg * y, u[:, S:]

def _ssm_combine(e1, e2):
    a1r, a1i, b1r, b1i = e1
    a2r, a2i, b2r, b2i = e2
    return (a2r * a1r - a2i * a1i,
            a2r * a1i + a2i * a1r,
            a2r * b1r - a2i * b1i + b2r,
            a2r * b1i + a2i * b1r + b2i)

def _s5(u, s0_re, s0_im, A_re, A_im, log_dt, B_re, B_im, C_re, C_im, D_skip, w_glu, b_glu):
    Bsz, S, _ = u.shape
    f32 = jnp.float32
    u32 = u.astype(f32)
    ug = u32.reshape(Bsz, S, S5_GROUPS, S5_GROUP_CH)
    A_re, A_im = A_re.astype(f32), A_im.astype(f32)
    dt = jnp.exp(log_dt.astype(f32))[:, None]
    mag = jnp.exp(A_re * dt)
    ab_re, ab_im = mag * jnp.cos(A_im * dt), mag * jnp.sin(A_im * dt)
    den = A_re * A_re + A_im * A_im
    co_re = ((ab_re - 1.0) * A_re + ab_im * A_im) / den
    co_im = (ab_im * A_re - (ab_re - 1.0) * A_im) / den
    B_re, B_im = B_re.astype(f32), B_im.astype(f32)
    bb_re = co_re[..., None] * B_re - co_im[..., None] * B_im
    bb_im = co_re[..., None] * B_im + co_im[..., None] * B_re
    bu_re = jnp.einsum('gpc,bsgc->bsgp', bb_re, ug)
    bu_im = jnp.einsum('gpc,bsgc->bsgp', bb_im, ug)
    s0_re, s0_im = s0_re.astype(f32), s0_im.astype(f32)
    bu_re = bu_re.at[:, 0].add(ab_re * s0_re - ab_im * s0_im)
    bu_im = bu_im.at[:, 0].add(ab_re * s0_im + ab_im * s0_re)
    a_re = jnp.broadcast_to(ab_re, bu_re.shape)
    a_im = jnp.broadcast_to(ab_im, bu_im.shape)
    _, _, x_re, x_im = lax.associative_scan(_ssm_combine, (a_re, a_im, bu_re, bu_im), axis=1)
    y = (jnp.einsum('gcp,bsgp->bsgc', C_re.astype(f32), x_re)
         - jnp.einsum('gcp,bsgp->bsgc', C_im.astype(f32), x_im))
    y = y.reshape(Bsz, S, D_GROUP) + D_skip.astype(f32) * u32
    y = jax.nn.gelu(y)
    y = y * jax.nn.sigmoid(y @ w_glu.astype(f32) + b_glu.astype(f32))
    return y, x_re[:, -1], x_im[:, -1]

def _layer(x, att_cache, ml_state, conv_buf, s5_state, p):
    (g, w_in, w_out, rel_bias, b_if, conv_w, A_re, A_im, log_dt,
     B_re, B_im, C_re, C_im, D_skip, w_glu, b_glu) = p
    Bsz, S, _ = x.shape
    h = _rmsnorm(x, g)
    (aq, ak, av, az, mq, mk, mv, mo, mz, mif, cb, cc, cx, cz, su, sz) = _split(h @ w_in)

    def heads(t, n_h):
        return t.reshape(Bsz, S, n_h, -1)

    aq, ak, av = heads(aq, ATT_HEADS), heads(ak, ATT_HEADS), heads(av, ATT_HEADS)
    if att_cache is None:
        ya = _band_attention_prompt(aq, ak, av, rel_bias)
        rows = min(BAND * CHUNK, S)
        new_k, new_v = ak[:, S - rows:], av[:, S - rows:]
    else:
        ya, new_k, new_v = _band_attention_sample(aq, ak, av, att_cache[0], att_cache[1], rel_bias)
    gates = mif.astype(jnp.float32) + b_if.astype(jnp.float32)
    ym, (C_new, n_new, m_new) = _mlstm(heads(mq, ML_HEADS), heads(mk, ML_HEADS), heads(mv, ML_HEADS),
                                      gates[..., :ML_HEADS], jax.nn.log_sigmoid(gates[..., ML_HEADS:]),
                                      ml_state)
    ym = jax.nn.sigmoid(mo.astype(jnp.float32)) * ym
    yc, conv_new = _short_conv(cb, cc, cx, conv_buf, conv_w)
    ys, s5_re, s5_im = _s5(su, s5_state[0], s5_state[1], A_re, A_im, log_dt,
                           B_re, B_im, C_re, C_im, D_skip, w_glu, b_glu)
    branches = ((ya, az), (ym, mz), (yc, cz), (ys, sz))
    y = jnp.concatenate([(jax.nn.silu(z.astype(jnp.float32)) * yb.astype(jnp.float32)).astype(x.dtype)
                         for yb, z in branches], axis=-1)
    x = x + (y @ w_out).astype(x.dtype)
    return x, (new_k, new_v, C_new, n_new, m_new, conv_new, s5_re, s5_im)

def _stack(states):
    return [jnp.stack(t) for t in zip(*states)]

def setup_inputs(seed: int = 0) -> dict:
    key = jax.random.key(seed)
    ks = jax.random.split(key, 32)
    f32 = jnp.float32

    def nrm(k, shape, scale):
        return jax.random.normal(k, shape, f32) * scale

    att_rows = min(BAND * CHUNK, PAST_LEN)
    b_if = jnp.concatenate([-1.0 + nrm(ks[20], (DEPTH, ML_HEADS), 0.1),
                            3.0 + nrm(ks[21], (DEPTH, ML_HEADS), 0.5)], axis=-1)
    a_im = math.pi * jnp.arange(S5_STATE, dtype=f32)[None, None, :] + nrm(ks[22], (DEPTH, S5_GROUPS, S5_STATE), 0.01)
    log_dt = jax.random.uniform(ks[23], (DEPTH, S5_GROUPS), f32, math.log(0.001), math.log(0.1))
    return {
        "x_prompt": nrm(ks[0], (BATCH, SEQ, D_MODEL), 1.0),
        "x_sample": nrm(ks[1], (DEC_BATCH, DEC_SEQ, D_MODEL), 1.0),
        "cache_attn_k": nrm(ks[2], (DEPTH, DEC_BATCH, att_rows, ATT_HEADS, ATT_DH), 1.0),
        "cache_attn_v": nrm(ks[3], (DEPTH, DEC_BATCH, att_rows, ATT_HEADS, ATT_DH), 1.0),
        "state_mlstm_C": nrm(ks[4], (DEPTH, DEC_BATCH, ML_HEADS, ML_DH, ML_DH), 0.1),
        "state_mlstm_n": nrm(ks[5], (DEPTH, DEC_BATCH, ML_HEADS, ML_DH), 0.1),
        "state_mlstm_m": nrm(ks[6], (DEPTH, DEC_BATCH, ML_HEADS), 0.5),
        "state_conv": nrm(ks[7], (DEPTH, DEC_BATCH, CONV_W - 1, D_GROUP), 1.0),
        "state_s5_re": nrm(ks[8], (DEPTH, DEC_BATCH, S5_GROUPS, S5_STATE), 0.5),
        "state_s5_im": nrm(ks[9], (DEPTH, DEC_BATCH, S5_GROUPS, S5_STATE), 0.5),
        "norm_g": 1.0 + nrm(ks[10], (DEPTH, D_MODEL), 0.02),
        "w_in": nrm(ks[11], (DEPTH, D_MODEL, D_IN), D_MODEL ** -0.5),
        "w_out": nrm(ks[12], (DEPTH, D_MIX, D_MODEL), 0.5 * D_MIX ** -0.5),
        "attn_rel_bias": nrm(ks[13], (DEPTH, ATT_HEADS, 2 * REL_CLIP + 1), 0.1),
        "mlstm_b_if": b_if,
        "conv_w": nrm(ks[14], (DEPTH, CONV_W, D_GROUP), CONV_W ** -0.5),
        "s5_A_re": -0.5 + nrm(ks[15], (DEPTH, S5_GROUPS, S5_STATE), 0.01),
        "s5_A_im": a_im,
        "s5_log_dt": log_dt,
        "s5_B_re": nrm(ks[16], (DEPTH, S5_GROUPS, S5_STATE, S5_GROUP_CH), (2 * S5_GROUP_CH) ** -0.5),
        "s5_B_im": nrm(ks[17], (DEPTH, S5_GROUPS, S5_STATE, S5_GROUP_CH), (2 * S5_GROUP_CH) ** -0.5),
        "s5_C_re": nrm(ks[18], (DEPTH, S5_GROUPS, S5_GROUP_CH, S5_STATE), (2 * S5_STATE) ** -0.5),
        "s5_C_im": nrm(ks[19], (DEPTH, S5_GROUPS, S5_GROUP_CH, S5_STATE), (2 * S5_STATE) ** -0.5),
        "s5_D": nrm(ks[24], (DEPTH, D_GROUP), 0.5),
        "s5_w_glu": nrm(ks[25], (DEPTH, D_GROUP, D_GROUP), D_GROUP ** -0.5),
        "s5_b_glu": nrm(ks[26], (DEPTH, D_GROUP), 0.01),
        "final_norm_g": 1.0 + nrm(ks[27], (D_MODEL,), 0.02),
    }

def reference(x_prompt, x_sample, cache_attn_k, cache_attn_v, state_mlstm_C, state_mlstm_n,
              state_mlstm_m, state_conv, state_s5_re, state_s5_im, norm_g, w_in, w_out,
              attn_rel_bias, mlstm_b_if, conv_w, s5_A_re, s5_A_im, s5_log_dt, s5_B_re, s5_B_im,
              s5_C_re, s5_C_im, s5_D, s5_w_glu, s5_b_glu, final_norm_g):
    f32 = jnp.float32
    Bp = x_prompt.shape[0]
    ml0 = (jnp.zeros((Bp, ML_HEADS, ML_DH, ML_DH), f32), jnp.zeros((Bp, ML_HEADS, ML_DH), f32),
           jnp.zeros((Bp, ML_HEADS), f32))
    conv0 = jnp.zeros((Bp, CONV_W - 1, D_GROUP), x_prompt.dtype)
    s50 = (jnp.zeros((Bp, S5_GROUPS, S5_STATE), f32), jnp.zeros((Bp, S5_GROUPS, S5_STATE), f32))
    xp, xs = x_prompt, x_sample
    st_p, st_s = [], []
    for l in range(DEPTH):
        p = (norm_g[l], w_in[l], w_out[l], attn_rel_bias[l], mlstm_b_if[l], conv_w[l],
             s5_A_re[l], s5_A_im[l], s5_log_dt[l], s5_B_re[l], s5_B_im[l], s5_C_re[l], s5_C_im[l],
             s5_D[l], s5_w_glu[l], s5_b_glu[l])
        xp, sp = _layer(xp, None, ml0, conv0, s50, p)
        xs, ss = _layer(xs, (cache_attn_k[l], cache_attn_v[l]),
                        (state_mlstm_C[l], state_mlstm_n[l], state_mlstm_m[l]),
                        state_conv[l], (state_s5_re[l], state_s5_im[l]), p)
        st_p.append(sp)
        st_s.append(ss)
    y_prompt = _rmsnorm(xp, final_norm_g)
    y_sample = _rmsnorm(xs, final_norm_g)
    (pk, pv, pC, pn, pm, pconv, pre, pim) = _stack(st_p)
    (sk, sv, sC, sn, sm, sconv, sre, sim) = _stack(st_s)
    return (y_prompt, y_sample, pk, pv, pC, pn, pm, pconv, pre, pim,
            sk, sv, sC, sn, sm, sconv, sre, sim)


_drawn_inputs = setup_inputs


def setup_inputs(seed=0):
    import zlib

    import numpy as np

    out = dict(_drawn_inputs(seed))
    spreads = {}
    factors = {'attn_rel_bias': 37.324,
     's5_A_re': 15.51,
     's5_C_re': 3.983,
     's5_C_im': 3.942,
     's5_w_glu': 8.0,
     's5_b_glu': 64.0,
     'final_norm_g': 7.98}
    for name, (base, spread) in spreads.items():
        noise = np.random.default_rng([zlib.crc32(name.encode()), seed]).standard_normal(out[name].shape)
        drawn = base * np.exp(spread * noise) if base else spread * noise
        out[name] = jnp.asarray(drawn.astype(out[name].dtype))
    for name, factor in factors.items():
        out[name] = (out[name] * factor).astype(out[name].dtype)
    return out
```

```python
import concourse.bass as bass
from concourse import mybir
from contextlib import ExitStack

D = 2048
NP, NSTR, DT = 1024, 8, 16
NS = NSTR * DT
NT = NP + NS
TT = NT // 128
KT = D // 128
GC = NT // 3
BAND_KEYS = 640
SK = 512 + DT
LC = 8
NCP = NP // LC
NCS = NS // LC
NC = NCP + NCS
EPS = 1e-6
NEG = -1e30
TWO_PI = 6.283185307179586
PI_LO = 3.1415925

T_GATE = 0
def T_ATT(i, kind): return 1 + 4 * i + kind
def T_ML(i, kind): return 17 + 4 * i + kind
def T_MG(i, kind): return 33 + 2 * i + kind
def T_S5(i, kind): return 41 + 3 * i + kind
def T_CV(i, kind): return 53 + 2 * i + kind
NTILES = 61

def encoder_program(nc, x_all, w_in_t, w_out_t, g_in, g_out, bias_p, bias_s, b_if, m_init,
                    k_cache, v_cache, c_init, n_init, conv_w, conv_buf, s5_par, s5_b, s5_c, s5_s0,
                    s5_d, w_glu, b_glu,
                    y_all, kv_new, k_shift, v_shift, c_prompt, n_prompt, m_last, c_stream,
                    n_stream, conv_p, conv_s, s5_last):
    F = mybir.dt.float32
    R = mybir.dt.float32r
    I32 = mybir.dt.int32
    ACT = mybir.ActivationFunctionType
    ALU = mybir.AluOpType
    AX = mybir.AxisListType.X
    ds = bass.ds

    def dram(name, shape):
        return nc.dram_tensor(name, shape, F, kind="Internal").ap()

    uT = dram("u_scratch", [NTILES, 128, NT])
    yT = dram("y_scratch", [KT, 128, NT])
    rows = dram("gate_rows", [4, 3, NT])
    gS5 = dram("s5_gelu", [4, 128, LC * NC])

    top = ExitStack()
    with top:
        def sem(name):
            return top.enter_context(nc.semaphore(name))

        def sb(stack, name, shape, dt=F):
            return stack.enter_context(nc.sbuf_tensor(name, shape, dt))

        x_in = [sem("x_in0"), sem("x_in1")]
        g_loaded = sem("g_loaded")
        sq_done = sem("sq_done")
        ms_done = sem("ms_done")
        rms_done = sem("rms_done")
        rstd_done = sem("rstd_done")
        xn_done = sem("xn_done")
        xt_mm = sem("xt_mm")
        hhi_done = sem("hhi_done")
        h_done = sem("h_done")
        wraw = [sem("wraw0"), sem("wraw1")]
        whi_done = sem("whi_done")
        w_split = sem("w_split")
        half0_mm = sem("half0_mm")
        bank_full = sem("bank_full")
        evac_done = sem("evac_done")
        u_stored = [sem(f"u_stored{j}") for j in range(3)]
        const_done = sem("const_done")
        outs_done = sem("outs_done")

        ident = sb(top, "ident", [128, 128])
        mask_p = sb(top, "mask_p", [128, 128])
        mask_s = sb(top, "mask_s", [128, 128])
        bmask = sb(top, "bmask", [128, NSTR])
        ones4 = sb(top, "ones4", [4, 128])
        sel = sb(top, "sel", [4, 4, 128])
        onec = sb(top, "onec", [128, 1])
        col = sb(top, "col", [128, TT, 96])
        dec = sb(top, "dec", [128, 4, 16])
        junk = sb(top, "junk", [128, 1])
        G = top.enter_context(nc.psum_tensor("G", [128, 3, 512], F))
        X = top.enter_context(nc.psum_tensor("X", [128, 5, 512], F))
        X2 = X[:, 0:2, :].rearrange("p a n -> p (a n)")
        T2 = X[:, 2:4, :].rearrange("p a n -> p (a n)")

        hstack = ExitStack()
        hhi = sb(hstack, "hhi", [128, KT, NT], R)
        hlo = sb(hstack, "hlo", [128, KT, NT], R)
        wr = sb(hstack, "wr", [128, 2, 8, 128])
        whi = sb(hstack, "whi", [128, 2, 8, 128], R)
        wlo = sb(hstack, "wlo", [128, 2, 8, 128], R)
        ev = sb(hstack, "ev", [128, 3, GC])

        st0 = ExitStack()
        xin = sb(st0, "xin", [128, 2, D])
        gb = sb(st0, "gb", [128, D])
        sqj = sb(st0, "sqj", [128, D])
        stat = sb(st0, "stat", [128, 4, TT])
        st0.close()

        st1 = ExitStack()
        gI = sb(st1, "gI", [4, NT])
        gF = sb(st1, "gF", [4, NT])
        gA = sb(st1, "gA", [4, NT])
        gB = sb(st1, "gB", [4, NT])
        gM = sb(st1, "gM", [4, NT])
        gK = sb(st1, "gK", [4, NT])
        gR = sb(st1, "gR", [96, NT])
        gsm = sb(st1, "gsm", [4, 8, 16])
        gbi = sb(st1, "gbi", [4, 2])
        dsel = sb(st1, "dsel", [4, 4, 16])
        st1.close()

        st2 = ExitStack()
        aq = sb(st2, "aq", [128, NP])
        ak = sb(st2, "ak", [128, NP])
        av = sb(st2, "av", [128, NP])
        az = sb(st2, "az", [128, NP])
        avn = sb(st2, "avn", [128, 8, 128])
        abias = sb(st2, "abias", [128, 2, BAND_KEYS])
        aS = sb(st2, "aS", [128, 2, BAND_KEYS])
        aPT = sb(st2, "aPT", [128, 2, BAND_KEYS])
        ast = sb(st2, "ast", [128, 2, 4])
        st2.close()

        st3 = ExitStack()
        kc = sb(st3, "kc", [128, 4, 512])
        vc = sb(st3, "vc", [128, 4, 512])
        sKT = sb(st3, "sKT", [128, 4, SK])
        sbias = sb(st3, "sbias", [128, SK])
        sS = sb(st3, "sS", [128, SK])
        sPT = sb(st3, "sPT", [128, 512])
        sPN = sb(st3, "sPN", [DT, 128])
        sq = sb(st3, "sq", [128, 4, NS])
        sk = sb(st3, "sk", [128, 4, NS])
        sv = sb(st3, "sv", [128, 4, NS])
        sz = sb(st3, "sz", [128, 4, NS])
        qblk = sb(st3, "qblk", [128, 4, 32])
        svb = sb(st3, "svb", [128, 4, DT])
        vnew = sb(st3, "vnew", [DT, 512])
        sst = sb(st3, "sst", [128, 4])
        st3.close()

        st4 = ExitStack()
        suP = sb(st4, "suP", [128, LC, NC])
        T1 = sb(st4, "T1", [128, NT])
        AC = sb(st4, "AC", [128, 2, LC, 128])
        VT = sb(st4, "VT", [128, 2, LC, 128])
        Kbd = sb(st4, "Kbd", [128, LC, 128])
        E5 = sb(st4, "E5", [128, 2, 4, NCP + 1])
        XS = sb(st4, "XS", [128, 2, 4, NC + 1])
        BC = sb(st4, "BC", [128, 2, 2, 4, 32])
        par = sb(st4, "par", [128, 3, 16])
        sm = sb(st4, "sm", [128, 16, 16])
        smi = sb(st4, "smi", [128, 16], I32)
        PW = sb(st4, "PW", [128, 2, LC + 1, 16])
        E1 = sb(st4, "E1", [128, 2, 16])
        s0 = sb(st4, "s0", [128, 2, 4, 8])
        FO = sb(st4, "FO", [128, 2, 4, 9])
        SX = sb(st4, "SX", [128, 2, 2, 4, 8])
        dD = sb(st4, "dD", [128, 4])
        st4.close()

        st5 = ExitStack()
        mqkv = sb(st5, "mqkv", [128, 2, 3, 4, 128])
        moz = sb(st5, "moz", [128, 2, 4, 128])
        mrow = sb(st5, "mrow", [4, 2, 3, 128])
        gs = sb(st5, "gs", [4, 2, 4, 128])
        q2 = sb(st5, "q2", [128, 4, 128])
        WT = sb(st5, "WT", [128, 4, 128])
        EM = sb(st5, "EM", [128, 4, 128])
        wsk = sb(st5, "wsk", [128, 4, 128])
        vn1 = sb(st5, "vn1", [128, 4, 129])
        CT = sb(st5, "CT", [128, 4, 129])
        hn = sb(st5, "hn", [128, 4, 128])
        yb = sb(st5, "yb", [128, 4, 128])
        md = sb(st5, "md", [128, 2, 4])
        st5.close()

        hstack.close()

        st6 = ExitStack()
        t_qkv = sb(st6, "t_qkv", [128, 5, 4, 128])
        t_row = sb(st6, "t_row", [4, 3, 128])
        t_gs = sb(st6, "t_gs", [4, 2, 4, 128])
        t_q2 = sb(st6, "t_q2", [128, 4, 128])
        t_WT = sb(st6, "t_WT", [128, 4, 128])
        t_EM = sb(st6, "t_EM", [128, 4, 128])
        t_wsk = sb(st6, "t_wsk", [128, 4, 128])
        t_vn1 = sb(st6, "t_vn1", [128, 4, 129])
        t_hn = sb(st6, "t_hn", [128, 4, 128])
        t_yb = sb(st6, "t_yb", [128, 4, 128])
        t_md = sb(st6, "t_md", [128, 2, 4])
        cnat = sb(st6, "cnat", [128, 2, NSTR, 128])
        ct8 = sb(st6, "ct8", [128, 2, NSTR, 129])
        qm = sb(st6, "qm", [128, 2, NSTR * (128 + DT)])
        wkm = sb(st6, "wkm", [128, 2, NSTR, 128])
        nin = sb(st6, "nin", [128, 4, NSTR])
        nout = sb(st6, "nout", [128, 4, NSTR])
        wsm = sb(st6, "wsm", [128, 4, NSTR])
        cv = sb(st6, "cv", [128, 2, 4, NT])
        cub = sb(st6, "cub", [128, 2, NP + 2])
        cus = sb(st6, "cus", [128, 2, NSTR, DT + 2])
        cy = sb(st6, "cy", [128, 2, NT])
        cw = sb(st6, "cw", [128, 3, 4])
        gl = sb(st6, "gl", [128, 4, NT])
        wg = sb(st6, "wg", [128, 4, 512])
        bg = sb(st6, "bg", [128, 4])
        gsz = sb(st6, "gsz", [128, NT])
        gsg = sb(st6, "gsg", [128, NT])
        st6.close()

        st7 = ExitStack()
        yhi = sb(st7, "yhi", [128, KT, GC], R)
        ylo = sb(st7, "ylo", [128, KT, GC], R)
        yr = sb(st7, "yr", [128, 2, 4, GC])
        ohi = sb(st7, "ohi", [128, 2, 8, 512], R)
        olo = sb(st7, "olo", [128, 2, 8, 512], R)
        orw = sb(st7, "orw", [128, 2, 2, 512])
        xo = sb(st7, "xo", [128, 3, D])
        fo = sb(st7, "fo", [128, 3, D])
        go = sb(st7, "go", [128, D])
        fst = sb(st7, "fst", [128, 3, 8])
        st7.close()

        gt_in = sem("gt_in")
        gt_dve = sem("gt_dve")
        gt_act = sem("gt_act")
        gt_mm = sem("gt_mm")
        gt_rows = sem("gt_rows")
        qk_in, v_in, z_in, ab_in = sem("qk_in"), sem("v_in"), sem("z_in"), sem("ab_in")
        s_mm = sem("s_mm")
        s_add = sem("s_add")
        s_max = sem("s_max")
        e_done = sem("e_done")
        r_done = sem("r_done")
        p_done = sem("p_done")
        tp_mm = sem("tp_mm")
        tp_evac = sem("tp_evac")
        o_mm = sem("o_mm")
        y_done = sem("y_done")
        ay_stored = sem("ay_stored")
        ss_in = sem("ss_in")
        kc_in, vc_in = sem("kc_in"), sem("vc_in")
        kt_mm = sem("kt_mm")
        kt_ev = sem("kt_ev")
        kq_done = sem("kq_done")
        vt_mm = sem("vt_mm")
        vt_ev = sem("vt_ev")
        ss_mm = sem("ss_mm")
        ss_add = sem("ss_add")
        ss_max = sem("ss_max")
        ss_e = sem("ss_e")
        ss_r = sem("ss_r")
        ss_p = sem("ss_p")
        pt_mm = sem("pt_mm")
        pt_ev = sem("pt_ev")
        so_mm = sem("so_mm")
        sy_done = sem("sy_done")
        qb_zero = sem("qb_zero")
        s5_in = sem("s5_in")
        su_in, bc_in = sem("su_in"), sem("bc_in")
        s5c = sem("s5c")
        s5a = sem("s5a")
        s5v = sem("s5v")
        su_done = sem("su_done")
        ab_done = sem("ab_done")
        vt5_mm = sem("vt5_mm")
        k5_mm = sem("k5_mm")
        vt5_ev = sem("vt5_ev")
        k5_ev = sem("k5_ev")
        x5_mm = sem("x5_mm")
        ca_done = sem("ca_done")
        xs_done = sem("xs_done")
        y5_mm = sem("y5_mm")
        t1_done = sem("t1_done")
        g5_done = sem("g5_done")
        g5_stored = sem("g5_stored")
        kz_done = sem("kz_done")
        mq_in = [sem("mq_in0"), sem("mq_in1")]
        mo_in = sem("mo_in")
        gs_done = sem("gs_done")
        wb_mm, vn_mm, kn_mm, st_mm, d_mm = (sem(n) for n in ("wb_mm", "vn_mm", "kn_mm", "st_mm", "d_mm"))
        q2_done, wk_done, vn_done = sem("q2_done"), sem("wk_done"), sem("vn_done")
        em_done, wt_done = sem("em_done"), sem("wt_done")
        p_mm, u_mm = sem("p_mm"), sem("u_mm")
        ct_done = sem("ct_done")
        den_c = sem("den_c")
        w_turn = sem("w_turn")
        hn_done = sem("hn_done")
        oz_done = sem("oz_done")
        ht_mm = sem("ht_mm")
        my_done = sem("my_done")
        my_stored = sem("my_stored")
        m_zero = sem("m_zero")
        tq_in, c_in = sem("tq_in"), [sem("c_in0"), sem("c_in1")]
        ctt_mm, ctt_ev = sem("ctt_mm"), sem("ctt_ev")
        qm_done, wkm_done, qz = sem("qm_done"), sem("wkm_done"), sem("qz")
        tp_done, cu_mm, cn_mm = sem("tp_done"), sem("cu_mm"), sem("cn_mm")
        cdec, cu_done, c_out = sem("cdec"), sem("cu_done"), [sem("c_out0"), sem("c_out1")]
        n_done = sem("n_done")
        cv_in, cp_in = [sem("cv_in0"), sem("cv_in1")], sem("cp_in")
        cvc = sem("cvc")
        cv_done = sem("cv_done")
        cv_out = [sem("cv_out0"), sem("cv_out1")]
        gl_in = sem("gl_in")
        gz_in = sem("gz_in")
        gl_mm = sem("gl_mm")
        sg_done = sem("sg_done")
        gm_done = sem("gm_done")
        gy_done = sem("gy_done")
        gy_stored = sem("gy_stored")
        y_in = [sem("y_in0"), sem("y_in1")]
        yhi_done, ylo_done = sem("yhi_done"), sem("ylo_done")
        ow_in = [sem("ow_in0"), sem("ow_in1")]
        ohi_done, olo_done = sem("ohi_done"), sem("olo_done")
        xo_in, go_in = sem("xo_in"), sem("go_in")
        ou_mm = sem("ou_mm")
        ob_mm = sem("ob_mm")
        xa_done = sem("xa_done")
        oq_done = sem("oq_done")
        f_ms, f_rt, f_rs, f_done = sem("f_ms"), sem("f_rt"), sem("f_rs"), sem("f_done")
        f_stored = sem("f_stored")
        kv_out = sem("kv_out")

        def gemm_segs(step, steps, tiles):
            for s in range(step * 6 * tiles // steps, (step + 1) * 6 * tiles // steps):
                yield s // 6, (s % 6) // 3, s % 3

        def outbank(c, a):
            return G[:, a] if c % 2 == 0 else X[:, a]

        class Chain:

            def __init__(self, eng, on, base=0):
                self.eng, self.on, self.base, self.count = eng, on, base, 0

            def __call__(self, ins):
                self.count += 1
                ins.then_inc(self.on, 1)
                self.eng.wait_ge(self.on, self.base + self.count)

        block = top.enter_context(nc.Block())

        @block.sync
        def _(sp):
            def load_w(T, kh):
                sp.wait_ge(w_split, 2 * T + kh + 1)
                sp.dma_start(wr[:, kh], w_in_t[T, :, 8 * kh:8 * kh + 8, :]).then_inc(wraw[kh], 16)

            def store_u(T, j):
                sp.wait_ge(evac_done, 3 * T + j + 4)
                sp.dma_start(uT[T, :, GC * j:GC * j + GC], ev[:, j]).then_inc(u_stored[j], 16)

            def gemm(T, kh, j, more=True):
                if j == 0 and more:
                    load_w(T + 1, kh)
                if kh == 1:
                    store_u(T, j)

            def stored(T):
                for j in range(3):
                    sp.wait_ge(u_stored[j], 16 * T + 32)

            def gemms(base, step, steps, tiles, last=False):
                for t, kh, j in gemm_segs(step, steps, tiles):
                    gemm(base + t, kh, j, not (last and t == tiles - 1))

            sp.dma_start(gb[:, :], g_in).then_inc(g_loaded, 16)

            def load_x(t, s):
                sp.wait_ge(xt_mm, 4 * t + 4)
                sp.dma_start(xin[:, s], x_all[ds(t * 128, 128), :]).then_inc(x_in[s], 16)

            with sp.Fori(0, 4) as i:
                for s in range(2):
                    load_x(2 * i + s, s)
            load_x(8, 0)
            load_w(0, 0)
            load_w(0, 1)
            for kh in range(2):
                for j in range(3):
                    gemm(0, kh, j)
            stored(T_GATE)
            sp.dma_start(gI[:, :], uT[0, 0:4, :]).then_inc(gt_in, 16)
            sp.dma_start(gF[:, :], uT[0, 32:36, :]).then_inc(gt_in, 16)
            sp.dma_start(gbi[:, :], b_if).then_inc(gt_in, 16)
            sp.dma_start(gsm[:, 0, 8:16], m_init).then_inc(gt_in, 16)
            for b in range(NSTR):
                sp.dma_start(k_shift[b], k_cache[b, DT:512, :]).then_inc(outs_done, 16)
                sp.dma_start(v_shift[b], v_cache[b, DT:512, :]).then_inc(outs_done, 16)
            with sp.Fori(0, 4) as i:
                gemms(1 + 4 * i, 0, 1, 4)
            sp.wait_ge(gt_dve, GATE_ROWS)
            sp.wait_ge(gt_act, GATE_WINT)
            sp.dma_start(rows[:, 0, :], gB[:, :]).then_inc(gt_rows, 16)
            sp.dma_start(rows[:, 1, :], gR[0:4, :]).then_inc(gt_rows, 16)
            sp.dma_start(rows[:, 2, :], gA[:, :]).then_inc(gt_rows, 16)
            sp.dma_start(m_last, gsm[:, 2, :]).then_inc(gt_rows, 16)
            stored(T_ATT(3, 3))
            for i in range(4):
                for k in range(2):
                    sp.dma_start(kv_new[i, k], uT[T_ATT(i, 1 + k), :, 512:NT]).then_inc(kv_out, 16)
            sp.wait_ge(gt_rows, 64)
            sp.wait_ge(gt_dve, GATE_END)

            with sp.Fori(0, 4) as i:
                sp.wait_ge(s_mm, 16 * i + 1)
                sp.dma_start(aq[:, :], uT[1 + 4 * i, :, 0:NP]).then_inc(qk_in, 16)
                sp.dma_start(ak[:, :], uT[2 + 4 * i, :, 0:NP]).then_inc(qk_in, 16)
                sp.wait_ge(tp_mm, 17 * i + 1)
                sp.dma_start(av[:, :], uT[3 + 4 * i, :, 0:NP]).then_inc(v_in, 16)
                sp.wait_ge(s_add, 16 * i + 1)
                sp.dma_start(abias[:, :, :], bias_p[ds(2 * i, 2)].rearrange("h p n -> p h n")).then_inc(ab_in, 16)
                sp.wait_ge(ay_stored, 16 * i + 16)
                sp.dma_start(az[:, :], uT[4 + 4 * i, :, 0:NP]).then_inc(z_in, 16)
                for u in range(16):
                    gemms(17 + 4 * i, u, 16, 4)
                sp.wait_ge(y_done, 16 * i + 17)
                sp.dma_start(yT[i, :, 0:NP], az[:, :]).then_inc(ay_stored, 16)
            sp.wait_ge(ay_stored, 80)
            sp.wait_ge(o_mm, 64)
            sp.wait_ge(p_done, 64)
            sp.wait_ge(tp_evac, 69)

            for n, dst in enumerate((sq, sk, sv, sz)):
                for i in range(4):
                    sp.dma_start(dst[:, i], uT[T_ATT(i, n), :, NP:NT]).then_inc(ss_in, 16)
            sp.dma_start(sbias[:, :], bias_s).then_inc(ss_in, 16)
            with sp.Fori(0, 4) as i:
                for s in range(2):
                    b = 2 * i + s
                    sp.wait_ge(kt_mm, 4 * b + 4)
                    sp.dma_start(kc[:, :, :], k_cache[b].rearrange("(t p) n -> p t n", p=128)).then_inc(kc_in, 16)
                    sp.wait_ge(so_mm, b + 1)
                    sp.dma_start(vc[:, :, :], v_cache[b].rearrange("(t p) n -> p t n", p=128)).then_inc(vc_in, 16)
                    gemms(33 + 2 * i, s, 2, 2)
            sp.wait_ge(sy_done, 9)
            for i in range(4):
                sp.dma_start(yT[i, :, NP:NT], sz[:, i]).then_inc(ay_stored, 16)
            sp.wait_ge(ay_stored, 144)
            sp.wait_ge(so_mm, 9)

            sp.dma_start(par[:, :, :], s5_par).then_inc(s5_in, 16)
            sp.dma_start(dD[:, :], s5_d).then_inc(s5_in, 16)
            with sp.Fori(0, 4) as f:
                sp.wait_ge(g5_stored, 32 * f + 16)
                sp.dma_start(T1[:, :], uT[20 + 4 * f]).then_inc(su_in, 16)
                sp.wait_ge(ca_done, f + 1)
                sp.dma_start(BC[:, 0], s5_b[:, :, ds(4 * f, 4), :]).then_inc(bc_in, 16)
                sp.dma_start(BC[:, 1], s5_c[:, :, ds(4 * f, 4), :]).then_inc(bc_in, 16)
                sp.wait_ge(xs_done, f + 1)
                sp.dma_start(s0[:, :, :, :], s5_s0[:, :, ds(4 * f, 4), :]).then_inc(bc_in, 16)
                for u in range(6):
                    gemms(41 + 3 * f, u, 6, 3)
                sp.wait_ge(g5_done, 3 * f + 3)
                sp.dma_start(gS5[f], T1[:, :]).then_inc(g5_stored, 16)
                sp.wait_ge(xs_done, f + 2)
                sp.dma_start(s5_last[:, :, ds(4 * f, 4), :], FO[:, :, :, :]).then_inc(g5_stored, 16)
            sp.wait_ge(g5_stored, 144)
            sp.wait_ge(y5_mm, 12)

            def mlstm(i, last):
                for s in range(2):
                    c = 2 * i + s
                    sp.wait_ge(my_done, c + 1)
                    for n in range(3):
                        sp.dma_start(mqkv[:, s, n], uT[17 + n:30 + n:4, :, ds(c * 128, 128)].rearrange("h p n -> p h n")).then_inc(mq_in[s], 16)
                    sp.dma_start(mrow[:, s], rows[:, :, ds(c * 128, 128)]).then_inc(mq_in[s], 16)
                    sp.wait_ge(my_done, c + 2)
                    for n in range(2):
                        sp.dma_start(moz[:, n], uT[33 + n:40 + n:2, :, ds(c * 128, 128)].rearrange("h p n -> p h n")).then_inc(mo_in, 16)
                    for u in range(3):
                        gemms(53 + 2 * i, 3 * s + u, 6, 2, last)
                    sp.wait_ge(my_done, c + 3)
                    sp.dma_start(yT[4:8, :, ds(c * 128, 128)].rearrange("h p n -> p h n"), yb[:, :, :]).then_inc(my_stored, 16)

            with sp.Fori(0, 3) as i:
                mlstm(i, False)
            mlstm(3, True)
            sp.wait_ge(ct_done, 9)
            sp.dma_start(c_prompt.rearrange("h k v -> k h v"), CT[:, :, 0:128]).then_inc(outs_done, 16)
            sp.dma_start(n_prompt, CT[:, :, 128], allow_slow_non_contiguous=True).then_inc(outs_done, 16)
            sp.wait_ge(outs_done, 16 * 18)
            sp.wait_ge(my_stored, 16 * 9)
            sp.wait_ge(bank_full, 3 * NTILES + 3)
            sp.wait_ge(w_split, 2 * NTILES + 2)
            stored(NTILES - 1)

            for n in range(3):
                sp.dma_start(t_qkv[:, n], uT[17 + n:30 + n:4, :, NP:NT].rearrange("h p n -> p h n")).then_inc(tq_in, 16)
            for n in range(2):
                sp.dma_start(t_qkv[:, 3 + n], uT[33 + n:40 + n:2, :, NP:NT].rearrange("h p n -> p h n")).then_inc(tq_in, 16)
            sp.dma_start(t_row[:, :, :], rows[:, :, NP:NT]).then_inc(tq_in, 16)
            sp.dma_start(nin[:, :, :], n_init).then_inc(tq_in, 16)
            sp.dma_start(cnat[:, 0], c_init[0]).then_inc(c_in[0], 16)
            sp.dma_start(cnat[:, 1], c_init[1]).then_inc(c_in[1], 16)
            sp.dma_start(cw[:, :, :], conv_w).then_inc(cp_in, 16)

            def load_conv(f):
                s = f % 2
                if f >= 2:
                    sp.wait_ge(cv_done, f - 1)
                    sp.wait_ge(cv_out[s], 48)
                sp.dma_start(cv[:, s, 0], uT[T_S5(f, 0)]).then_inc(cv_in[s], 16)
                sp.dma_start(cv[:, s, 1], uT[T_S5(f, 1)]).then_inc(cv_in[s], 16)
                sp.dma_start(cv[:, s, 2], uT[T_CV(f, 0)]).then_inc(cv_in[s], 16)
                sp.dma_start(cv[:, s, 3], uT[T_CV(f, 1)]).then_inc(cv_in[s], 16)
                sp.dma_start(cus[:, s, :, 0:2], conv_buf[f]).then_inc(cv_in[s], 16)

            def store_conv(f):
                s = f % 2
                sp.wait_ge(cv_done, f + 1)
                sp.dma_start(yT[8 + f], cy[:, s]).then_inc(cv_out[s], 16)
                sp.dma_start(conv_p[f], cub[:, s, NP:NP + 2]).then_inc(cv_out[s], 16)
                sp.dma_start(conv_s[f], cus[:, s, :, DT:DT + 2]).then_inc(cv_out[s], 16)

            sp.dma_start(wg[:, :, :], w_glu).then_inc(gl_in, 16)
            sp.dma_start(bg[:, :], b_glu).then_inc(gl_in, 16)
            sp.dma_start(gl[:, :, :], gS5.rearrange("f p n -> p f n")).then_inc(gl_in, 16)
            load_conv(0)
            load_conv(1)
            for f in range(4):
                if f > 0:
                    sp.wait_ge(gy_stored, 16 * f)
                sp.dma_start(gsz[:, :], uT[T_S5(f, 2)]).then_inc(gz_in, 16)
                sp.wait_ge(gy_done, f + 1)
                sp.dma_start(yT[12 + f], gsz[:, :]).then_inc(gy_stored, 16)
            for h in range(4):
                sp.wait_ge(cu_done, h + 1)
                sp.dma_start(c_stream[h], cnat[:, h % 2]).then_inc(c_out[h % 2], 16)
                if h < 2:
                    sp.wait_ge(c_out[h], 16)
                    sp.dma_start(cnat[:, h], c_init[h + 2]).then_inc(c_in[h], 16)
            sp.wait_ge(n_done, 4)
            sp.dma_start(n_stream, nout[:, :, :]).then_inc(outs_done, 16)
            for f in range(4):
                store_conv(f)
                if f < 2:
                    load_conv(f + 2)
            sp.wait_ge(my_done, 11)
            sp.dma_start(yT[4:8, :, NP:NT].rearrange("h p n -> p h n"), t_yb[:, :, :]).then_inc(my_stored, 16)
            sp.wait_ge(outs_done, 16 * 19)
            sp.wait_ge(c_out[0], 32)
            sp.wait_ge(c_out[1], 32)
            sp.wait_ge(gy_stored, 64)
            sp.wait_ge(cv_out[0], 96)
            sp.wait_ge(cv_out[1], 96)
            sp.wait_ge(my_stored, 160)

            sp.dma_start(go[:, :], g_out).then_inc(go_in, 16)

            def load_y(t):
                for p in range(4):
                    sp.wait_ge(ylo_done, 4 * t + p + 1)
                    sp.dma_start(yr[:, p % 2], yT[4 * p:4 * p + 4, :, t * GC:t * GC + GC].rearrange("k p n -> p k n")).then_inc(y_in[p % 2], 16)

            def load_out_w(t, c):
                for p in range(8):
                    sp.wait_ge(olo_done, 32 * t + 8 * c + p + 1)
                    sp.dma_start(orw[:, p % 2], w_out_t[c, :, 2 * p:2 * p + 2, :]).then_inc(ow_in[p % 2], 16)

            load_y(0)
            sp.dma_start(xo[:, :, :], x_all[0:GC, :].rearrange("(a p) n -> p a n", p=128)).then_inc(xo_in, 16)
            load_out_w(0, 0)
            for t in range(3):
                for c in range(4):
                    if c < 3:
                        load_out_w(t, c + 1)
                    elif t < 2:
                        load_y(t + 1)
                        load_out_w(t + 1, 0)
                for a in range(3):
                    sp.wait_ge(f_done, 3 * t + a + 4)
                    sp.dma_start(y_all[(3 * t + a) * 128:(3 * t + a + 1) * 128, :], fo[:, a]).then_inc(f_stored, 16)
                if t < 2:
                    sp.dma_start(xo[:, :, :], x_all[GC * (t + 1):GC * (t + 2), :].rearrange("(a p) n -> p a n", p=128)).then_inc(xo_in, 16)
            sp.wait_ge(f_stored, 16 * 10)
            sp.wait_ge(kv_out, 128)

        @block.gpsimd
        def _(pool):
            g = nc.gpsimd
            for s, n in ((xt_mm, 8), (h_done, 2), (w_split, 2), (half0_mm, 1), (bank_full, 3), (evac_done, 3),
                         (u_stored[0], 16), (u_stored[1], 16), (u_stored[2], 16), (s_mm, 1), (s_add, 1),
                         (tp_mm, 1), (tp_evac, 1), (y_done, 1), (ay_stored, 16), (kt_mm, 4), (so_mm, 1), (sy_done, 1),
                         (g5_stored, 16), (gs_done, 1), (ct_done, 1), (hn_done, 1), (my_done, 2), (my_stored, 16),
                         (ca_done, 1), (xs_done, 1), (t1_done, 3), (sg_done, 3), (ylo_done, 2), (olo_done, 2), (f_done, 3), (f_stored, 16),
                         (xa_done, 6), (ou_mm, 1), (ob_mm, 1), (sq_done, 1)):
                pool.sem_inc(s, n)
            g.memset(ident[:, :], 0.0).then_inc(const_done, 1)
            g.memset(mask_p[:, :], 0.0).then_inc(const_done, 1)
            g.memset(mask_s[:, :], 0.0).then_inc(const_done, 1)
            g.memset(bmask[:, :], 1.0).then_inc(const_done, 1)
            g.memset(ones4[:, :], 1.0).then_inc(const_done, 1)
            g.memset(onec[:, :], 1.0).then_inc(const_done, 1)
            g.memset(sel[:, :, :], 0.0).then_inc(const_done, 1)
            pool.wait_ge(const_done, 7)
            g.affine_select(out=ident[:, :], in_=ident[:, :], compare_op=ALU.not_equal, fill=1.0, base=0,
                            pattern=[[-1, 128]], channel_multiplier=1).then_inc(const_done, 1)
            g.affine_select(out=mask_p[:, :], in_=mask_p[:, :], compare_op=ALU.is_ge, fill=NEG, base=0,
                            pattern=[[1, 128]], channel_multiplier=-1).then_inc(const_done, 1)
            g.affine_select(out=mask_s[:, :], in_=mask_s[:, :], compare_op=ALU.is_ge, fill=NEG, base=0,
                            pattern=[[1, 128]], channel_multiplier=-1).then_inc(const_done, 1)
            g.affine_select(out=bmask[:, :], in_=bmask[:, :], compare_op=ALU.is_ge, fill=0.0, base=0,
                            pattern=[[-DT, NSTR]], channel_multiplier=1).then_inc(const_done, 1)
            g.affine_select(out=sel[:, :, :], in_=sel[:, :, :], compare_op=ALU.not_equal, fill=1.0, base=0,
                            pattern=[[-1, 4], [0, 128]], channel_multiplier=1).then_inc(const_done, 1)
            pool.wait_ge(const_done, 12)
            g.affine_select(out=mask_s[:, :].rearrange("p (b t) -> p b t", t=DT),
                            in_=mask_s[:, :].rearrange("p (b t) -> p b t", t=DT), compare_op=ALU.is_ge, fill=NEG,
                            base=0, pattern=[[-DT, NSTR], [0, DT]], channel_multiplier=1).then_inc(const_done, 1)
            g.affine_select(out=bmask[:, :], in_=bmask[:, :], compare_op=ALU.is_ge, fill=0.0, base=DT - 1,
                            pattern=[[DT, NSTR]], channel_multiplier=-1).then_inc(const_done, 1)
            with pool.Fori(0, NTILES) as T:
                for kh in range(2):
                    pool.wait_ge(wraw[kh], 16 * T + 16)
                    if kh == 0:
                        pool.wait_ge(half0_mm, T + 1)
                    else:
                        pool.wait_ge(bank_full, 3 * T + 3)
                    pool.sem_inc(w_turn, 1)
                    g.tensor_copy(whi[:, kh], wr[:, kh]).then_inc(whi_done, 1)
                    pool.wait_ge(whi_done, 2 * T + kh + 1)
                    g.tensor_tensor(wlo[:, kh], wr[:, kh], whi[:, kh].bitcast(F), ALU.subtract).then_inc(w_split, 1)

        @block.tensor
        def _(pe):
            mm = nc.tensor.matmul
            tr = nc.tensor.transpose

            def gemm(T, kh, j, first=False):
                if j == 0:
                    pe.wait_ge(w_split, 2 * T + kh + 3)
                if first:
                    pe.wait_ge(h_done, 2 + 12 * (j + 1))
                if kh == 0:
                    pe.wait_ge(evac_done, 3 * T + j + 1)
                for k in range(8):
                    kk = 8 * kh + k
                    hs = slice(GC * j, GC * j + GC)
                    mm(G[:, j, 0:GC], whi[:, kh, k], hhi[:, kk, hs], start=(kk == 0), stop=False)
                    mm(G[:, j, 0:GC], whi[:, kh, k], hlo[:, kk, hs], start=False, stop=False)
                    last = mm(G[:, j, 0:GC], wlo[:, kh, k], hhi[:, kk, hs], start=False, stop=(kk == 15))
                if kh == 1:
                    last.then_inc(bank_full, 1)
                elif j == 2:
                    last.then_inc(half0_mm, 1)

            def gemms(base, step, steps, tiles):
                for t, kh, j in gemm_segs(step, steps, tiles):
                    gemm(base + t, kh, j)

            pe.wait_ge(const_done, 14)

            def xpose(t, s):
                pe.wait_ge(xn_done, t + 1)
                for qd in range(4):
                    pe.wait_ge(h_done, 4 * t + qd + 1)
                    for k in range(4):
                        last = tr(X[:, qd % 2, 128 * k:128 * k + 128],
                                  xin[:, s, 512 * qd + 128 * k:512 * qd + 128 * k + 128], ident[:, :])
                    last.then_inc(xt_mm, 1)

            with pe.Fori(0, 4) as i:
                for s in range(2):
                    xpose(2 * i + s, s)
            xpose(8, 0)
            for kh in range(2):
                for j in range(3):
                    gemm(0, kh, j, first=True)
            with pe.Fori(0, 4) as i:
                gemms(1 + 4 * i, 0, 1, 4)
            pe.wait_ge(gt_act, GATE_R)
            for t in range(TT):
                last = tr(X[:, t // 5, 96 * (t % 5):96 * (t % 5) + 96], gR[0:96, 128 * t:128 * t + 128],
                          ident[0:96, 0:96])
            last.then_inc(gt_mm, 1)
            pe.wait_ge(gt_dve, GATE_DSEL)
            mm(X[:, 2, 0:64], ones4[:, :], dsel[:, :, :].rearrange("p a b -> p (a b)"), start=True, stop=True).then_inc(gt_mm, 1)
            pe.wait_ge(gt_dve, GATE_END)

            def span(u):
                g = u % 8
                return g, max(0, g - 4), min(g + 1, 5)

            with pe.Fori(0, 4) as i:
                pe.wait_ge(v_in, 16 * i + 16)
                pe.wait_ge(tp_evac, 17 * i + 1)
                for t in range(8):
                    last = tr(T2[:, 128 * t:128 * t + 128], av[:, 128 * t:128 * t + 128], ident[:, :])
                last.then_inc(tp_mm, 1)
                pe.wait_ge(qk_in, 32 * i + 32)

                def scores(u):
                    g, k0, nk = span(u)
                    ps = slice(64 * (u // 8), 64 * (u // 8) + 64)
                    pe.wait_ge(s_add, 16 * i + u + 1)
                    n = 128 * nk
                    last = mm(X2[:, 0:min(n, 512)], aq[ps, 128 * g:128 * g + 128],
                              ak[ps, 128 * k0:128 * k0 + min(n, 512)], start=True, stop=True)
                    if n > 512:
                        last = mm(X2[:, 512:n], aq[ps, 128 * g:128 * g + 128],
                                  ak[ps, 128 * k0 + 512:128 * k0 + n], start=True, stop=True)
                    last.then_inc(s_mm, 1)

                scores(0)
                for u in range(16):
                    g, k0, nk = span(u)
                    ps = slice(64 * (u // 8), 64 * (u // 8) + 64)
                    if u < 15:
                        scores(u + 1)
                    pe.wait_ge(p_done, 16 * i + u + 1)
                    pe.wait_ge(tp_evac, 17 * i + u + 2)
                    for t in range(nk):
                        last = tr(T2[:, 128 * t:128 * t + 128], aS[:, u % 2, 128 * t:128 * t + 128], ident[:, :])
                    last.then_inc(tp_mm, 1)
                    gemms(17 + 4 * i, u, 16, 4)
                    pe.wait_ge(tp_evac, 17 * i + u + 3)
                    pe.wait_ge(y_done, 16 * i + u + 1)
                    for t in range(nk):
                        last = mm(X[ps, 4, 0:128], avn[:, k0 + t, 64 * (u // 8):64 * (u // 8) + 64],
                                  aPT[:, u % 2, 128 * t:128 * t + 128], start=(t == 0), stop=(t == nk - 1))
                    last.then_inc(o_mm, 1)

            pe.wait_ge(s_add, 65)
            pe.wait_ge(y_done, 65)
            pe.wait_ge(ss_in, 16 * 17)
            with pe.Fori(0, 4) as i:
                for s in range(2):
                    b = 2 * i + s
                    pe.wait_ge(kc_in, 16 * b + 16)
                    pe.wait_ge(sy_done, b + 1)
                    for t in range(4):
                        for hp in range(4):
                            last = tr(X[:, t, 128 * hp:128 * hp + 128], kc[:, t, 128 * hp:128 * hp + 128], ident[:, :])
                        last.then_inc(kt_mm, 1)
                    pe.wait_ge(kq_done, 4 * b + 1)
                    for hp in range(4):
                        last = tr(X[0:DT, 4, 128 * hp:128 * hp + 128], svb[:, hp], ident[:, :])
                    last.then_inc(vt_mm, 1)
                    tg = list(gemm_segs(s, 2, 2))
                    for t, kh, j in tg[:2]:
                        gemm(33 + 2 * i + t, kh, j)
                    pe.wait_ge(kt_ev, 4 * b + 4)
                    pe.wait_ge(kq_done, 4 * b + 4)
                    for hp in range(4):
                        mm(X2[32 * hp:32 * hp + 32, 0:512], qblk[:, hp], sKT[:, hp, 0:512], start=True, stop=True)
                    for hp in range(4):
                        last = mm(X2[32 * hp:32 * hp + 32, 512:SK], qblk[:, hp], sKT[:, hp, 512:SK], start=True, stop=True)
                    last.then_inc(ss_mm, 1)
                    for t, kh, j in tg[2:4]:
                        gemm(33 + 2 * i + t, kh, j)
                    pe.wait_ge(ss_p, b + 1)
                    for t in range(4):
                        tr(X[:, 2, 128 * t:128 * t + 128], sS[:, 128 * t:128 * t + 128], ident[:, :])
                    tr(X[0:DT, 3, 0:128], sS[:, 512:SK], ident[:, :]).then_inc(pt_mm, 1)
                    pe.wait_ge(vc_in, 16 * b + 16)
                    pe.wait_ge(vt_ev, b + 1)
                    for t, kh, j in tg[4:6]:
                        gemm(33 + 2 * i + t, kh, j)
                    pe.wait_ge(pt_ev, 2 * b + 2)
                    for hp in range(4):
                        for t in range(4):
                            mm(X[:, 4, 32 * hp:32 * hp + 32], vc[:, t, 128 * hp:128 * hp + 128],
                               sPT[:, 128 * t + 32 * hp:128 * t + 32 * hp + 32], start=(t == 0), stop=False)
                        last = mm(X[:, 4, 32 * hp:32 * hp + 32], vnew[:, 128 * hp:128 * hp + 128],
                                  sPN[:, 32 * hp:32 * hp + 32], start=False, stop=True)
                    last.then_inc(so_mm, 1)

            pe.wait_ge(sy_done, 9)
            with pe.Fori(0, 4) as f:
                pe.wait_ge(ab_done, f + 1)
                pe.wait_ge(t1_done, 3 * f + 3)
                for ri in range(2):
                    for hf in range(2):
                        for t in range(4):
                            last = tr(X[:, 2 * ri + hf, 128 * t:128 * t + 128], AC[:, ri, 4 * hf + t], ident[:, :])
                        last.then_inc(vt5_mm, 1)
                for t in range(LC):
                    for st in range(4):
                        o = X[32 * st:32 * st + 32, 4, 32 * t:32 * t + 32]
                        mm(o, AC[:, 0, t, 32 * st:32 * st + 32], BC[:, 1, 0, st], start=True, stop=False)
                        last = mm(o, AC[:, 1, t, 32 * st:32 * st + 32], BC[:, 1, 1, st], start=False, stop=True)
                last.then_inc(k5_mm, 1)
                gemms(41 + 3 * f, 0, 3, 3)
                pe.wait_ge(vt5_ev, 4 * f + 4)
                pe.wait_ge(su_done, 2 * f + 2)
                for st in range(4):
                    ps = slice(32 * st, 32 * st + 32)
                    for ri in range(2):
                        for j in range(LC):
                            last = mm(X[:, st, NC * ri:NC * ri + NC], VT[ps, ri, LC - 1 - j], suP[ps, j],
                                      start=(j == 0), stop=(j == LC - 1))
                last.then_inc(x5_mm, 1)
                gemms(41 + 3 * f, 1, 3, 3)
                pe.wait_ge(k5_ev, f + 1)
                pe.wait_ge(ca_done, f + 2)
                pe.wait_ge(xs_done, f + 2)
                for bk, (i0, i1) in enumerate(((0, 3), (3, 6), (6, 8))):
                    for st in range(4):
                        for i in range(i0, i1):
                            for ri in range(2):
                                mm(X[32 * st:32 * st + 32, bk, NC * (i - i0):NC * (i - i0) + NC],
                                   AC[:, ri, i, 32 * st:32 * st + 32], XS[:, ri, st, 0:NC],
                                   start=(i == i0 and ri == 0), stop=False)
                    for t in range(i1 - 1, -1, -1):
                        a = max(i0, t)
                        last = mm(X[:, bk, NC * (a - i0):NC * (i1 - i0)], Kbd[:, t],
                                  suP[:, a - t:i1 - t].rearrange("p a n -> p (a n)"), start=False, stop=(t == 0))
                    last.then_inc(y5_mm, 1)
                gemms(41 + 3 * f, 2, 3, 3)

            def ml_front(c, qkv, row, g2, mask, waits):
                pe.wait_ge(gs_done, c + 2)
                waits()
                mm(X[:, 2], ones4[:, :], g2[:, 1].rearrange("p a b -> p (a b)"), start=True, stop=True).then_inc(wb_mm, 1)
                for h in range(4):
                    last = tr(X[:, 3, 128 * h:128 * h + 128], qkv[2][:, h], ident[:, :])
                last.then_inc(vn_mm, 1)
                for h in range(4):
                    last = tr(X[:, 4, 128 * h:128 * h + 128], qkv[1][:, h], ident[:, :])
                last.then_inc(kn_mm, 1)
                for h in range(4):
                    last = mm(X[:, 0, 128 * h:128 * h + 128], qkv[1][:, h], qkv[0][:, h], start=True, stop=True)
                last.then_inc(st_mm, 1)
                for h in range(4):
                    mm(X[:, 1, 128 * h:128 * h + 128], ident[:, :], mask[:, :], start=(h == 0), stop=False)
                mm(X[:, 1], row[:, 2], sel[:, :, :].rearrange("p a b -> p (a b)"), start=False, stop=False)
                last = mm(X[:, 1], ones4[:, :], g2[:, 0].rearrange("p a b -> p (a b)"), start=False, stop=True)
                last.then_inc(d_mm, 1)

            pe.wait_ge(t1_done, 15)
            with pe.Fori(0, 4) as i:
                for s in range(2):
                    c = 2 * i + s

                    def waits():
                        pe.wait_ge(mq_in[s], 64 * i + 64)
                        pe.wait_ge(ct_done, c + 1)
                        pe.wait_ge(hn_done, c + 1)
                        pe.wait_ge(my_done, c + 2)

                    ml_front(c, [mqkv[:, s, n] for n in range(3)], mrow[:, s], gs, mask_p, waits)
                    gemms(53 + 2 * i, 3 * s, 6, 2)
                    pe.wait_ge(q2_done, c + 1)
                    pe.wait_ge(wt_done, c + 1)
                    pe.wait_ge(vn_done, c + 1)
                    for h in range(4):
                        o = X[:, 2 + h // 2, 129 * (h % 2):129 * (h % 2) + 129]
                        mm(o, q2[:, h], CT[:, h], start=True, stop=False)
                        last = mm(o, WT[:, h], vn1[:, h], start=False, stop=True)
                    last.then_inc(p_mm, 1)
                    pe.wait_ge(wk_done, c + 1)
                    for h in range(4):
                        last = mm(X[:, 4 * (h // 2), 129 * (h % 2):129 * (h % 2) + 129], wsk[:, h], vn1[:, h],
                                  start=True, stop=True)
                    last.then_inc(u_mm, 1)
                    gemms(53 + 2 * i, 3 * s + 1, 6, 2)
                    pe.wait_ge(hn_done, c + 2)
                    for h in range(4):
                        last = tr(X[:, 1, 128 * h:128 * h + 128], hn[:, h], ident[:, :])
                    last.then_inc(ht_mm, 1)
                    gemms(53 + 2 * i, 3 * s + 2, 6, 2)

            pe.wait_ge(gl_in, 48)
            for f in range(4):
                for j in range(3):
                    pe.wait_ge(sg_done, 3 * f + j + 1)
                    for k in range(4):
                        last = mm(G[:, j, 0:GC], wg[:, k, 128 * f:128 * f + 128], gl[:, k, GC * j:GC * j + GC],
                                  start=(k == 0), stop=(k == 3))
                    last.then_inc(gl_mm, 1)

            def waits():
                pe.wait_ge(tq_in, 16 * 7)
                pe.wait_ge(ct_done, 9)
                pe.wait_ge(hn_done, 9)
                pe.wait_ge(my_done, 10)

            ml_front(8, [t_qkv[:, n] for n in range(3)], t_row, t_gs, mask_s, waits)
            pe.wait_ge(q2_done, 9)
            pe.wait_ge(wt_done, 9)
            pe.wait_ge(vn_done, 9)
            pe.wait_ge(wk_done, 9)
            for h in range(4):
                pe.wait_ge(c_in[h % 2], 16 * (h // 2) + 16)
                if h:
                    pe.wait_ge(cu_done, h)
                for hf in range(2):
                    for b in range(4):
                        last = tr(X[:, hf, 128 * b:128 * b + 128], cnat[:, h % 2, 4 * hf + b], ident[:, :])
                    last.then_inc(ctt_mm, 1)
                pe.wait_ge(ctt_ev, 3 * h + 3)
                pe.wait_ge(qm_done, h + 1)
                o = X[:, 2 + h // 2, 129 * (h % 2):129 * (h % 2) + 129]
                for b in range(NSTR):
                    mm(o, qm[:, h % 2, 128 * b:128 * b + 128], ct8[:, h % 2, b], start=(b == 0), stop=False)
                mm(o, t_WT[:, h], t_vn1[:, h], start=False, stop=True).then_inc(tp_done, 1)
                pe.wait_ge(wkm_done, h + 1)
                for hf in range(2):
                    last = mm(X[:, hf], t_vn1[:, h, 0:128],
                              wkm[:, h % 2, 4 * hf:4 * hf + 4].rearrange("p b k -> p (b k)"), start=True, stop=True)
                last.then_inc(cu_mm, 1)
                if h:
                    pe.wait_ge(n_done, h)
                for b in range(NSTR):
                    last = mm(X[:, 4, b:b + 1], wkm[:, h % 2, b], onec[:, :], start=True, stop=True)
                last.then_inc(cn_mm, 1)
            pe.wait_ge(hn_done, 10)
            pe.wait_ge(cu_done, 4)
            for h in range(4):
                last = tr(X[:, 1, 128 * h:128 * h + 128], t_hn[:, h], ident[:, :])
            last.then_inc(ht_mm, 1)
            pe.wait_ge(my_done, 11)
            pe.wait_ge(sg_done, 15)

            with pe.Fori(0, 3) as t:
                for c in range(4):
                    for kh in range(2):
                        pe.wait_ge(olo_done, 32 * t + 8 * c + 4 * kh + 6)
                        if c == 0:
                            pe.wait_ge(ylo_done, 4 * t + 2 * kh + 4)
                        for a in range(3):
                            o = outbank(c, a)
                            if kh == 0:
                                pe.wait_ge(xa_done, 12 * t + 3 * c + a + 1)
                            for k in range(8):
                                kk = 8 * kh + k
                                ysl = slice(128 * a, 128 * a + 128)
                                mm(o, yhi[:, kk, ysl], ohi[:, kh, k], start=(kk == 0), stop=False)
                                mm(o, ylo[:, kk, ysl], ohi[:, kh, k], start=False, stop=False)
                                last = mm(o, yhi[:, kk, ysl], olo[:, kh, k], start=False, stop=(kk == 15))
                            if kh == 1:
                                last.then_inc(ob_mm, 1)
                        if kh == 0:
                            last.then_inc(ou_mm, 1)

        @block.scalar
        def _(act):
            fn = nc.scalar.activation

            def evac(T, kh, j, func, scale=1.0):
                if kh == 1:
                    act.wait_ge(bank_full, 3 * T + j + 4)
                    act.wait_ge(u_stored[j], 16 * T + 16)
                    fn(ev[:, j], G[:, j, 0:GC], func, scale=scale).then_inc(evac_done, 1)

            def evacs(base, step, steps, funcs):
                for t, kh, j in gemm_segs(step, steps, len(funcs)):
                    evac(base + t, kh, j, *funcs[t])

            COPY, SILU, SIGM = (ACT.Copy,), (ACT.Silu,), (ACT.Sigmoid,)

            def rms(t, s, n):
                act.wait_ge(x_in[s], n)
                act.wait_ge(sq_done, t + 1)
                fn(sqj[:, :], xin[:, s], ACT.Square, accum_out=stat[:, 0, ds(t, 1)]).then_inc(sq_done, 1)
                act.wait_ge(ms_done, t + 1)
                fn(stat[:, 2, ds(t, 1)], stat[:, 1, ds(t, 1)], ACT.Sqrt).then_inc(rms_done, 1)

            def high(t):
                for qd in range(4):
                    act.wait_ge(xt_mm, 4 * t + qd + 9)
                    fn(hhi[:, 4 * qd:4 * qd + 4, ds(t * 128, 128)], X[:, qd % 2].rearrange("p (k n) -> p k n", k=4),
                       ACT.Copy).then_inc(hhi_done, 1)

            rms(0, 0, 16)
            with act.Fori(0, 4) as i:
                rms(2 * i + 1, 1, 16 * i + 16)
                high(2 * i)
                rms(2 * i + 2, 0, 16 * i + 32)
                high(2 * i + 1)
            high(8)
            for kh in range(2):
                for j in range(3):
                    evac(0, kh, j, ACT.Copy)
            act.wait_ge(gt_dve, 4)
            fn(gB[:, :], gA[:, :], ACT.Exp, scale=-1.0).then_inc(gt_act, 1)
            act.wait_ge(gt_act, 1)
            fn(gB[:, :], gB[:, :], ACT.Ln, bias=1.0).then_inc(gt_act, 1)
            act.wait_ge(gt_dve, GATE_ARGS)
            fn(gR[0:4, :], gF[:, :], ACT.Exp).then_inc(gt_act, 1)
            fn(gR[32:36, :], gM[:, :], ACT.Exp, scale=-1.0).then_inc(gt_act, 1)
            fn(gR[64:68, :], gK[:, :], ACT.Exp).then_inc(gt_act, 1)
            fn(gsm[:, 5, :], gsm[:, 4, :], ACT.Exp).then_inc(gt_act, 1)
            with act.Fori(0, 4) as i:
                evacs(1 + 4 * i, 0, 1, [COPY, COPY, COPY, SILU])

            with act.Fori(0, 4) as i:
                act.wait_ge(tp_mm, 17 * i + 2)
                fn(avn[:, :, :].rearrange("p a n -> p (a n)"), T2, ACT.Copy).then_inc(tp_evac, 1)

                def exps(u):
                    n = 128 * min(u % 8 + 1, 5)
                    act.wait_ge(s_max, 16 * i + u + 1)
                    fn(aS[:, u % 2, 0:n], aS[:, u % 2, 0:n], ACT.Exp, bias=ast[:, u % 2, 0:1],
                       accum_out=ast[:, u % 2, 1:2]).then_inc(e_done, 1)

                exps(0)
                for u in range(16):
                    n = 128 * min(u % 8 + 1, 5)
                    act.wait_ge(tp_mm, 17 * i + u + 3)
                    fn(aPT[:, u % 2, 0:n], T2[:, 0:n], ACT.Copy).then_inc(tp_evac, 1)
                    if u < 15:
                        exps(u + 1)
                    evacs(17 + 4 * i, u, 16, [COPY, (ACT.Copy, 128 ** -0.5), COPY, COPY])

            with act.Fori(0, 4) as i:
                for s in range(2):
                    b = 2 * i + s
                    for t in (0, 2):
                        act.wait_ge(kt_mm, 4 * b + t + 5)
                        fn(sKT[:, :, 128 * t:128 * t + 128], X[:, t].rearrange("p (h n) -> p h n", h=4),
                           ACT.Copy).then_inc(kt_ev, 1)
                    act.wait_ge(vt_mm, b + 1)
                    fn(vnew[:, :], X[0:DT, 4], ACT.Copy).then_inc(vt_ev, 1)
                    act.wait_ge(ss_max, b + 1)
                    fn(sS[:, :], sS[:, :], ACT.Exp, bias=sst[:, 0:1], accum_out=sst[:, 1:2]).then_inc(ss_e, 1)
                    act.wait_ge(pt_mm, b + 1)
                    fn(sPT[:, :], X[:, 2], ACT.Copy).then_inc(pt_ev, 1)
                    fn(sPN[:, :], X[0:DT, 3, 0:128], ACT.Copy).then_inc(pt_ev, 1)
                    evacs(33 + 2 * i, s, 2, [SIGM, SILU])

            act.wait_ge(s5_in, 32)
            fn(sm[:, 0], par[:, 2], ACT.Exp).then_inc(s5a, 1)
            act.wait_ge(s5v, 1)
            fn(sm[:, 3], sm[:, 1], ACT.Exp).then_inc(s5a, 1)
            fn(sm[:, 4], sm[:, 1], ACT.Exp, scale=float(LC)).then_inc(s5a, 1)
            act.wait_ge(s5v, 2)
            fn(sm[:, 8], sm[:, 5], ACT.Sin).then_inc(s5a, 1)
            fn(sm[:, 9], sm[:, 6], ACT.Sin).then_inc(s5a, 1)
            fn(sm[:, 10], sm[:, 7], ACT.Sin).then_inc(s5a, 1)
            fn(sm[:, 11], sm[:, 2], ACT.Sin).then_inc(s5a, 1)
            with act.Fori(0, 4) as f:
                act.wait_ge(su_in, 16 * f + 16)
                act.wait_ge(t1_done, 3 * f + 3)
                fn(suP[:, :, 0:NCS], T1[:, NP:NT].rearrange("p (n i) -> p i n", i=LC), ACT.Copy).then_inc(su_done, 1)
                fn(suP[:, :, NCS:NC], T1[:, 0:NP].rearrange("p (n i) -> p i n", i=LC), ACT.Copy).then_inc(su_done, 1)
                act.wait_ge(s5c, S5_PREP + f * S5_STEPS + S5_TABLES)
                for e in (0, 2):
                    act.wait_ge(vt5_mm, 4 * f + e + 1)
                    fn(VT[:, e // 2, 4 * (e % 2):4 * (e % 2) + 4].rearrange("p a n -> p (a n)"), X[:, e],
                       ACT.Copy).then_inc(vt5_ev, 1)
                evacs(41 + 3 * f, 0, 3, [COPY, COPY, SILU])
                evacs(41 + 3 * f, 1, 3, [COPY, COPY, SILU])
                for bk in range(3):
                    act.wait_ge(t1_done, 3 * f + bk + 4)
                    fs = slice(432 * bk, min(432 * bk + 432, NT))
                    fn(T1[:, fs], T1[:, fs], ACT.Gelu_apprx_tanh).then_inc(g5_done, 1)
                evacs(41 + 3 * f, 2, 3, [COPY, COPY, SILU])

            with act.Fori(0, 4) as i:
                for s in range(2):
                    c = 2 * i + s
                    act.wait_ge(vn_mm, c + 1)
                    fn(vn1[:, :, 0:128], X[:, 3].rearrange("p (h n) -> p h n", h=4), ACT.Copy).then_inc(vn_done, 1)
                    act.wait_ge(d_mm, c + 1)
                    fn(EM[:, :, :].rearrange("p h n -> p (h n)"), X[:, 1], ACT.Exp).then_inc(em_done, 1)
                    for u in range(3):
                        evacs(53 + 2 * i, 3 * s + u, 6, [COPY, SILU])

            for f in range(4):
                for j in range(3):
                    act.wait_ge(gl_mm, 3 * f + j + 1)
                    if f:
                        act.wait_ge(gy_done, f)
                    fn(gsg[:, GC * j:GC * j + GC], G[:, j, 0:GC], ACT.Sigmoid, bias=bg[:, f:f + 1]).then_inc(sg_done, 1)
            act.wait_ge(vn_mm, 9)
            act.wait_ge(m_zero, 6)
            fn(t_vn1[:, :, 0:128], X[:, 3].rearrange("p (h n) -> p h n", h=4), ACT.Copy).then_inc(vn_done, 1)
            act.wait_ge(d_mm, 9)
            fn(t_EM[:, :, :].rearrange("p h n -> p (h n)"), X[:, 1], ACT.Exp).then_inc(em_done, 1)
            for h in range(4):
                if h >= 2:
                    act.wait_ge(tp_done, h - 1)
                for hf in range(2):
                    act.wait_ge(ctt_mm, 2 * h + hf + 1)
                    fn(ct8[:, h % 2, 4 * hf:4 * hf + 4, 0:128], X[:, hf].rearrange("p (b n) -> p b n", b=4),
                       ACT.Copy).then_inc(ctt_ev, 1)

            def high_y(t):
                for p in range(4):
                    act.wait_ge(y_in[p % 2], 16 * (2 * t + p // 2) + 16)
                    if p < 2:
                        act.wait_ge(ou_mm, 4 * t + 1)
                    else:
                        act.wait_ge(ob_mm, 12 * t + 1)
                    fn(yhi[:, 4 * p:4 * p + 4], yr[:, p % 2], ACT.Copy).then_inc(yhi_done, 1)

            def high_w(t, c):
                for p in range(8):
                    act.wait_ge(ow_in[p % 2], 16 * (16 * t + 4 * c + p // 2) + 16)
                    if p < 4:
                        act.wait_ge(ou_mm, 4 * t + c + 1)
                    else:
                        act.wait_ge(ob_mm, 12 * t + 3 * c + 1)
                    fn(ohi[:, p // 4, 2 * (p % 4):2 * (p % 4) + 2], orw[:, p % 2], ACT.Copy).then_inc(ohi_done, 1)

            high_y(0)
            high_w(0, 0)
            for t in range(3):
                for c in range(4):
                    if c < 3:
                        high_w(t, c + 1)
                    elif t < 2:
                        high_y(t + 1)
                        high_w(t + 1, 0)
                    for a in range(3):
                        act.wait_ge(xa_done, 12 * t + 3 * c + a + 7)
                        if (t, c, a) != (0, 0, 0):
                            act.wait_ge(oq_done, 12 * t + 3 * c + a)
                        fn(X[:, 4], xo[:, a, 512 * c:512 * c + 512], ACT.Square,
                           accum_out=fst[:, a, c:c + 1]).then_inc(oq_done, 1)
                act.wait_ge(f_ms, 2 * t + 2)
                fn(fst[:, :, 6], fst[:, :, 5], ACT.Sqrt).then_inc(f_rt, 1)

        @block.vector
        def _(dve):
            v = nc.vector
            tt, stt, tsc, cp = v.tensor_tensor, v.scalar_tensor_tensor, v.tensor_scalar, v.tensor_copy
            MUL, ADD, SUB, MAX, MIN = ALU.mult, ALU.add, ALU.subtract, ALU.max, ALU.min

            dve.wait_ge(g_loaded, 16)

            def norm(t, s):
                dve.wait_ge(sq_done, t + 2)
                tsc(stat[:, 1, ds(t, 1)], stat[:, 0, ds(t, 1)], 1.0 / D, EPS, MUL, ADD).then_inc(ms_done, 1)
                dve.wait_ge(rms_done, t + 1)
                v.reciprocal(stat[:, 3, ds(t, 1)], stat[:, 2, ds(t, 1)]).then_inc(rstd_done, 1)
                dve.wait_ge(rstd_done, t + 1)
                stt(xin[:, s], xin[:, s], stat[:, 3, ds(t, 1)], gb[:, :], MUL, MUL).then_inc(xn_done, 1)

            def low(t):
                for qd in range(4):
                    dve.wait_ge(hhi_done, 4 * t + qd + 1)
                    sl = (slice(None), slice(4 * qd, 4 * qd + 4), ds(t * 128, 128))
                    tt(hlo[sl], X[:, qd % 2].rearrange("p (k n) -> p k n", k=4), hhi[sl].bitcast(F), SUB).then_inc(h_done, 1)

            norm(0, 0)
            with dve.Fori(0, 4) as i:
                norm(2 * i + 1, 1)
                low(2 * i)
                norm(2 * i + 2, 0)
                low(2 * i + 1)
            low(8)

            g = Chain(dve, gt_dve)
            dve.wait_ge(evac_done, 6)
            dve.wait_ge(const_done, 14)
            g(v.memset(gR[:, :], 0.0))
            dve.wait_ge(gt_in, 64)
            g(tsc(gF[:, :], gF[:, :], gbi[:, 1:2], None, ADD))
            g(tsc(gA[:, :], gF[:, :], -1.0, None, MUL))
            g(tt(gA[:, :], gA[:, :], gF[:, :], MAX))
            assert g.count == 4
            g(tsc(gI[:, :], gI[:, :], gbi[:, 0:1], None, ADD))
            g(tsc(gF[:, :], gF[:, :], 0.0, None, MIN))
            g(v.memset(gK[:, :], 1.0))
            g(v.memset(gK[:, 0:NP:128], 0.0))
            g(v.memset(gK[:, NP:NT:DT], 0.0))
            dve.wait_ge(gt_act, 2)
            g(tt(gF[:, :], gF[:, :], gB[:, :], SUB))
            g(v.tensor_tensor_scan(gB[:, :], gK[:, :], gF[:, :], 0.0, MUL, ADD))
            g(tt(gsm[:, 3, 8:16], gF[:, NP:NT:DT], gsm[:, 0, 8:16], ADD))
            g(tt(gsm[:, 4, 8:16], gsm[:, 3, 8:16], gI[:, NP:NT:DT], MAX))
            g(tt(gA[:, :], gI[:, :], gB[:, :], SUB))
            g(cp(gI[:, NP:NT:DT], gsm[:, 4, 8:16]))
            g(v.memset(gF[:, NP:NT:DT], NEG))
            g(v.tensor_tensor_scan(gM[:, :], gF[:, :], gI[:, :], 0.0, ADD, MAX))
            g(v.memset(gsm[:, 0, 0:1], 0.0))
            g(cp(gsm[:, 0, 1:8], gM[:, 127:NP - 128:128]))
            g(cp(gsm[:, 2, 0:8], gM[:, 127:NP:128]))
            g(cp(gsm[:, 2, 8:16], gM[:, NP + DT - 1:NT:DT]))
            g(cp(gsm[:, 1, 0:8], gB[:, 127:NP:128]))
            g(cp(gsm[:, 1, 8:16], gB[:, NP + DT - 1:NT:DT]))
            g(tt(gB[:, :], gB[:, :], gM[:, :], SUB))
            assert g.count == GATE_ROWS, g.count

            def per_chunk(out, a, small):
                for sl, n, so in ((slice(0, NP), 128, slice(0, 8)), (slice(NP, NT), DT, slice(8, 16))):
                    g(tt(out[:, sl].rearrange("p (c n) -> p c n", n=n), a[:, sl].rearrange("p (c n) -> p c n", n=n),
                         small[:, so].unsqueeze(2).broadcast_to([4, 8, n]), ADD))

            per_chunk(gF, gB, gsm[:, 0])
            g(tt(gsm[:, 3], gsm[:, 1], gsm[:, 2], SUB))
            per_chunk(gK, gA, gsm[:, 3])
            g(tt(gsm[:, 4], gsm[:, 3], gsm[:, 0], ADD))
            assert g.count == GATE_ARGS, g.count
            dve.wait_ge(gt_act, GATE_R + 1)
            g(tt(dsel[:, :, :], sel[:, :, 0:16], gsm[:, 5:6, :].broadcast_to([4, 4, 16]), MUL))
            assert g.count == GATE_DSEL, g.count
            dve.wait_ge(gt_mm, 2)
            g(cp(col[:, 0:5, :].rearrange("p a n -> p (a n)"), X[:, 0, 0:480]))
            g(cp(col[:, 5:9, :].rearrange("p a n -> p (a n)"), X[:, 1, 0:384]))
            g(cp(dec[:, :, :].rearrange("p a n -> p (a n)"), X[:, 2, 0:64]))
            assert g.count == GATE_END, g.count

            with dve.Fori(0, 4) as i:
                def add_max(u):
                    n = 128 * min(u % 8 + 1, 5)
                    if u == 0:
                        dve.wait_ge(ab_in, 16 * i + 16)
                    dve.wait_ge(s_mm, 16 * i + u + 2)
                    dve.wait_ge(tp_mm, 17 * i + u + 1)
                    stt(aS[:, u % 2, 0:n], X2[:, 0:n], 0.125, abias[:, u // 8, BAND_KEYS - n:], MUL, ADD).then_inc(s_add, 1)
                    dve.wait_ge(s_add, 16 * i + u + 2)
                    v.reduce_max(ast[:, u % 2, 0:1], aS[:, u % 2, 0:n], AX, negate=True).then_inc(s_max, 1)

                add_max(0)
                for u in range(16):
                    n = 128 * min(u % 8 + 1, 5)
                    qs = slice(128 * (u % 8), 128 * (u % 8) + 128)
                    ps = slice(64 * (u // 8), 64 * (u // 8) + 64)
                    dve.wait_ge(e_done, 16 * i + u + 1)
                    v.reciprocal(ast[:, u % 2, 2:3], ast[:, u % 2, 1:2]).then_inc(r_done, 1)
                    dve.wait_ge(r_done, 16 * i + u + 1)
                    tsc(aS[:, u % 2, 0:n], aS[:, u % 2, 0:n], ast[:, u % 2, 2:3], None, MUL).then_inc(p_done, 1)
                    if u < 15:
                        add_max(u + 1)
                    if u == 0:
                        dve.wait_ge(z_in, 16 * i + 16)
                    dve.wait_ge(o_mm, 16 * i + u + 1)
                    tt(az[ps, qs], X[ps, 4, 0:128], az[ps, qs], MUL).then_inc(y_done, 1)

            dve.wait_ge(ss_in, 16 * 17)
            v.memset(qblk[:, :, :], 0.0).then_inc(qb_zero, 1)
            dve.wait_ge(qb_zero, 1)
            with dve.Fori(0, 4) as i:
                for s in range(2):
                    b = 2 * i + s
                    bs = ds(b * DT, DT)
                    cp(svb[:, :, :], sv[:, :, bs]).then_inc(kq_done, 1)
                    for t in (1, 3):
                        dve.wait_ge(kt_mm, 4 * b + t + 5)
                        cp(sKT[:, :, 128 * t:128 * t + 128], X[:, t].rearrange("p (h n) -> p h n", h=4)).then_inc(kt_ev, 1)
                    cp(sKT[:, :, 512:SK], sk[:, :, bs]).then_inc(kq_done, 1)
                    cp(qblk[0:64, :, 0:DT], sq[0:64, :, bs]).then_inc(kq_done, 1)
                    cp(qblk[64:128, :, DT:2 * DT], sq[64:128, :, bs]).then_inc(kq_done, 1)
                    dve.wait_ge(ss_mm, b + 1)
                    stt(sS[:, :], X2[:, 0:SK], 0.125, sbias[:, :], MUL, ADD).then_inc(ss_add, 1)
                    dve.wait_ge(ss_add, b + 1)
                    v.reduce_max(sst[:, 0:1], sS[:, :], AX, negate=True).then_inc(ss_max, 1)
                    dve.wait_ge(ss_e, b + 1)
                    v.reciprocal(sst[:, 2:3], sst[:, 1:2]).then_inc(ss_r, 1)
                    dve.wait_ge(ss_r, b + 1)
                    tsc(sS[:, :], sS[:, :], sst[:, 2:3], None, MUL).then_inc(ss_p, 1)
                    dve.wait_ge(so_mm, b + 2)
                    o = X[:, 4, 0:128].rearrange("p (h n) -> p h n", h=4)
                    tt(sz[0:64, :, bs], o[0:64, :, 0:DT], sz[0:64, :, bs], MUL)
                    tt(sz[64:128, :, bs], o[64:128, :, DT:2 * DT], sz[64:128, :, bs], MUL).then_inc(sy_done, 1)

            c5 = Chain(dve, s5c)
            C1, C2 = 6.28125, 0.0019350051879882812
            C3 = TWO_PI_EXACT - C1 - C2

            def reduce_angle(dst, src, whole):
                c5(tsc(smi[:, :], src, 1.0 / TWO_PI_EXACT, None, MUL))
                c5(cp(whole, smi[:, :]))
                c5(stt(dst, whole, -C1, src, MUL, ADD))
                c5(stt(dst, whole, -C2, dst, MUL, ADD))
                c5(stt(dst, whole, -C3, dst, MUL, ADD))
                c5(tsc(dst, dst, -PI_LO, PI_LO, MAX, MIN))

            def quarter_turn(dst, src):
                c5(tsc(dst, src, -1.0, None, MUL))
                c5(tt(dst, dst, src, MAX))
                return tsc(dst, dst, -1.0, TWO_PI_EXACT / 4, MUL, ADD)

            dve.wait_ge(s5_in, 32)
            c5(v.memset(Kbd[:, :, :], 0.0))
            c5(v.memset(XS[:, :, :, NCS:NCS + 1], 0.0))
            dve.wait_ge(s5a, 1)
            c5(tt(sm[:, 2], par[:, 1], sm[:, 0], MUL))
            tt(sm[:, 1], par[:, 0], sm[:, 0], MUL).then_inc(s5v, 1)
            reduce_angle(sm[:, 5], sm[:, 2], sm[:, 12])
            c5(tsc(sm[:, 2], sm[:, 5], float(LC), None, MUL))
            reduce_angle(sm[:, 7], sm[:, 2], sm[:, 12])
            c5(quarter_turn(sm[:, 6], sm[:, 5]))
            quarter_turn(sm[:, 2], sm[:, 7]).then_inc(s5v, 1)
            dve.wait_ge(s5a, 7)
            c5(v.memset(PW[:, 0, 0], 1.0))
            c5(v.memset(PW[:, 1, 0], 0.0))
            c5(tt(PW[:, 0, 1], sm[:, 3], sm[:, 9], MUL))
            c5(tt(PW[:, 1, 1], sm[:, 3], sm[:, 8], MUL))
            c5(cp(E1[:, 0], sm[:, 11]))
            c5(tsc(E1[:, 1], sm[:, 10], -1.0, None, MUL))
            for m in (1, 2, 4):
                a, b = slice(1, m + 1), slice(m + 1, 2 * m + 1)
                top_re, top_im = (PW[:, n, m:m + 1].broadcast_to([128, m, 16]) for n in range(2))
                w = sm[:, 12:12 + m]
                c5(tt(PW[:, 0, b], PW[:, 0, a], top_re, MUL))
                c5(tt(w, PW[:, 1, a], top_im, MUL))
                c5(tt(PW[:, 0, b], PW[:, 0, b], w, SUB))
                c5(tt(PW[:, 1, b], PW[:, 0, a], top_im, MUL))
                c5(tt(w, PW[:, 1, a], top_re, MUL))
                c5(tt(PW[:, 1, b], PW[:, 1, b], w, ADD))
            c5(tt(sm[:, 12], par[:, 0], par[:, 0], MUL))
            c5(tt(sm[:, 13], par[:, 1], par[:, 1], MUL))
            c5(tt(sm[:, 12], sm[:, 12], sm[:, 13], ADD))
            c5(v.reciprocal(sm[:, 13], sm[:, 12]))
            c5(tsc(sm[:, 14], PW[:, 0, 1], -1.0, None, ADD))
            c5(tt(sm[:, 5], sm[:, 14], par[:, 0], MUL))
            c5(tt(sm[:, 12], PW[:, 1, 1], par[:, 1], MUL))
            c5(tt(sm[:, 5], sm[:, 5], sm[:, 12], ADD))
            c5(tt(sm[:, 5], sm[:, 5], sm[:, 13], MUL))
            c5(tt(sm[:, 6], PW[:, 1, 1], par[:, 0], MUL))
            c5(tt(sm[:, 12], sm[:, 14], par[:, 1], MUL))
            c5(tt(sm[:, 6], sm[:, 6], sm[:, 12], SUB))
            c5(tt(sm[:, 6], sm[:, 6], sm[:, 13], MUL))
            assert c5.count == S5_PREP, c5.count

            Va = VT[:, 0].rearrange("p (a b) n -> p a b n", a=2)
            Vb = VT[:, 1].rearrange("p (a b) n -> p a b n", a=2)
            T1f = T1[:, 0:1024]
            with dve.Fori(0, 4) as f:
                c5 = Chain(dve, s5c, S5_PREP + f * S5_STEPS)
                st4s = ds(4 * f, 4)
                dve.wait_ge(bc_in, 48 * f + 48)
                dve.wait_ge(g5_stored, 32 * f + 16)
                c5(tsc(BC[:, 1, 1], BC[:, 1, 1], -1.0, None, MUL))
                Bb = [VT[:, 1, n].rearrange("p (s c) -> p s c", s=4) for n in range(2)]
                w = VT[:, 1, 2].rearrange("p (s c) -> p s c", s=4)
                co_re, co_im = (sm[:, n, st4s].unsqueeze(2).broadcast_to([128, 4, 32]) for n in (5, 6))
                c5(tt(Bb[0], BC[:, 0, 0], co_re, MUL))
                c5(tt(w, BC[:, 0, 1], co_im, MUL))
                c5(tt(Bb[0], Bb[0], w, SUB))
                c5(tt(Bb[1], BC[:, 0, 1], co_re, MUL))
                c5(tt(w, BC[:, 0, 0], co_im, MUL))
                c5(tt(Bb[1], Bb[1], w, ADD))
                ACv = [AC[:, n].rearrange("p t (s c) -> p t s c", s=4) for n in range(2)]
                full = [128, LC, 4, 32]
                pw = [[PW[:, n, o:o + LC, st4s].unsqueeze(3).broadcast_to(full) for n in range(2)] for o in range(2)]
                Bx = [x.unsqueeze(1).broadcast_to(full) for x in Bb]
                w = VT[:, 0].rearrange("p t (s c) -> p t s c", s=4)
                c5(tt(ACv[0], pw[0][0], Bx[0], MUL))
                c5(tt(w, pw[0][1], Bx[1], MUL))
                c5(tt(ACv[0], ACv[0], w, SUB))
                c5(tt(ACv[1], pw[0][0], Bx[1], MUL))
                c5(tt(w, pw[0][1], Bx[0], MUL))
                tt(ACv[1], ACv[1], w, ADD).then_inc(ab_done, 1)
                dve.wait_ge(ab_done, f + 1)
                c5(v.memset(E5[:, 0, :, 0:1], 1.0))
                c5(v.memset(E5[:, 1, :, 0:1], 0.0))
                c5(cp(E5[:, :, :, 1], E1[:, :, st4s]))
                m = 1
                while m < NCP:
                    a, b = slice(1, m + 1), slice(m + 1, 2 * m + 1)
                    mul = [E5[:, n:n + 1, :, m:m + 1].broadcast_to([128, 2, 4, m]) for n in range(2)]
                    w = Va[:, :, :, 0:m]
                    c5(tt(E5[:, :, :, b], E5[:, :, :, a], mul[0], MUL))
                    c5(tt(w, E5[:, :, :, a], mul[1], MUL))
                    c5(tt(E5[:, 0, :, b], E5[:, 0, :, b], w[:, 1], SUB))
                    c5(tt(E5[:, 1, :, b], E5[:, 1, :, b], w[:, 0], ADD))
                    m *= 2
                assert c5.count == S5_TABLES, c5.count
                for e in (1, 3):
                    dve.wait_ge(vt5_mm, 4 * f + e + 1)
                    cp(VT[:, e // 2, 4 * (e % 2):4 * (e % 2) + 4].rearrange("p a n -> p (a n)"), X[:, e]).then_inc(vt5_ev, 1)
                dve.wait_ge(k5_mm, f + 1)
                for st in range(4):
                    ps = slice(32 * st, 32 * st + 32)
                    last = cp(Kbd[ps, :, ps], X[ps, 4, 0:256].rearrange("p (t c) -> p t c", t=LC))
                last.then_inc(k5_ev, 1)
                dve.wait_ge(su_done, 2 * f + 2)
                Cx = [BC[:, 1, n].unsqueeze(1).broadcast_to(full) for n in range(2)]
                w = T1f.rearrange("p (t s c) -> p t s c", t=LC, s=4)
                c5(tt(ACv[0], pw[1][0], Cx[0], MUL))
                c5(tt(w, pw[1][1], Cx[1], MUL))
                c5(tt(ACv[0], ACv[0], w, ADD))
                c5(tt(ACv[1], pw[1][0], Cx[1], MUL))
                c5(tt(w, pw[1][1], Cx[0], MUL))
                tt(ACv[1], ACv[1], w, SUB).then_inc(ca_done, 1)
                dve.wait_ge(ca_done, f + 2)
                dve.wait_ge(x5_mm, f + 1)
                Xp = X[:, 0:4, 0:2 * NC].rearrange("p s (r n) -> p r s n", r=2)
                Ex = [E5[:, n:n + 1, :, 0:NCP].broadcast_to([128, 2, 4, NCP]) for n in range(2)]
                c5(tt(Va, Xp[:, :, :, NCS:NC], Ex[0], MUL))
                c5(tt(Vb, Xp[:, :, :, NCS:NC], Ex[1], MUL))
                c5(tt(Va[:, 0], Va[:, 0], Vb[:, 1], SUB))
                c5(tt(Va[:, 1], Va[:, 1], Vb[:, 0], ADD))
                for n in range(2):
                    for st in range(4):
                        r8 = sm[:, 4, ds(4 * f + st, 1)]
                        c5(v.tensor_tensor_scan(Vb[:, n, st], r8.broadcast_to([128, NCP]), Va[:, n, st], 0.0, MUL, ADD))
                w = T1f.rearrange("p (r s n) -> p r s n", r=2, s=4)
                c5(tt(Va, Vb, Ex[0], MUL))
                c5(tt(w, Vb, Ex[1], MUL))
                c5(tt(XS[:, 0, :, NCS + 1:], Va[:, 0], w[:, 1], ADD))
                c5(tt(XS[:, 1, :, NCS + 1:], Va[:, 1], w[:, 0], SUB))
                A8 = [PW[:, n:n + 1, LC, st4s].unsqueeze(3).broadcast_to([128, 2, 4, 8]) for n in range(2)]
                c5(cp(XS[:, :, :, 0:NCS:2], s0[:, :, :, :]))
                for step in range(2):
                    src = XS[:, :, :, step:NCS:2]
                    c5(tt(SX[:, 0], src, A8[0], MUL))
                    c5(tt(SX[:, 1], src, A8[1], MUL))
                    c5(tt(SX[:, 0, 0], SX[:, 0, 0], SX[:, 1, 1], SUB))
                    c5(tt(SX[:, 0, 1], SX[:, 0, 1], SX[:, 1, 0], ADD))
                    dst = XS[:, :, :, 1:NCS:2] if step == 0 else FO[:, :, :, 0:8]
                    c5(tt(dst, SX[:, 0], Xp[:, :, :, step:NCS:2], ADD))
                cp(FO[:, :, :, 8], XS[:, :, :, NC]).then_inc(xs_done, 1)
                for bk in range(3):
                    i0, i1 = 3 * bk, min(3 * bk + 3, LC)
                    dve.wait_ge(y5_mm, 3 * f + bk + 1)
                    stt(T1[:, NC * i0:NC * i1], suP[:, i0:i1].rearrange("p a n -> p (a n)"), dD[:, ds(f, 1)],
                        X[:, bk, 0:NC * (i1 - i0)], MUL, ADD).then_inc(t1_done, 1)
                assert c5.count == S5_STEPS, c5.count

            for z in (v.memset(CT[:, :, :], 0.0), v.memset(vn1[:, :, 128:129], 1.0)):
                z.then_inc(m_zero, 1)
            dve.wait_ge(m_zero, 2)

            def ml_gates(c, row, g2, oz, ozin):
                tt(g2[:, :, :, :], sel[:, :, :].unsqueeze(1).broadcast_to([4, 2, 4, 128]),
                   row[:, 0:2].unsqueeze(2).broadcast_to([4, 2, 4, 128]), MUL).then_inc(gs_done, 1)

            def ml_mid(c, q, k_scaled, q_out, wt_out, em):
                dve.wait_ge(wb_mm, c + 1)
                tt(q_out, q, X[:, 2].rearrange("p (h n) -> p h n", h=4), MUL).then_inc(q2_done, 1)
                dve.wait_ge(kn_mm, c + 1)
                kx = X[:, 4].rearrange("p (h n) -> p h n", h=4)
                k_scaled(kx).then_inc(wk_done, 1)
                dve.wait_ge(em_done, c + 1)
                dve.wait_ge(st_mm, c + 1)
                tt(wt_out, em, X[:, 0].rearrange("p (h n) -> p h n", h=4), MUL).then_inc(wt_done, 1)

            def ml_norm(c, d2, h_out):
                P = X[:, 2:4, 0:258].rearrange("p a (h n) -> p a h n", h=2)
                den = d2[:, 0].rearrange("p (a h) -> p a h", a=2)
                inv = d2[:, 1].rearrange("p (a h) -> p a h", a=2)
                floor = col[:, ds(c, 1), 32:36].rearrange("p o (a h) -> p (o a) h", a=2)
                k = Chain(dve, den_c, 4 * c)
                k(tsc(den, P[:, :, :, 128], -1.0, None, MUL))
                k(tt(den, P[:, :, :, 128], den, MAX))
                k(tt(den, den, floor, MAX))
                k(v.reciprocal(inv, den))
                tt(h_out.rearrange("p (a h) n -> p a h n", a=2), P[:, :, :, 0:128],
                   inv.unsqueeze(3).broadcast_to([128, 2, 2, 128]), MUL).then_inc(hn_done, 1)

            with dve.Fori(0, 4) as i:
                for s in range(2):
                    c = 2 * i + s
                    dve.wait_ge(mq_in[s], 64 * i + 64)
                    ml_gates(c, mrow[:, s], gs, None, None)
                    dve.wait_ge(mo_in, 32 * c + 32)
                    tt(moz[:, 0], moz[:, 0], moz[:, 1], MUL).then_inc(oz_done, 1)
                    ml_mid(c, mqkv[:, s, 0],
                           lambda kx: tt(wsk[:, :, :], kx, col[:, ds(c, 1), 64:68].rearrange("p o h -> p (o h)").unsqueeze(2).broadcast_to([128, 4, 128]), MUL),
                           q2[:, :, :], WT[:, :, :], EM[:, :, :])
                    dve.wait_ge(u_mm, c + 1)
                    for h in range(4):
                        last = stt(CT[:, h], CT[:, h], dec[:, h, ds(c, 1)],
                                   X[:, 4 * (h // 2), 129 * (h % 2):129 * (h % 2) + 129], MUL, ADD)
                    last.then_inc(ct_done, 1)
                    ml_norm(c, md, hn[:, :, :])
                    dve.wait_ge(ht_mm, c + 1)
                    dve.wait_ge(oz_done, c + 1)
                    dve.wait_ge(my_stored, 16 * c + 16)
                    tt(yb[:, :, :], X[:, 1].rearrange("p (h n) -> p h n", h=4), moz[:, 0], MUL).then_inc(my_done, 1)

            dve.wait_ge(bank_full, 3 * NTILES + 3)
            dve.wait_ge(w_split, 2 * NTILES + 2)
            dve.wait_ge(outs_done, 16 * 18)
            dve.wait_ge(my_stored, 16 * 9)
            k = Chain(dve, m_zero, 2)
            k(v.memset(t_vn1[:, :, 128:129], 1.0))
            k(v.memset(qm[:, :, :], 0.0))
            k(v.memset(cub[:, :, 0:2], 0.0))
            dve.wait_ge(tq_in, 16 * 7)
            k(tt(wsm[:, :, :], col[:, 8, 64:68].unsqueeze(2).broadcast_to([128, 4, NSTR]),
                 bmask[:, :].unsqueeze(1).broadcast_to([128, 4, NSTR]), MUL))
            ml_gates(8, t_row, t_gs, None, None)
            tt(t_qkv[:, 3], t_qkv[:, 3], t_qkv[:, 4], MUL).then_inc(oz_done, 1)

            dve.wait_ge(cp_in, 16)
            dve.wait_ge(gl_in, 48)
            kc_ = Chain(dve, cvc)

            def conv(f):
                s = f % 2
                B, Cg, xi, z = (cv[:, s, n] for n in range(4))
                two = lambda a: a[:, NP:NT].rearrange("p (b t) -> p b t", b=NSTR)
                dve.wait_ge(cv_in[s], 80 * (f // 2) + 80)
                if f >= 2:
                    dve.wait_ge(cv_out[s], 48)
                kc_(tt(cub[:, s, 2:], Cg[:, 0:NP], xi[:, 0:NP], MUL))
                kc_(tt(cus[:, s, :, 2:], two(Cg), two(xi), MUL))
                up = lambda j: (cub[:, s, j:j + NP], cus[:, s, :, j:j + DT])
                outs = (cy[:, s, 0:NP], two(cy[:, s]))
                for o, x in zip(outs, up(0)):
                    kc_(tsc(o, x, cw[:, 0, f:f + 1], None, MUL))
                for j in (1, 2):
                    for o, x in zip(outs, up(j)):
                        kc_(stt(o, x, cw[:, j, f:f + 1], o, MUL, ADD))
                kc_(tt(cy[:, s], cy[:, s], B, MUL))
                tt(cy[:, s], cy[:, s], z, MUL).then_inc(cv_done, 1)

            def glu(f):
                dve.wait_ge(sg_done, 3 * f + 6)
                tt(gsg[:, :], gsg[:, :], gl[:, f], MUL).then_inc(gm_done, 1)
                dve.wait_ge(gm_done, f + 1)
                dve.wait_ge(gz_in, 16 * f + 16)
                st_major = gsg[:, :].rearrange("p (i n) -> p n i", i=LC)
                p_ = gsz[:, 0:NP].rearrange("p (n i) -> p n i", i=LC)
                s_ = gsz[:, NP:NT].rearrange("p (n i) -> p n i", i=LC)
                tt(p_, p_, st_major[:, NCS:NC], MUL)
                tt(s_, s_, st_major[:, 0:NCS], MUL).then_inc(gy_done, 1)

            for f in range(4):
                glu(f)
            ml_mid(8, t_qkv[:, 0], lambda kx: cp(t_wsk[:, :, :], kx), t_q2[:, :, :], t_WT[:, :, :], t_EM[:, :, :])
            dve.wait_ge(q2_done, 9)
            dve.wait_ge(wk_done, 9)
            for h in range(4):
                s = h % 2
                if h >= 2:
                    dve.wait_ge(cn_mm, h - 1)
                    dve.wait_ge(tp_done, h - 1)
                cp(ct8[:, s, :, 128], nin[:, h]).then_inc(ctt_ev, 1)
                cp(qm[:, s].rearrange("p (b n) -> p b n", b=NSTR)[:, :, 0:DT],
                   t_q2[:, h].rearrange("p (b n) -> p b n", b=NSTR)).then_inc(qm_done, 1)
                tt(wkm[:, s], t_wsk[:, h:h + 1].broadcast_to([128, NSTR, 128]),
                   wsm[:, h].unsqueeze(2).broadcast_to([128, NSTR, 128]), MUL).then_inc(wkm_done, 1)
                dve.wait_ge(ctt_mm, 2 * h + 2)
                tt(cnat[:, s], cnat[:, s], dec[:, h, 8:16].unsqueeze(2).broadcast_to([128, NSTR, 128]), MUL).then_inc(cdec, 1)
                tt(nout[:, h], nin[:, h], dec[:, h, 8:16], MUL).then_inc(cdec, 1)
                dve.wait_ge(cdec, 2 * h + 2)
                dve.wait_ge(cu_mm, h + 1)
                for hf in range(2):
                    cs = cnat[:, s, 4 * hf:4 * hf + 4].rearrange("p b k -> p (b k)")
                    last = tt(cs, cs, X[:, hf], ADD)
                last.then_inc(cu_done, 1)
                dve.wait_ge(cn_mm, h + 1)
                tt(nout[:, h], nout[:, h], X[:, 4, 0:NSTR], ADD).then_inc(n_done, 1)
            dve.wait_ge(tp_done, 4)
            ml_norm(8, t_md, t_hn[:, :, :])
            for f in range(4):
                conv(f)
            dve.wait_ge(ht_mm, 9)
            dve.wait_ge(oz_done, 9)
            tt(t_yb[:, :, :], X[:, 1].rearrange("p (h n) -> p h n", h=4), t_qkv[:, 3], MUL).then_inc(my_done, 1)

            def low_y(t):
                for p in range(4):
                    dve.wait_ge(yhi_done, 4 * t + p + 1)
                    tt(ylo[:, 4 * p:4 * p + 4], yr[:, p % 2], yhi[:, 4 * p:4 * p + 4].bitcast(F), SUB).then_inc(ylo_done, 1)

            def low_w(t, c):
                for p in range(8):
                    dve.wait_ge(ohi_done, 32 * t + 8 * c + p + 1)
                    sl = (slice(None), p // 4, slice(2 * (p % 4), 2 * (p % 4) + 2))
                    tt(olo[sl], orw[:, p % 2], ohi[sl].bitcast(F), SUB).then_inc(olo_done, 1)

            low_y(0)
            low_w(0, 0)
            dve.wait_ge(go_in, 16)
            for t in range(3):
                for c in range(4):
                    if c < 3:
                        low_w(t, c + 1)
                    elif t < 2:
                        low_y(t + 1)
                        low_w(t + 1, 0)
                    dve.wait_ge(xo_in, 16 * t + 16)
                    for a in range(3):
                        dve.wait_ge(ob_mm, 12 * t + 3 * c + a + 2)
                        cs = slice(512 * c, 512 * c + 512)
                        tt(xo[:, a, cs], outbank(c, a), xo[:, a, cs], ADD).then_inc(xa_done, 1)
                dve.wait_ge(oq_done, 12 * t + 12)
                v.reduce_sum(fst[:, :, 4], fst[:, :, 0:4], AX).then_inc(f_ms, 1)
                dve.wait_ge(f_ms, 2 * t + 1)
                tsc(fst[:, :, 5], fst[:, :, 4], 1.0 / D, EPS, MUL, ADD).then_inc(f_ms, 1)
                dve.wait_ge(f_rt, t + 1)
                v.reciprocal(fst[:, :, 7], fst[:, :, 6]).then_inc(f_rs, 1)
                dve.wait_ge(f_rs, t + 1)
                dve.wait_ge(f_stored, 48 * t + 16)
                for a in range(3):
                    stt(fo[:, a], xo[:, a], fst[:, a, 7:8], go[:, :], MUL, MUL).then_inc(f_done, 1)

GATE_ROWS, GATE_ARGS, GATE_DSEL, GATE_END = 24, 30, 31, 34
GATE_WINT, GATE_R = 3, 5
S5_PREP, S5_TABLES, S5_STEPS = 58, 43, 75
TWO_PI_EXACT = 6.283185307179586

_OUTS = [("y_all", (NT, D)), ("kv_new", (4, 2, 128, 640)), ("k_shift", (NSTR, 512 - DT, 512)),
         ("v_shift", (NSTR, 512 - DT, 512)), ("c_prompt", (4, 128, 128)), ("n_prompt", (128, 4)),
         ("m_last", (4, 16)), ("c_stream", (4, 128, NSTR, 128)), ("n_stream", (128, 4, NSTR)),
         ("conv_p", (4, 128, 2)), ("conv_s", (4, 128, NSTR, 2)), ("s5_last", (128, 2, 16, 9))]

def kernel(**inputs):
    import numpy as np
    import concourse.bacc as bacc
    from concourse.bass_utils import run_bass_kernel_spmd

    a = {k: np.asarray(v) for k, v in inputs.items()}
    x_all = np.concatenate([a["x_prompt"][0], a["x_sample"].reshape(NS, D)], axis=0)
    w = a["w_in"][0].reshape(KT, 128, -1)
    start = {"aq": 0, "ak": 512, "av": 1024, "az": 1536, "mq": 2048, "mk": 2560, "mv": 3072, "mo": 3584, "mz": 4096,
             "cb": 4616, "cc": 5128, "cx": 5640, "cz": 6152, "su": 6664, "sz": 7176}
    w_in_t = np.zeros((NTILES, 128, KT, 128), np.float32)
    w_in_t[T_GATE, :, :, 0:4] = w[:, :, 4608:4612].transpose(1, 0, 2)
    w_in_t[T_GATE, :, :, 32:36] = w[:, :, 4612:4616].transpose(1, 0, 2)
    for names, tile in ((("aq", "ak", "av", "az"), T_ATT), (("mq", "mk", "mv", "su"), T_ML), (("mo", "mz"), T_MG),
                        (("cb", "cc", "sz"), T_S5), (("cx", "cz"), T_CV)):
        for kind, n in enumerate(names):
            for i in range(4):
                c0 = start[n] + 128 * i
                w_in_t[tile(i, kind)] = w[:, :, c0:c0 + 128].transpose(1, 0, 2)
    w_out_t = a["w_out"][0].reshape(KT, 128, 4, 512).transpose(2, 1, 0, 3)
    rb = a["attn_rel_bias"][0]
    q, j = np.arange(128)[:, None], np.arange(BAND_KEYS)[None, :]
    idx = np.clip(q + 512 - j, -128, 128) + 128
    hidden = ((q < 64) & (j >= 576)) | ((q >= 64) & (j < 64))
    bias_p = np.where(hidden[None], np.float32(NEG), rb[:, idx]).astype(np.float32)
    q, j = np.arange(DT)[:, None], np.arange(SK)[None, :]
    bias_s = rb[:, np.clip(q + 512 - j, -128, 128) + 128].reshape(128, SK)

    def states(x):
        return x.reshape((16, 2, 64) + x.shape[2:]).transpose((1, 2, 0) + tuple(range(3, x.ndim + 1))).reshape((128, 16) + x.shape[2:])

    def spread(x):
        x = x.reshape(16, 2, 64, 16)
        out = np.zeros((2, 64, 16, 32), np.float32)
        out[0, :, :, 0:16] = x[:, 0].transpose(1, 0, 2)
        out[1, :, :, 16:32] = x[:, 1].transpose(1, 0, 2)
        return out.reshape(128, 16, 32)

    arrays = {
        "x_all": x_all, "w_in_t": w_in_t, "w_out_t": w_out_t,
        "g_in": np.broadcast_to(a["norm_g"][0], (128, D)), "g_out": np.broadcast_to(a["final_norm_g"], (128, D)),
        "bias_p": bias_p, "bias_s": bias_s,
        "b_if": a["mlstm_b_if"][0].reshape(2, 4).T, "m_init": a["state_mlstm_m"][0].T,
        "k_cache": a["cache_attn_k"][0].reshape(NSTR, 512, 512), "v_cache": a["cache_attn_v"][0].reshape(NSTR, 512, 512),
        "c_init": a["state_mlstm_C"][0].transpose(1, 2, 0, 3), "n_init": a["state_mlstm_n"][0].transpose(2, 1, 0),
        "conv_w": a["conv_w"][0].reshape(3, 4, 128).transpose(2, 0, 1),
        "conv_buf": a["state_conv"][0].reshape(NSTR, 2, 4, 128).transpose(2, 3, 0, 1),
        "s5_par": np.stack([states(a["s5_A_re"][0]), states(a["s5_A_im"][0]),
                            states(np.broadcast_to(a["s5_log_dt"][0][:, None], (32, 64)))], axis=1),
        "s5_b": np.stack([spread(a["s5_B_re"][0]), spread(a["s5_B_im"][0])], axis=1),
        "s5_c": np.stack([spread(a["s5_C_re"][0].transpose(0, 2, 1)), spread(a["s5_C_im"][0].transpose(0, 2, 1))], axis=1),
        "s5_s0": np.stack([states(a["state_s5_re"][0].transpose(1, 2, 0)), states(a["state_s5_im"][0].transpose(1, 2, 0))], axis=1),
        "s5_d": a["s5_D"][0].reshape(4, 128).T,
        "w_glu": a["s5_w_glu"][0].reshape(4, 128, 512).transpose(1, 0, 2), "b_glu": a["s5_b_glu"][0].reshape(4, 128).T,
    }
    nc = bacc.Bacc("TRN2", target_bir_lowering=False, num_devices=1, dynamic_dma_scratch_size=256)
    arrays = {k: np.ascontiguousarray(v) for k, v in arrays.items()}
    args = [nc.dram_tensor(k, v.shape, mybir.dt.from_np(v.dtype), kind="ExternalInput").ap() for k, v in arrays.items()]
    args += [nc.dram_tensor(k, s, mybir.dt.float32, kind="ExternalOutput").ap() for k, s in _OUTS]
    encoder_program(nc, *args)
    r = run_bass_kernel_spmd(nc, [arrays], core_ids=[0]).results[0]

    y, kv, m, s5 = r["y_all"], r["kv_new"], r["m_last"], r["s5_last"]
    kv = kv.transpose(1, 3, 0, 2).reshape(2, 640, 8, 64)
    caches = [np.concatenate([r[n].reshape(NSTR, 512 - DT, 8, 64), kv[i, 512:].reshape(NSTR, DT, 8, 64)], axis=1)[None]
              for i, n in enumerate(("k_shift", "v_shift"))]
    s5 = s5.reshape(2, 64, 2, 16, 9).transpose(2, 4, 3, 0, 1).reshape(2, 9, 32, 64)
    return (y[None, :NP], y[NP:].reshape(NSTR, DT, D),
            kv[0, :512][None, None], kv[1, :512][None, None],
            r["c_prompt"].transpose(0, 2, 1)[None, None], r["n_prompt"].T[None, None], m[:, 7][None, None],
            r["conv_p"].transpose(2, 0, 1).reshape(2, 512)[None, None],
            s5[0, 8][None, None], s5[1, 8][None, None],
            caches[0], caches[1],
            r["c_stream"].transpose(2, 0, 1, 3)[None], r["n_stream"].transpose(2, 1, 0)[None], m[:, 8:16].T[None],
            r["conv_s"].transpose(2, 3, 0, 1).reshape(NSTR, 2, 512)[None],
            s5[0, 0:8][None], s5[1, 0:8][None])
```

```python
import concourse.bass as bass
from concourse import mybir
from contextlib import ExitStack

D = 2048
NP, NSTR, DT = 1024, 8, 16
NS = NSTR * DT
NT = NP + NS
TT = NT // 128
KT = D // 128
GC = NT // 3
BAND_KEYS = 640
SK = 512 + DT
LC = 8
NCP = NP // LC
NCS = NS // LC
NC = NCP + NCS
EPS = 1e-6
NEG = -1e30
TWO_PI = 6.283185307179586
PI_LO = 3.1415925

T_GATE = 0
def T_ATT(i, kind): return 1 + 4 * i + kind
def T_ML(i, kind): return 17 + 4 * i + kind
def T_MG(i, kind): return 33 + 2 * i + kind
def T_S5(i, kind): return 41 + 3 * i + kind
def T_CV(i, kind): return 53 + 2 * i + kind
NTILES = 61

def encoder_program(nc, x_all, w_in_t, w_out_t, g_in, g_out, bias_p, bias_s, b_if, m_init,
                    k_cache, v_cache, c_init, n_init, conv_w, conv_buf, s5_par, s5_b, s5_c, s5_s0,
                    s5_d, w_glu, b_glu,
                    y_all, kv_new, k_shift, v_shift, c_prompt, n_prompt, m_last, c_stream,
                    n_stream, conv_p, conv_s, s5_last):
    F = mybir.dt.float32
    R = mybir.dt.float32r
    I32 = mybir.dt.int32
    ACT = mybir.ActivationFunctionType
    ALU = mybir.AluOpType
    AX = mybir.AxisListType.X
    ds = bass.ds

    def dram(name, shape):
        return nc.dram_tensor(name, shape, F, kind="Internal").ap()

    uT = dram("u_scratch", [NTILES, 128, NT])
    yT = dram("y_scratch", [KT, 128, NT])
    rows = dram("gate_rows", [4, 3, NT])
    gS5 = dram("s5_gelu", [4, 128, LC * NC])

    top = ExitStack()
    with top:
        def sem(name):
            return top.enter_context(nc.semaphore(name))

        def sb(stack, name, shape, dt=F):
            return stack.enter_context(nc.sbuf_tensor(name, shape, dt))

        x_in = [sem(f"x_in{n}") for n in range(4)]
        g_loaded = sem("g_loaded")
        sq_done = sem("sq_done")
        ms_done = sem("ms_done")
        rms_done = sem("rms_done")
        rstd_done = sem("rstd_done")
        xn_done = sem("xn_done")
        xt_mm = sem("xt_mm")
        hhi_done = sem("hhi_done")
        h_done = sem("h_done")
        wraw = [sem("wraw0"), sem("wraw1")]
        whi_done = sem("whi_done")
        w_split = sem("w_split")
        half0_mm = sem("half0_mm")
        bank_full = sem("bank_full")
        evac_done = sem("evac_done")
        u_stored = [sem(f"u_stored{j}") for j in range(3)]
        const_done = sem("const_done")
        outs_done = sem("outs_done")

        ident = sb(top, "ident", [128, 128])
        mask_p = sb(top, "mask_p", [128, 128])
        mask_s = sb(top, "mask_s", [128, 128])
        bmask = sb(top, "bmask", [128, NSTR])
        ones4 = sb(top, "ones4", [4, 128])
        sel = sb(top, "sel", [4, 4, 128])
        onec = sb(top, "onec", [128, 1])
        col = sb(top, "col", [128, TT, 96])
        dec = sb(top, "dec", [128, 4, 16])
        PW = sb(top, "PW", [128, 2, LC + 1, 16])
        E1 = sb(top, "E1", [128, 2, 16])
        s5k = sb(top, "s5k", [128, 3, 16])
        G = top.enter_context(nc.psum_tensor("G", [128, 3, 512], F))
        X = top.enter_context(nc.psum_tensor("X", [128, 5, 512], F))
        X2 = X[:, 0:2, :].rearrange("p a n -> p (a n)")
        T2 = X[:, 2:4, :].rearrange("p a n -> p (a n)")

        hstack = ExitStack()
        hhi = sb(hstack, "hhi", [128, KT, NT], R)
        hlo = sb(hstack, "hlo", [128, KT, NT], R)
        wr = sb(hstack, "wr", [128, 2, 8, 128])
        whi = sb(hstack, "whi", [128, 2, 8, 128], R)
        wlo = sb(hstack, "wlo", [128, 2, 8, 128], R)
        ev = sb(hstack, "ev", [128, 3, GC])

        st0 = ExitStack()
        xin = sb(st0, "xin", [128, 4, D])
        gb = sb(st0, "gb", [128, D])
        stat = sb(st0, "stat", [128, 4, TT])
        st0.close()

        st1 = ExitStack()
        gI = sb(st1, "gI", [4, NT])
        gF = sb(st1, "gF", [4, NT])
        gA = sb(st1, "gA", [4, NT])
        gB = sb(st1, "gB", [4, NT])
        gM = sb(st1, "gM", [4, NT])
        gK = sb(st1, "gK", [4, NT])
        gR = sb(st1, "gR", [96, NT])
        gsm = sb(st1, "gsm", [4, 8, 16])
        gbi = sb(st1, "gbi", [4, 2])
        dsel = sb(st1, "dsel", [4, 4, 16])
        par = sb(st1, "par", [128, 3, 16])
        sm = sb(st1, "sm", [128, 16, 16])
        smi = sb(st1, "smi", [128, 16], I32)
        st1.close()

        st2 = ExitStack()
        aq = sb(st2, "aq", [128, NP])
        ak = sb(st2, "ak", [128, NP])
        av = sb(st2, "av", [128, NP])
        az = sb(st2, "az", [128, NP])
        avn = sb(st2, "avn", [128, 8, 128])
        abias = sb(st2, "abias", [128, 2, BAND_KEYS])
        aS = sb(st2, "aS", [128, 2, BAND_KEYS])
        aPT = sb(st2, "aPT", [128, 2, BAND_KEYS])
        ast = sb(st2, "ast", [128, 2, 4])
        st2.close()

        st3 = ExitStack()
        kc = sb(st3, "kc", [128, 4, 512])
        vc = sb(st3, "vc", [128, 4, 512])
        sKT = sb(st3, "sKT", [128, 4, SK])
        sbias = sb(st3, "sbias", [128, SK])
        sS = sb(st3, "sS", [128, SK])
        sPT = sb(st3, "sPT", [128, 512])
        sPN = sb(st3, "sPN", [DT, 128])
        sq = sb(st3, "sq", [128, 4, NS])
        sk = sb(st3, "sk", [128, 4, NS])
        sv = sb(st3, "sv", [128, 4, NS])
        sz = sb(st3, "sz", [128, 4, NS])
        qblk = sb(st3, "qblk", [128, 4, 32])
        svb = sb(st3, "svb", [128, 4, DT])
        vnew = sb(st3, "vnew", [DT, 512])
        sst = sb(st3, "sst", [128, 4])
        st3.close()

        st4 = ExitStack()
        suP = sb(st4, "suP", [128, LC, NC])
        T1 = sb(st4, "T1", [128, NT])
        AC = sb(st4, "AC", [128, 2, 4, LC, 32])
        VT = sb(st4, "VT", [128, 2, LC, 128])
        Kbd = sb(st4, "Kbd", [128, LC, 128])
        E5 = sb(st4, "E5", [128, 2, 4, NCP + 1])
        XS = sb(st4, "XS", [128, 2, 4, NC + 1])
        u4 = [XS[:, :, :, :].rearrange("p r s n -> p (r s n)")[:, 0:NT], T1[:, :]]
        wq = sb(st4, "wq", [128, 2, 4, 32])
        BC = sb(st4, "BC", [128, 2, 2, 4, 32])
        s0 = sb(st4, "s0", [128, 2, 4, 8])
        FO = sb(st4, "FO", [128, 2, 4, 9])
        SX = sb(st4, "SX", [128, 2, 2, 4, 8])
        dD = sb(st4, "dD", [128, 4])
        st4.close()

        st5 = ExitStack()
        mqkv = sb(st5, "mqkv", [128, 2, 3, 4, 128])
        moz = sb(st5, "moz", [128, 2, 4, 128])
        mrow = sb(st5, "mrow", [4, 2, 3, 128])
        gs = sb(st5, "gs", [4, 2, 4, 128])
        q2 = sb(st5, "q2", [128, 4, 128])
        WT = sb(st5, "WT", [128, 4, 128])
        EM = sb(st5, "EM", [128, 4, 128])
        wsk = sb(st5, "wsk", [128, 4, 128])
        vn1 = sb(st5, "vn1", [128, 4, 129])
        CT = sb(st5, "CT", [128, 4, 129])
        hn = sb(st5, "hn", [128, 4, 128])
        yb = sb(st5, "yb", [128, 4, 128])
        md = sb(st5, "md", [128, 2, 4])
        st5.close()

        hstack.close()

        st6 = ExitStack()
        gl = sb(st6, "gl", [128, 4, NT])
        wg = sb(st6, "wg", [128, 4, 512])
        bg = sb(st6, "bg", [128, 4])
        gsz = sb(st6, "gsz", [128, NT])
        gsg = sb(st6, "gsg", [128, NT])
        t_hn = sb(st6, "t_hn", [128, 4, 128])
        t_md = sb(st6, "t_md", [128, 2, 4])
        nout = sb(st6, "nout", [128, 4, NSTR])
        t_oz = sb(st6, "t_oz", [128, 2, 4, 128])
        t_q2 = sb(st6, "t_q2", [128, 4, 128])
        t_WT = sb(st6, "t_WT", [128, 4, 128])
        t_EM = sb(st6, "t_EM", [128, 4, 128])
        t_wsk = sb(st6, "t_wsk", [128, 4, 128])
        t_vn1 = sb(st6, "t_vn1", [128, 4, 129])
        ct8 = sb(st6, "ct8", [128, 2, NSTR, 129])
        qm = sb(st6, "qm", [128, 2, NSTR * (128 + DT)])
        wkm = sb(st6, "wkm", [128, 2, NSTR, 128])
        nin = sb(st6, "nin", [128, 4, NSTR])
        wsm = sb(st6, "wsm", [128, 4, NSTR])
        cv = sb(st6, "cv", [128, 2, 4, NT])
        cub = sb(st6, "cub", [128, 2, NP + 2])
        cus = sb(st6, "cus", [128, 2, NSTR, DT + 2])
        cy = sb(st6, "cy", [128, 2, NT])
        cw = sb(st6, "cw", [128, 3, 4])
        cnat = sb(st6, "cnat", [128, 2, NSTR, 128])
        ohi = sb(st6, "ohi", [128, 2, 8, 512], R)
        olo = sb(st6, "olo", [128, 2, 8, 512], R)
        go = sb(st6, "go", [128, D])
        fst = sb(st6, "fst", [128, 3, 8])
        st6.close()

        st7 = ExitStack()
        orw = sb(st7, "orw", [128, 4, 2, 512])
        yr = sb(st7, "yr", [128, 4, 4, GC])
        yhi = sb(st7, "yhi", [128, KT, GC], R)
        ylo = sb(st7, "ylo", [128, KT, GC], R)
        xo = sb(st7, "xo", [128, 3, D])
        fo = sb(st7, "fo", [128, 3, D])
        st7.close()

        gt_in = sem("gt_in")
        gt_dve = sem("gt_dve")
        gt_act = sem("gt_act")
        gt_mm = sem("gt_mm")
        gt_rows = sem("gt_rows")
        qk_in, v_in, z_in, ab_in = sem("qk_in"), sem("v_in"), sem("z_in"), sem("ab_in")
        s_mm = sem("s_mm")
        s_add = sem("s_add")
        s_max = sem("s_max")
        e_done = sem("e_done")
        r_done = sem("r_done")
        p_done = sem("p_done")
        tp_mm = sem("tp_mm")
        tp_evac = sem("tp_evac")
        o_mm = sem("o_mm")
        y_done = sem("y_done")
        ay_stored = sem("ay_stored")
        ss_in = sem("ss_in")
        kc_in, vc_in = sem("kc_in"), sem("vc_in")
        kt_mm = sem("kt_mm")
        kt_ev = sem("kt_ev")
        kq_done = sem("kq_done")
        vt_mm = sem("vt_mm")
        vt_ev = sem("vt_ev")
        ss_mm = sem("ss_mm")
        ss_add = sem("ss_add")
        ss_max = sem("ss_max")
        ss_e = sem("ss_e")
        ss_r = sem("ss_r")
        ss_p = sem("ss_p")
        pt_mm = sem("pt_mm")
        pt_ev = sem("pt_ev")
        so_mm = sem("so_mm")
        sy_done = sem("sy_done")
        s5_in = sem("s5_in")
        su_in, bc_in = sem("su_in"), sem("bc_in")
        s5c = sem("s5c")
        s5a = sem("s5a")
        s5v = sem("s5v")
        su_done = sem("su_done")
        ab_done = sem("ab_done")
        vt5_mm = sem("vt5_mm")
        k5_mm = sem("k5_mm")
        vt5_ev = sem("vt5_ev")
        k5_ev = sem("k5_ev")
        x5_mm = sem("x5_mm")
        u4_in = [sem("u4_in0"), sem("u4_in1")]
        ca_done = sem("ca_done")
        xs_done = sem("xs_done")
        y5_mm = sem("y5_mm")
        t1_done = sem("t1_done")
        g5_done = sem("g5_done")
        g5_stored = sem("g5_stored")
        mq_in = [sem("mq_in0"), sem("mq_in1")]
        mo_in = sem("mo_in")
        gs_done = sem("gs_done")
        wb_mm, vn_mm, kn_mm, st_mm, d_mm = (sem(n) for n in ("wb_mm", "vn_mm", "kn_mm", "st_mm", "d_mm"))
        q2_done, wk_done, vn_done = sem("q2_done"), sem("wk_done"), sem("vn_done")
        em_done, wt_done = sem("em_done"), sem("wt_done")
        u_mm = sem("u_mm")
        ct_done = sem("ct_done")
        den_c = sem("den_c")
        w_turn = sem("w_turn")
        hn_done = sem("hn_done")
        oz_done = sem("oz_done")
        ht_mm = sem("ht_mm")
        my_done = sem("my_done")
        my_stored = sem("my_stored")
        zero_done = sem("zero_done")
        tq_in, c_in = sem("tq_in"), [sem("c_in0"), sem("c_in1")]
        ctt_mm, ctt_ev = sem("ctt_mm"), sem("ctt_ev")
        qm_done, wkm_done = sem("qm_done"), sem("wkm_done")
        tp_done, cu_mm, cn_mm = sem("tp_done"), sem("cu_mm"), sem("cn_mm")
        cdec, cu_done, c_out = sem("cdec"), sem("cu_done"), [sem("c_out0"), sem("c_out1")]
        n_done = sem("n_done")
        cv_in, cp_in = [sem("cv_in0"), sem("cv_in1")], sem("cp_in")
        cv_done = [sem("cv_done0"), sem("cv_done1")]
        cv_out = [sem("cv_out0"), sem("cv_out1")]
        gl_in = sem("gl_in")
        gz_in = sem("gz_in")
        gl_mm = sem("gl_mm")
        sg_done = sem("sg_done")
        gm_done = sem("gm_done")
        gy_done = sem("gy_done")
        gy_stored = sem("gy_stored")
        y_in = [sem(f"y_in{n}") for n in range(4)]
        yhi_done, ylo_done = sem("yhi_done"), sem("ylo_done")
        ow_in = [sem(f"ow_in{n}") for n in range(4)]
        ohi_done, olo_done = sem("ohi_done"), sem("olo_done")
        xo_in = sem("xo_in")
        ou_mm = sem("ou_mm")
        ob_mm = sem("ob_mm")
        xa_done = sem("xa_done")
        oq_done = sem("oq_done")
        f_done = sem("f_done")
        f_stored = sem("f_stored")
        kv_out = sem("kv_out")

        def gemm_segs(step, steps, tiles):
            cuts = steps if isinstance(steps, tuple) else [n * 6 * tiles // steps for n in range(steps + 1)]
            for s in range(cuts[step], cuts[step + 1]):
                yield s // 6, (s % 6) // 3, s % 3

        def yslot(p):
            return (0, 1, 3, 2)[p]

        def outbank(c, a):
            return G[:, a] if c % 2 == 0 else X[:, a]

        class Chain:

            def __init__(self, eng, on, base=0):
                self.eng, self.on, self.base, self.count = eng, on, base, 0

            def __call__(self, ins):
                self.count += 1
                ins.then_inc(self.on, 1)
                self.eng.wait_ge(self.on, self.base + self.count)

        def rows_of_streams(a):
            return a[:, NP:NT].rearrange("p (b t) -> p b t", b=NSTR)

        def conv_in(eng, e, own, f):
            s = f % 2
            if f >= 2:
                eng.wait_ge(cv_out[s], 48)
            own(e.memset(cub[:, s, 0:2], 0.0))
            eng.wait_ge(cv_in[s], 80 * (f // 2) + 80)
            own(e.tensor_tensor(cub[:, s, 2:], cv[:, s, 1, 0:NP], cv[:, s, 2, 0:NP], ALU.mult))
            own(e.tensor_tensor(cus[:, s, :, 2:], rows_of_streams(cv[:, s, 1]), rows_of_streams(cv[:, s, 2]), ALU.mult))

        def conv_taps(e, own, f):
            s = f % 2
            outs = (cy[:, s, 0:NP], rows_of_streams(cy[:, s]))
            parts = (cv[:, s, 1, 0:NP], rows_of_streams(cv[:, s, 1]))
            for j in range(3):
                for o, part, x in zip(outs, parts, (cub[:, s, j:j + NP], cus[:, s, :, j:j + DT])):
                    if j == 0:
                        own(e.tensor_scalar(o, x, cw[:, 0, f:f + 1], None, ALU.mult))
                    elif s == 0:
                        own(e.scalar_tensor_tensor(o, x, cw[:, j, f:f + 1], o, ALU.mult, ALU.add))
                    else:
                        own(e.tensor_scalar(part, x, cw[:, j, f:f + 1], None, ALU.mult))
                        own(e.tensor_tensor(o, o, part, ALU.add))

        def conv_out(e, own, f):
            s = f % 2
            own(e.tensor_tensor(cy[:, s], cy[:, s], cv[:, s, 0], ALU.mult))
            e.tensor_tensor(cy[:, s], cy[:, s], cv[:, s, 3], ALU.mult).then_inc(cv_done[s], 1)

        block = top.enter_context(nc.Block())

        @block.sync
        def _(sp):
            def load_w(T, kh):
                sp.wait_ge(w_split, 2 * T + kh + 1)
                sp.dma_start(wr[:, kh], w_in_t[T, :, 8 * kh:8 * kh + 8, :]).then_inc(wraw[kh], 16)

            def store_u(T, j):
                sp.wait_ge(evac_done, 3 * T + j + 4)
                sp.dma_start(uT[T, :, GC * j:GC * j + GC], ev[:, j]).then_inc(u_stored[j], 16)

            def gemm(T, kh, j, more=True):
                if j == 0 and more:
                    load_w(T + 1, kh)
                if kh == 1:
                    store_u(T, j)

            def stored(T):
                for j in range(3):
                    sp.wait_ge(u_stored[j], 16 * T + 32)

            def gemms(base, step, steps, tiles, last=False):
                for t, kh, j in gemm_segs(step, steps, tiles):
                    gemm(base + t, kh, j, not (last and t == tiles - 1))


            def load_x(t, s):
                sp.wait_ge(xt_mm, 4 * t + 4)
                sp.dma_start(xin[:, s], x_all[ds(t * 128, 128), :]).then_inc(x_in[s], 16)

            load_x(0, 0)
            sp.dma_start(gb[:, :], g_in).then_inc(g_loaded, 16)
            for s in range(1, 4):
                load_x(s, s)
            for s in range(4):
                load_x(4 + s, s)
            load_x(8, 0)
            load_w(0, 0)
            load_w(0, 1)
            for kh in range(2):
                for j in range(3):
                    gemm(0, kh, j)
            stored(T_GATE)
            sp.dma_start(gI[:, :], uT[0, 0:4, :]).then_inc(gt_in, 16)
            sp.dma_start(gF[:, :], uT[0, 32:36, :]).then_inc(gt_in, 16)
            sp.dma_start(gbi[:, :], b_if).then_inc(gt_in, 16)
            sp.dma_start(gsm[:, 0, 8:16], m_init).then_inc(gt_in, 16)
            sp.dma_start(par[:, :, :], s5_par).then_inc(s5_in, 16)
            with sp.Fori(0, 3) as i:
                gemms(1 + 4 * i, 0, 1, 4)
            sp.wait_ge(gt_dve, GATE_ROWS)
            sp.wait_ge(gt_act, GATE_WINT)
            sp.dma_start(rows[:, 0, :], gB[:, :]).then_inc(gt_rows, 16)
            sp.dma_start(rows[:, 1, :], gR[0:4, :]).then_inc(gt_rows, 16)
            sp.dma_start(rows[:, 2, :], gA[:, :]).then_inc(gt_rows, 16)
            sp.dma_start(m_last, gsm[:, 2, :]).then_inc(gt_rows, 16)
            gemms(13, 0, 2, 4)

            def load_pair(i):
                sp.wait_ge(s_mm, 16 * i + 1)
                sp.dma_start(aq[:, :], uT[1 + 4 * i, :, 0:NP]).then_inc(qk_in, 16)
                sp.dma_start(ak[:, :], uT[2 + 4 * i, :, 0:NP]).then_inc(qk_in, 16)
                sp.wait_ge(s_add, 16 * i + 1)
                sp.dma_start(abias[:, :, :], bias_p[ds(2 * i, 2)].rearrange("h p n -> p h n")).then_inc(ab_in, 16)
                sp.dma_start(av[:, :], uT[3 + 4 * i, :, 0:NP]).then_inc(v_in, 16)

            def load_keys(b):
                sp.wait_ge(s_mm, 65)
                sp.wait_ge(kt_mm, 4 * b + 4)
                sp.dma_start(kc[:, :, :], k_cache[b].rearrange("(t p) n -> p t n", p=128)).then_inc(kc_in, 16)

            def attention(i, last):
                sp.wait_ge(ay_stored, 16 * i + 16)
                sp.dma_start(az[:, :], uT[4 + 4 * i, :, 0:NP]).then_inc(z_in, 16)
                for src, dst in ((k_cache, k_shift), (v_cache, v_shift)):
                    sp.dma_start(dst[ds(2 * i, 2)], src[ds(2 * i, 2), DT:512, :]).then_inc(outs_done, 16)
                for u in range(16):
                    gemms(17 + 4 * i, u, 16, 4)
                    if u == 14 and not last:
                        sp.wait_ge(tp_mm, 17 * i + 17)
                        load_pair(i + 1)
                    if u == 14 and last:
                        load_keys(0)
                sp.wait_ge(y_done, 16 * i + 17)
                sp.dma_start(yT[i, :, 0:NP], az[:, :]).then_inc(ay_stored, 16)

            sp.wait_ge(gt_rows, 64)
            sp.wait_ge(gt_dve, GATE_END)
            sp.wait_ge(s5c, S5_PREP)
            load_pair(0)
            gemms(13, 1, 2, 4)
            stored(T_ATT(3, 3))
            for i in range(4):
                for k in range(2):
                    sp.dma_start(kv_new[i, k], uT[T_ATT(i, 1 + k), :, 512:NT]).then_inc(kv_out, 16)
            with sp.Fori(0, 3) as i:
                attention(i, False)
            attention(3, True)
            sp.wait_ge(ay_stored, 80)
            sp.wait_ge(o_mm, 64)
            sp.wait_ge(p_done, 64)
            sp.wait_ge(tp_evac, 69)

            for n, dst in enumerate((sq, sk, sv, sz)):
                for i in range(4):
                    sp.dma_start(dst[:, i], uT[T_ATT(i, n), :, NP:NT]).then_inc(ss_in, 16)
            sp.dma_start(sbias[:, :], bias_s).then_inc(ss_in, 16)
            def streams(i, last):
                for s in range(2):
                    b = 2 * i + s
                    sp.wait_ge(so_mm, b + 1)
                    sp.dma_start(vc[:, :, :], v_cache[b].rearrange("(t p) n -> p t n", p=128)).then_inc(vc_in, 16)
                    if not (last and s == 1):
                        load_keys(b + 1)
                    gemms(33 + 2 * i, s, 2, 2)

            with sp.Fori(0, 3) as i:
                streams(i, False)
            streams(3, True)
            sp.wait_ge(sy_done, 9)
            for i in range(4):
                sp.dma_start(yT[i, :, NP:NT], sz[:, i]).then_inc(ay_stored, 16)
            sp.wait_ge(ay_stored, 144)
            sp.wait_ge(so_mm, 9)

            sp.dma_start(dD[:, :], s5_d).then_inc(s5_in, 16)
            def load_u4(f, st):
                for g in range(4):
                    src = uT[20 + 4 * f, 32 * st:32 * st + 32]
                    sp.dma_start(u4[st % 2][32 * g:32 * g + 32, 0:NS - 3 + g], src[:, NP + 3 - g:NT]).then_inc(u4_in[st % 2], 16)
                    sp.dma_start(u4[st % 2][32 * g:32 * g + 32, NS:NT - 3 + g], src[:, 3 - g:NP]).then_inc(u4_in[st % 2], 16)

            with sp.Fori(0, 4) as f:
                sp.wait_ge(g5_stored, 32 * f + 16)
                sp.dma_start(T1[:, :], uT[20 + 4 * f]).then_inc(su_in, 16)
                sp.wait_ge(ca_done, f + 1)
                sp.dma_start(BC[:, 0], s5_b[:, :, ds(4 * f, 4), :]).then_inc(bc_in, 16)
                sp.dma_start(BC[:, 1], s5_c[:, :, ds(4 * f, 4), :]).then_inc(bc_in, 16)
                sp.wait_ge(xs_done, f + 1)
                sp.dma_start(s0[:, :, :, :], s5_s0[:, :, ds(4 * f, 4), :]).then_inc(bc_in, 16)
                sp.wait_ge(t1_done, 3 * f + 3)
                load_u4(f, 0)
                gemms(41 + 3 * f, 0, S5_CUTS, 3)
                sp.wait_ge(su_done, 2 * f + 2)
                load_u4(f, 1)
                gemms(41 + 3 * f, 1, S5_CUTS, 3)
                for n, (t, kh, j) in enumerate(gemm_segs(2, S5_CUTS, 3)):
                    if n < 2:
                        sp.wait_ge(x5_mm, 4 * f + n + 1)
                        load_u4(f, n + 2)
                    gemm(41 + 3 * f + t, kh, j)
                gemms(41 + 3 * f, 3, S5_CUTS, 3)
                gemms(41 + 3 * f, 4, S5_CUTS, 3)
                sp.wait_ge(g5_done, 3 * f + 3)
                sp.dma_start(gS5[f], T1[:, :]).then_inc(g5_stored, 16)
                sp.wait_ge(xs_done, f + 2)
                sp.dma_start(s5_last[:, :, ds(4 * f, 4), :], FO[:, :, :, :]).then_inc(g5_stored, 16)
            sp.wait_ge(g5_stored, 144)
            sp.wait_ge(y5_mm, 12)

            def load_chunk(c, s):
                sp.wait_ge(my_done, c + 1)
                for n in range(3):
                    sp.dma_start(mqkv[:, s, n], uT[17 + n:30 + n:4, :, ds(c * 128, 128)].rearrange("h p n -> p h n")).then_inc(mq_in[s], 16)
                sp.dma_start(mrow[:, s], rows[:, :, ds(c * 128, 128)]).then_inc(mq_in[s], 16)

            def mlstm(i, last):
                for s in range(2):
                    c = 2 * i + s
                    sp.wait_ge(my_done, c + 2)
                    for n in range(2):
                        sp.dma_start(moz[:, n], uT[33 + n:40 + n:2, :, ds(c * 128, 128)].rearrange("h p n -> p h n")).then_inc(mo_in, 16)
                    load_chunk(c + 1, 1 - s)
                    for u in range(3):
                        gemms(53 + 2 * i, 3 * s + u, 6, 2, last)
                    sp.wait_ge(my_done, c + 3)
                    sp.dma_start(yT[4:8, :, ds(c * 128, 128)].rearrange("h p n -> p h n"), yb[:, :, :]).then_inc(my_stored, 16)

            load_chunk(0, 0)
            with sp.Fori(0, 3) as i:
                mlstm(i, False)
            mlstm(3, True)
            sp.wait_ge(ct_done, 9)
            sp.dma_start(c_prompt.rearrange("h k v -> k h v"), CT[:, :, 0:128]).then_inc(outs_done, 16)
            sp.dma_start(n_prompt, CT[:, :, 128], allow_slow_non_contiguous=True).then_inc(outs_done, 16)
            sp.wait_ge(bank_full, 3 * NTILES + 3)
            sp.wait_ge(w_split, 2 * NTILES + 2)

            for n in range(2):
                sp.dma_start(t_oz[:, n], uT[33 + n:40 + n:2, :, NP:NT].rearrange("h p n -> p h n")).then_inc(tq_in, 16)
            sp.dma_start(nin[:, :, :], n_init).then_inc(tq_in, 16)
            sp.dma_start(wg[:, :, :], w_glu).then_inc(gl_in, 16)
            sp.dma_start(bg[:, :], b_glu).then_inc(gl_in, 16)
            sp.dma_start(gl[:, :, :], gS5.rearrange("f p n -> p f n")).then_inc(gl_in, 16)

            def load_conv(f):
                s = f % 2
                if f >= 2:
                    sp.wait_ge(cv_done[s], 1)
                    sp.wait_ge(cv_out[s], 48)
                sp.dma_start(cv[:, s, 1], uT[T_S5(f, 1)]).then_inc(cv_in[s], 16)
                sp.dma_start(cv[:, s, 2], uT[T_CV(f, 0)]).then_inc(cv_in[s], 16)
                sp.dma_start(cv[:, s, 0], uT[T_S5(f, 0)]).then_inc(cv_in[s], 16)
                sp.dma_start(cv[:, s, 3], uT[T_CV(f, 1)]).then_inc(cv_in[s], 16)
                sp.dma_start(cus[:, s, :, 0:2], conv_buf[f]).then_inc(cv_in[s], 16)

            def store_conv(f):
                s = f % 2
                sp.wait_ge(cv_done[s], f // 2 + 1)
                sp.dma_start(yT[8 + f], cy[:, s]).then_inc(cv_out[s], 16)
                sp.dma_start(conv_p[f], cub[:, s, NP:NP + 2]).then_inc(cv_out[s], 16)
                sp.dma_start(conv_s[f], cus[:, s, :, DT:DT + 2]).then_inc(cv_out[s], 16)

            def load_out_w(t, c, kh):
                for p in range(4 * kh, 4 * kh + 4):
                    sp.wait_ge(olo_done, 32 * t + 8 * c + p + 1)
                    sp.dma_start(orw[:, p % 4], w_out_t[c, :, 2 * p:2 * p + 2, :]).then_inc(ow_in[p % 4], 16)

            def load_y(t, p):
                sp.wait_ge(ylo_done, 4 * t + p + 1)
                sp.dma_start(yr[:, yslot(p)], yT[4 * p:4 * p + 4, :, t * GC:t * GC + GC].rearrange("k p n -> p k n")).then_inc(y_in[p], 16)

            stored(NTILES - 1)
            sp.dma_start(cw[:, :, :], conv_w).then_inc(cp_in, 16)
            load_conv(1)
            sp.dma_start(gsz[:, :], uT[T_S5(0, 2)]).then_inc(gz_in, 16)
            load_conv(0)
            sp.dma_start(cnat[:, 0], c_init[0]).then_inc(c_in[0], 16)
            sp.dma_start(cnat[:, 1], c_init[1]).then_inc(c_in[1], 16)
            for f in range(4):
                sp.wait_ge(gy_done, f + 1)
                sp.dma_start(yT[12 + f], gsz[:, :]).then_inc(gy_stored, 16)
                if f < 3:
                    sp.wait_ge(gy_stored, 16 * f + 16)
                    sp.dma_start(gsz[:, :], uT[T_S5(f + 1, 2)]).then_inc(gz_in, 16)
            store_conv(1)
            load_conv(3)
            for h in range(4):
                sp.wait_ge(cu_done, h + 1)
                sp.dma_start(c_stream[h], cnat[:, h % 2]).then_inc(c_out[h % 2], 16)
                if h < 2:
                    sp.wait_ge(c_out[h], 16)
                    sp.dma_start(cnat[:, h], c_init[h + 2]).then_inc(c_in[h], 16)
                if h == 1:
                    store_conv(0)
                    load_conv(2)
                    sp.wait_ge(gy_stored, 64)
                    sp.wait_ge(outs_done, 16 * 10)
                    sp.wait_ge(my_stored, 16 * 9)
                    sp.wait_ge(gl_mm, 12)
                    load_out_w(0, 0, 0)
                    for p in (0, 1, 3):
                        load_y(0, p)

            sp.wait_ge(n_done, 4)
            sp.dma_start(n_stream, nout[:, :, :]).then_inc(outs_done, 16)
            sp.wait_ge(my_done, 11)
            sp.dma_start(yT[4:8, :, NP:NT].rearrange("h p n -> p h n"), t_hn[:, :, :]).then_inc(my_stored, 16)
            store_conv(3)
            store_conv(2)
            load_out_w(0, 0, 1)
            sp.wait_ge(outs_done, 16 * 11)
            sp.wait_ge(cv_out[0], 96)
            sp.wait_ge(cv_out[1], 96)
            sp.wait_ge(c_out[0], 32)
            sp.wait_ge(c_out[1], 32)
            sp.wait_ge(my_stored, 160)

            load_y(0, 2)
            sp.dma_start(xo[:, :, :], x_all[0:GC, :].rearrange("(a p) n -> p a n", p=128)).then_inc(xo_in, 16)
            sp.dma_start(go[:, :], g_out).then_inc(g_loaded, 16)
            for t in range(3):
                for c in range(4):
                    if c < 3:
                        if t == 0 or c > 0:
                            load_out_w(t, c + 1, 0)
                        load_out_w(t, c + 1, 1)
                    elif t < 2:
                        for kh in range(2):
                            load_y(t + 1, 2 * kh)
                            load_y(t + 1, 2 * kh + 1)
                            load_out_w(t + 1, 0, kh)
                        load_out_w(t + 1, 1, 0)
                for a in range(3):
                    sp.wait_ge(f_done, 3 * t + a + 4)
                    sp.dma_start(y_all[(3 * t + a) * 128:(3 * t + a + 1) * 128, :], fo[:, a]).then_inc(f_stored, 16)
                if t < 2:
                    sp.dma_start(xo[:, :, :], x_all[GC * (t + 1):GC * (t + 2), :].rearrange("(a p) n -> p a n", p=128)).then_inc(xo_in, 16)
            sp.wait_ge(f_stored, 16 * 10)
            sp.wait_ge(kv_out, 128)

        @block.gpsimd
        def _(pool):
            g = nc.gpsimd
            for s, n in ((xt_mm, 16), (h_done, 4), (w_split, 2), (half0_mm, 1), (bank_full, 3), (evac_done, 3),
                         (u_stored[0], 16), (u_stored[1], 16), (u_stored[2], 16), (s_mm, 1), (s_add, 1),
                         (tp_mm, 1), (tp_evac, 1), (y_done, 1), (ay_stored, 16), (kt_mm, 4), (so_mm, 1), (sy_done, 1),
                         (g5_stored, 16), (gs_done, 1), (ct_done, 1), (hn_done, 1), (my_done, 2), (my_stored, 16),
                         (ca_done, 1), (xs_done, 1), (t1_done, 3), (sg_done, 3), (ylo_done, 4), (olo_done, 4), (f_done, 3), (f_stored, 16),
                         (xa_done, 6), (ou_mm, 1), (ob_mm, 1)):
                pool.sem_inc(s, n)
            g.memset(ident[:, :], 0.0).then_inc(const_done, 1)
            g.memset(mask_p[:, :], 0.0).then_inc(const_done, 1)
            g.memset(mask_s[:, :], 0.0).then_inc(const_done, 1)
            g.memset(bmask[:, :], 1.0).then_inc(const_done, 1)
            g.memset(ones4[:, :], 1.0).then_inc(const_done, 1)
            g.memset(onec[:, :], 1.0).then_inc(const_done, 1)
            g.memset(sel[:, :, :], 0.0).then_inc(const_done, 1)
            pool.wait_ge(const_done, 7)
            g.affine_select(out=ident[:, :], in_=ident[:, :], compare_op=ALU.not_equal, fill=1.0, base=0,
                            pattern=[[-1, 128]], channel_multiplier=1).then_inc(const_done, 1)
            g.affine_select(out=mask_p[:, :], in_=mask_p[:, :], compare_op=ALU.is_ge, fill=NEG, base=0,
                            pattern=[[1, 128]], channel_multiplier=-1).then_inc(const_done, 1)
            g.affine_select(out=mask_s[:, :], in_=mask_s[:, :], compare_op=ALU.is_ge, fill=NEG, base=0,
                            pattern=[[1, 128]], channel_multiplier=-1).then_inc(const_done, 1)
            g.affine_select(out=bmask[:, :], in_=bmask[:, :], compare_op=ALU.is_ge, fill=0.0, base=0,
                            pattern=[[-DT, NSTR]], channel_multiplier=1).then_inc(const_done, 1)
            g.affine_select(out=sel[:, :, :], in_=sel[:, :, :], compare_op=ALU.not_equal, fill=1.0, base=0,
                            pattern=[[-1, 4], [0, 128]], channel_multiplier=1).then_inc(const_done, 1)
            pool.wait_ge(const_done, 12)
            g.affine_select(out=mask_s[:, :].rearrange("p (b t) -> p b t", t=DT),
                            in_=mask_s[:, :].rearrange("p (b t) -> p b t", t=DT), compare_op=ALU.is_ge, fill=NEG,
                            base=0, pattern=[[-DT, NSTR], [0, DT]], channel_multiplier=1).then_inc(const_done, 1)
            g.affine_select(out=bmask[:, :], in_=bmask[:, :], compare_op=ALU.is_ge, fill=0.0, base=DT - 1,
                            pattern=[[DT, NSTR]], channel_multiplier=-1).then_inc(const_done, 1)
            with pool.Fori(0, NTILES) as T:
                for kh in range(2):
                    pool.wait_ge(wraw[kh], 16 * T + 16)
                    if kh == 0:
                        pool.wait_ge(half0_mm, T + 1)
                    else:
                        pool.wait_ge(bank_full, 3 * T + 3)
                    pool.sem_inc(w_turn, 1)
                    g.tensor_copy(whi[:, kh], wr[:, kh]).then_inc(whi_done, 1)
                    pool.wait_ge(whi_done, 2 * T + kh + 1)
                    g.tensor_tensor(wlo[:, kh], wr[:, kh], whi[:, kh].bitcast(F), ALU.subtract).then_inc(w_split, 1)
            pool.wait_ge(cp_in, 16)
            pool.wait_ge(cv_in[1], 80)
            own = Chain(pool, w_turn, 2 * NTILES)
            for f in (1, 3):
                conv_in(pool, g, own, f)
                conv_taps(g, own, f)
                conv_out(g, own, f)

        @block.tensor
        def _(pe):
            mm = nc.tensor.matmul
            tr = nc.tensor.transpose

            def gemm(T, kh, j, first=False):
                if j == 0:
                    pe.wait_ge(w_split, 2 * T + kh + 3)
                if first:
                    pe.wait_ge(h_done, 4 + 12 * (j + 1))
                if kh == 0:
                    pe.wait_ge(evac_done, 3 * T + j + 1)
                for k in range(8):
                    kk = 8 * kh + k
                    hs = slice(GC * j, GC * j + GC)
                    mm(G[:, j, 0:GC], whi[:, kh, k], hhi[:, kk, hs], start=(kk == 0), stop=False)
                    mm(G[:, j, 0:GC], whi[:, kh, k], hlo[:, kk, hs], start=False, stop=False)
                    last = mm(G[:, j, 0:GC], wlo[:, kh, k], hhi[:, kk, hs], start=False, stop=(kk == 15))
                if kh == 1:
                    last.then_inc(bank_full, 1)
                elif j == 2:
                    last.then_inc(half0_mm, 1)

            def gemms(base, step, steps, tiles):
                for t, kh, j in gemm_segs(step, steps, tiles):
                    gemm(base + t, kh, j)

            pe.wait_ge(const_done, 14)

            def xpose(t, s):
                pe.wait_ge(xn_done, t + 1)
                for qd in range(4):
                    pe.wait_ge(h_done, 4 * t + qd + 1)
                    for k in range(4):
                        last = tr(X[:, qd, 128 * k:128 * k + 128],
                                  xin[:, s, 512 * qd + 128 * k:512 * qd + 128 * k + 128], ident[:, :])
                    last.then_inc(xt_mm, 1)

            with pe.Fori(0, 2) as i:
                for s in range(4):
                    xpose(4 * i + s, s)
            xpose(8, 0)
            for kh in range(2):
                for j in range(3):
                    gemm(0, kh, j, first=True)
            with pe.Fori(0, 3) as i:
                gemms(1 + 4 * i, 0, 1, 4)
            pe.wait_ge(gt_act, GATE_R)
            for t in range(TT):
                last = tr(X[:, t // 5, 96 * (t % 5):96 * (t % 5) + 96], gR[0:96, 128 * t:128 * t + 128],
                          ident[0:96, 0:96])
            last.then_inc(gt_mm, 1)
            pe.wait_ge(gt_dve, GATE_DSEL)
            mm(X[:, 2, 0:64], ones4[:, :], dsel[:, :, :].rearrange("p a b -> p (a b)"), start=True, stop=True).then_inc(gt_mm, 1)
            gemms(13, 0, 1, 4)
            pe.wait_ge(gt_dve, GATE_END)

            def span(u):
                g = u % 8
                return g, max(0, g - 4), min(g + 1, 5)

            with pe.Fori(0, 4) as i:
                pe.wait_ge(v_in, 16 * i + 16)
                pe.wait_ge(tp_evac, 17 * i + 1)
                for t in range(8):
                    last = tr(T2[:, 128 * t:128 * t + 128], av[:, 128 * t:128 * t + 128], ident[:, :])
                last.then_inc(tp_mm, 1)
                pe.wait_ge(qk_in, 32 * i + 32)

                def scores(u):
                    g, k0, nk = span(u)
                    ps = slice(64 * (u // 8), 64 * (u // 8) + 64)
                    pe.wait_ge(s_add, 16 * i + u + 1)
                    n = 128 * nk
                    last = mm(X2[:, 0:min(n, 512)], aq[ps, 128 * g:128 * g + 128],
                              ak[ps, 128 * k0:128 * k0 + min(n, 512)], start=True, stop=True)
                    if n > 512:
                        last = mm(X2[:, 512:n], aq[ps, 128 * g:128 * g + 128],
                                  ak[ps, 128 * k0 + 512:128 * k0 + n], start=True, stop=True)
                    last.then_inc(s_mm, 1)

                scores(0)
                for u in range(16):
                    g, k0, nk = span(u)
                    ps = slice(64 * (u // 8), 64 * (u // 8) + 64)
                    if u < 15:
                        scores(u + 1)
                    pe.wait_ge(p_done, 16 * i + u + 1)
                    pe.wait_ge(tp_evac, 17 * i + u + 2)
                    for t in range(nk):
                        last = tr(T2[:, 128 * t:128 * t + 128], aS[:, u % 2, 128 * t:128 * t + 128], ident[:, :])
                    last.then_inc(tp_mm, 1)
                    gemms(17 + 4 * i, u, 16, 4)
                    pe.wait_ge(tp_evac, 17 * i + u + 3)
                    pe.wait_ge(y_done, 16 * i + u + 1)
                    for t in range(nk):
                        last = mm(X[ps, 4, 0:128], avn[:, k0 + t, 64 * (u // 8):64 * (u // 8) + 64],
                                  aPT[:, u % 2, 128 * t:128 * t + 128], start=(t == 0), stop=(t == nk - 1))
                    last.then_inc(o_mm, 1)

            with pe.Fori(0, 4) as i:
                for s in range(2):
                    b = 2 * i + s
                    tg = list(gemm_segs(s, 2, 2))
                    for t, kh, j in tg[:2]:
                        gemm(33 + 2 * i + t, kh, j)
                    pe.wait_ge(s_add, 65)
                    pe.wait_ge(y_done, 65)
                    pe.wait_ge(kc_in, 16 * b + 16)
                    pe.wait_ge(sy_done, b + 1)
                    for t in range(4):
                        for hp in range(4):
                            last = tr(X[:, t, 128 * hp:128 * hp + 128], kc[:, t, 128 * hp:128 * hp + 128], ident[:, :])
                        last.then_inc(kt_mm, 1)
                    pe.wait_ge(kq_done, 4 * b + 1)
                    for hp in range(4):
                        last = tr(X[0:DT, 4, 128 * hp:128 * hp + 128], svb[:, hp], ident[:, :])
                    last.then_inc(vt_mm, 1)
                    for t, kh, j in tg[2:3]:
                        gemm(33 + 2 * i + t, kh, j)
                    pe.wait_ge(kt_ev, 4 * b + 4)
                    pe.wait_ge(kq_done, 4 * b + 4)
                    for hp in range(4):
                        mm(X2[32 * hp:32 * hp + 32, 0:512], qblk[:, hp], sKT[:, hp, 0:512], start=True, stop=True)
                    for hp in range(4):
                        last = mm(X2[32 * hp:32 * hp + 32, 512:SK], qblk[:, hp], sKT[:, hp, 512:SK], start=True, stop=True)
                    last.then_inc(ss_mm, 1)
                    for t, kh, j in tg[3:5]:
                        gemm(33 + 2 * i + t, kh, j)
                    pe.wait_ge(ss_p, b + 1)
                    for t in range(4):
                        tr(X[:, 2, 128 * t:128 * t + 128], sS[:, 128 * t:128 * t + 128], ident[:, :])
                    tr(X[0:DT, 3, 0:128], sS[:, 512:SK], ident[:, :]).then_inc(pt_mm, 1)
                    pe.wait_ge(vc_in, 16 * b + 16)
                    pe.wait_ge(vt_ev, b + 1)
                    for t, kh, j in tg[5:6]:
                        gemm(33 + 2 * i + t, kh, j)
                    pe.wait_ge(pt_ev, 2 * b + 2)
                    for hp in range(4):
                        for t in range(4):
                            mm(X[:, 4, 32 * hp:32 * hp + 32], vc[:, t, 128 * hp:128 * hp + 128],
                               sPT[:, 128 * t + 32 * hp:128 * t + 32 * hp + 32], start=(t == 0), stop=False)
                        last = mm(X[:, 4, 32 * hp:32 * hp + 32], vnew[:, 128 * hp:128 * hp + 128],
                                  sPN[:, 32 * hp:32 * hp + 32], start=False, stop=True)
                    last.then_inc(so_mm, 1)

            with pe.Fori(0, 4) as f:
                gemms(41 + 3 * f, 0, S5_CUTS, 3)
                pe.wait_ge(sy_done, 9)
                pe.wait_ge(ab_done, f + 1)
                pe.wait_ge(t1_done, 3 * f + 3)
                for ri in range(2):
                    for hf in range(2):
                        for st in range(4):
                            last = tr(X[:, 2 * ri + hf, 128 * st:128 * st + 128],
                                      AC[:, ri, st, 4 - 4 * hf:8 - 4 * hf].rearrange("p t c -> p (t c)"), ident[:, :])
                        last.then_inc(vt5_mm, 1)
                for t in range(LC):
                    for st in range(4):
                        o = X[32 * st:32 * st + 32, 4, 32 * t:32 * t + 32]
                        mm(o, AC[:, 0, st, t], BC[:, 1, 0, st], start=True, stop=False)
                        last = mm(o, AC[:, 1, st, t], BC[:, 1, 1, st], start=False, stop=True)
                last.then_inc(k5_mm, 1)
                gemms(41 + 3 * f, 1, S5_CUTS, 3)
                pe.wait_ge(vt5_ev, 4 * f + 4)
                pe.wait_ge(su_done, 2 * f + 2)
                between = list(gemm_segs(2, S5_CUTS, 3))
                for st in range(4):
                    pe.wait_ge(u4_in[st % 2], 256 * f + 128 * (st // 2) + 128)
                    for ri in range(2):
                        for hf in range(2):
                            last = mm(X[:, st, NC * ri:NC * ri + NC], VT[:, ri, 4 * hf + st], u4[st % 2][:, 4 * hf:NT:LC],
                                      start=(hf == 0), stop=(hf == 1))
                    last.then_inc(x5_mm, 1)
                    if st < 3:
                        t, kh, j = between[st]
                        gemm(41 + 3 * f + t, kh, j)
                gemms(41 + 3 * f, 3, S5_CUTS, 3)
                pe.wait_ge(k5_ev, f + 1)
                pe.wait_ge(ca_done, f + 2)
                pe.wait_ge(xs_done, f + 2)
                for bk, (i0, i1) in enumerate(((0, 3), (3, 6), (6, 8))):
                    for st in range(4):
                        for i in range(i0, i1):
                            for ri in range(2):
                                mm(X[32 * st:32 * st + 32, bk, NC * (i - i0):NC * (i - i0) + NC],
                                   AC[:, ri, st, i], XS[:, ri, st, 0:NC],
                                   start=(i == i0 and ri == 0), stop=False)
                    for t in range(i1 - 1, -1, -1):
                        a = max(i0, t)
                        last = mm(X[:, bk, NC * (a - i0):NC * (i1 - i0)], Kbd[:, t],
                                  suP[:, a - t:i1 - t].rearrange("p a n -> p (a n)"), start=False, stop=(t == 0))
                    last.then_inc(y5_mm, 1)
                gemms(41 + 3 * f, 4, S5_CUTS, 3)

            def ml_front(c, qkv, row, g2, mask, waits):
                pe.wait_ge(gs_done, c + 2)
                waits()
                mm(X[:, 2], ones4[:, :], g2[:, 1].rearrange("p a b -> p (a b)"), start=True, stop=True).then_inc(wb_mm, 1)
                for h in range(4):
                    last = tr(X[:, 3, 128 * h:128 * h + 128], qkv[2][:, h], ident[:, :])
                last.then_inc(vn_mm, 1)
                for h in range(4):
                    last = tr(X[:, 4, 128 * h:128 * h + 128], qkv[1][:, h], ident[:, :])
                last.then_inc(kn_mm, 1)
                for h in range(4):
                    last = mm(X[:, 0, 128 * h:128 * h + 128], qkv[1][:, h], qkv[0][:, h], start=True, stop=True)
                last.then_inc(st_mm, 1)
                for h in range(4):
                    mm(X[:, 1, 128 * h:128 * h + 128], ident[:, :], mask[:, :], start=(h == 0), stop=False)
                mm(X[:, 1], row[:, 2], sel[:, :, :].rearrange("p a b -> p (a b)"), start=False, stop=False)
                last = mm(X[:, 1], ones4[:, :], g2[:, 0].rearrange("p a b -> p (a b)"), start=False, stop=True)
                last.then_inc(d_mm, 1)

            with pe.Fori(0, 4) as i:
                for s in range(2):
                    c = 2 * i + s

                    def waits():
                        pe.wait_ge(t1_done, 15)
                        pe.wait_ge(mq_in[s], 64 * i + 64)
                        pe.wait_ge(ct_done, c + 1)
                        pe.wait_ge(hn_done, c + 1)
                        pe.wait_ge(my_done, c + 2)

                    gemms(53 + 2 * i, 3 * s, 6, 2)
                    ml_front(c, [mqkv[:, s, n] for n in range(3)], mrow[:, s], gs, mask_p, waits)
                    gemms(53 + 2 * i, 3 * s + 1, 6, 2)
                    pe.wait_ge(q2_done, c + 1)
                    pe.wait_ge(wt_done, c + 1)
                    pe.wait_ge(vn_done, c + 1)
                    for h in range(4):
                        o = X[:, 2 + h // 2, 129 * (h % 2):129 * (h % 2) + 129]
                        mm(o, q2[:, h], CT[:, h], start=True, stop=False)
                        last = mm(o, WT[:, h], vn1[:, h], start=False, stop=True)
                    pe.wait_ge(wk_done, c + 1)
                    for h in range(4):
                        last = mm(X[:, 4 * (h // 2), 129 * (h % 2):129 * (h % 2) + 129], wsk[:, h], vn1[:, h],
                                  start=True, stop=True)
                    last.then_inc(u_mm, 1)
                    gemms(53 + 2 * i, 3 * s + 2, 6, 2)
                    pe.wait_ge(hn_done, c + 2)
                    for h in range(4):
                        last = tr(X[:, 1, 128 * h:128 * h + 128], hn[:, h], ident[:, :])
                    last.then_inc(ht_mm, 1)

            def waits():
                pe.wait_ge(mq_in[0], 64 * 5)
                pe.wait_ge(ct_done, 9)
                pe.wait_ge(hn_done, 9)
                pe.wait_ge(my_done, 10)

            ml_front(8, [mqkv[:, 0, n] for n in range(3)], mrow[:, 0], gs, mask_s, waits)

            pe.wait_ge(gl_in, 48)
            for f in range(4):
                for j in range(3):
                    pe.wait_ge(sg_done, 3 * f + j + 1)
                    for k in range(4):
                        last = mm(G[:, j, 0:GC], wg[:, k, 128 * f:128 * f + 128], gl[:, k, GC * j:GC * j + GC],
                                  start=(k == 0), stop=(k == 3))
                    last.then_inc(gl_mm, 1)

            pe.wait_ge(q2_done, 9)
            pe.wait_ge(wt_done, 9)
            pe.wait_ge(vn_done, 9)
            pe.wait_ge(wk_done, 9)
            for h in range(4):
                pe.wait_ge(c_in[h % 2], 16 * (h // 2) + 16)
                if h:
                    pe.wait_ge(cu_done, h)
                for hf in range(2):
                    for b in range(4):
                        last = tr(X[:, hf, 128 * b:128 * b + 128], cnat[:, h % 2, 4 * hf + b], ident[:, :])
                    last.then_inc(ctt_mm, 1)
                pe.wait_ge(ctt_ev, 3 * h + 3)
                pe.wait_ge(qm_done, h + 1)
                o = X[:, 2 + h // 2, 129 * (h % 2):129 * (h % 2) + 129]
                for b in range(NSTR):
                    mm(o, qm[:, h % 2, 128 * b:128 * b + 128], ct8[:, h % 2, b], start=(b == 0), stop=False)
                mm(o, t_WT[:, h], t_vn1[:, h], start=False, stop=True).then_inc(tp_done, 1)
                pe.wait_ge(wkm_done, h + 1)
                for hf in range(2):
                    last = mm(X[:, hf], t_vn1[:, h, 0:128],
                              wkm[:, h % 2, 4 * hf:4 * hf + 4].rearrange("p b k -> p (b k)"), start=True, stop=True)
                last.then_inc(cu_mm, 1)
                if h:
                    pe.wait_ge(n_done, h)
                for b in range(NSTR):
                    last = mm(X[:, 4, b:b + 1], wkm[:, h % 2, b], onec[:, :], start=True, stop=True)
                last.then_inc(cn_mm, 1)
            pe.wait_ge(hn_done, 10)
            pe.wait_ge(cu_done, 4)
            for h in range(4):
                last = tr(X[:, 1, 128 * h:128 * h + 128], t_hn[:, h], ident[:, :])
            last.then_inc(ht_mm, 1)
            pe.wait_ge(my_done, 11)
            pe.wait_ge(sg_done, 15)

            with pe.Fori(0, 3) as t:
                for c in range(4):
                    for kh in range(2):
                        pe.wait_ge(olo_done, 32 * t + 8 * c + 4 * kh + 8)
                        if c == 0:
                            pe.wait_ge(ylo_done, 4 * t + 2 * kh + 6)
                        for a in range(3):
                            o = outbank(c, a)
                            if kh == 0:
                                pe.wait_ge(xa_done, 12 * t + 3 * c + a + 1)
                            for k in range(8):
                                kk = 8 * kh + k
                                ysl = slice(128 * a, 128 * a + 128)
                                mm(o, yhi[:, kk, ysl], ohi[:, kh, k], start=(kk == 0), stop=False)
                                mm(o, ylo[:, kk, ysl], ohi[:, kh, k], start=False, stop=False)
                                last = mm(o, yhi[:, kk, ysl], olo[:, kh, k], start=False, stop=(kk == 15))
                            if kh == 1:
                                last.then_inc(ob_mm, 1)
                        if kh == 0:
                            last.then_inc(ou_mm, 1)

        @block.scalar
        def _(act):
            fn = nc.scalar.activation

            def evac(T, kh, j, func, scale=1.0):
                if kh == 1:
                    act.wait_ge(bank_full, 3 * T + j + 4)
                    act.wait_ge(u_stored[j], 16 * T + 16)
                    fn(ev[:, j], G[:, j, 0:GC], func, scale=scale).then_inc(evac_done, 1)

            def evacs(base, step, steps, funcs):
                for t, kh, j in gemm_segs(step, steps, len(funcs)):
                    evac(base + t, kh, j, *funcs[t])

            COPY, SILU, SIGM = (ACT.Copy,), (ACT.Silu,), (ACT.Sigmoid,)

            def rms(t, s, n):
                act.wait_ge(x_in[s], n)
                fn(hlo[:, :, ds(t * 128, 128)], xin[:, s].rearrange("p (k n) -> p k n", k=KT), ACT.Square,
                   accum_out=stat[:, 0, ds(t, 1)]).then_inc(sq_done, 1)
                act.wait_ge(ms_done, t + 1)
                fn(stat[:, 2, ds(t, 1)], stat[:, 1, ds(t, 1)], ACT.Sqrt).then_inc(rms_done, 1)

            def high(t):
                for qd in range(4):
                    act.wait_ge(xt_mm, 4 * t + qd + 17)
                    fn(hhi[:, 4 * qd:4 * qd + 4, ds(t * 128, 128)], X[:, qd].rearrange("p (k n) -> p k n", k=4),
                       ACT.Copy).then_inc(hhi_done, 1)

            rms(0, 0, 16)
            with act.Fori(0, 2) as i:
                for s in range(4):
                    rms(4 * i + s + 1, (s + 1) % 4, 16 * i + 16 + 16 * ((s + 1) // 4))
                    high(4 * i + s)
            high(8)
            for kh in range(2):
                for j in range(3):
                    evac(0, kh, j, ACT.Copy)
            def evac_tile(T, func):
                for kh in range(2):
                    for j in range(3):
                        evac(T, kh, j, func)

            evac_tile(1, ACT.Copy)
            act.wait_ge(gt_dve, 4)
            fn(gB[:, :], gA[:, :], ACT.Exp, scale=-1.0).then_inc(gt_act, 1)
            act.wait_ge(gt_act, 1)
            fn(gB[:, :], gB[:, :], ACT.Ln, bias=1.0).then_inc(gt_act, 1)
            evac_tile(2, ACT.Copy)
            act.wait_ge(gt_dve, GATE_ARGS)
            fn(gR[0:4, :], gF[:, :], ACT.Exp).then_inc(gt_act, 1)
            fn(gR[32:36, :], gM[:, :], ACT.Exp, scale=-1.0).then_inc(gt_act, 1)
            fn(gR[64:68, :], gK[:, :], ACT.Exp).then_inc(gt_act, 1)
            fn(gsm[:, 5, :], gsm[:, 4, :], ACT.Exp).then_inc(gt_act, 1)
            act.wait_ge(s5_in, 16)
            fn(sm[:, 0], par[:, 2], ACT.Exp).then_inc(s5a, 1)
            evac_tile(3, ACT.Copy)
            act.wait_ge(s5v, 1)
            fn(sm[:, 3], sm[:, 1], ACT.Exp).then_inc(s5a, 1)
            fn(s5k[:, 0], sm[:, 1], ACT.Exp, scale=float(LC)).then_inc(s5a, 1)
            evac_tile(4, ACT.Silu)
            act.wait_ge(s5v, 2)
            fn(sm[:, 8], sm[:, 5], ACT.Sin).then_inc(s5a, 1)
            fn(sm[:, 9], sm[:, 6], ACT.Sin).then_inc(s5a, 1)
            fn(sm[:, 10], sm[:, 7], ACT.Sin).then_inc(s5a, 1)
            fn(sm[:, 11], sm[:, 2], ACT.Sin).then_inc(s5a, 1)
            with act.Fori(1, 4) as i:
                evacs(1 + 4 * i, 0, 1, [COPY, COPY, COPY, SILU])

            with act.Fori(0, 4) as i:
                act.wait_ge(tp_mm, 17 * i + 2)
                fn(avn[:, :, :].rearrange("p a n -> p (a n)"), T2, ACT.Copy).then_inc(tp_evac, 1)

                def exps(u):
                    n = 128 * min(u % 8 + 1, 5)
                    act.wait_ge(s_max, 16 * i + u + 1)
                    fn(aS[:, u % 2, 0:n], aS[:, u % 2, 0:n], ACT.Exp, bias=ast[:, u % 2, 0:1],
                       accum_out=ast[:, u % 2, 1:2]).then_inc(e_done, 1)

                exps(0)
                for u in range(16):
                    n = 128 * min(u % 8 + 1, 5)
                    act.wait_ge(tp_mm, 17 * i + u + 3)
                    fn(aPT[:, u % 2, 0:n], T2[:, 0:n], ACT.Copy).then_inc(tp_evac, 1)
                    if u < 15:
                        exps(u + 1)
                    evacs(17 + 4 * i, u, 16, [COPY, (ACT.Copy, 128 ** -0.5), COPY, COPY])

            with act.Fori(0, 4) as i:
                for s in range(2):
                    b = 2 * i + s
                    for t in (0, 2):
                        act.wait_ge(kt_mm, 4 * b + t + 5)
                        fn(sKT[:, :, 128 * t:128 * t + 128], X[:, t].rearrange("p (h n) -> p h n", h=4),
                           ACT.Copy).then_inc(kt_ev, 1)
                    act.wait_ge(vt_mm, b + 1)
                    fn(vnew[:, :], X[0:DT, 4], ACT.Copy).then_inc(vt_ev, 1)
                    act.wait_ge(ss_max, b + 1)
                    fn(sS[:, :], sS[:, :], ACT.Exp, bias=sst[:, 0:1], accum_out=sst[:, 1:2]).then_inc(ss_e, 1)
                    act.wait_ge(pt_mm, b + 1)
                    fn(sPT[:, :], X[:, 2], ACT.Copy).then_inc(pt_ev, 1)
                    fn(sPN[:, :], X[0:DT, 3, 0:128], ACT.Copy).then_inc(pt_ev, 1)
                    evacs(33 + 2 * i, s, 2, [SIGM, SILU])

            with act.Fori(0, 4) as f:
                act.wait_ge(su_in, 16 * f + 16)
                act.wait_ge(t1_done, 3 * f + 3)
                fn(suP[:, :, 0:NCS], T1[:, NP:NT].rearrange("p (n i) -> p i n", i=LC), ACT.Copy).then_inc(su_done, 1)
                fn(suP[:, :, NCS:NC], T1[:, 0:NP].rearrange("p (n i) -> p i n", i=LC), ACT.Copy).then_inc(su_done, 1)
                evacs(41 + 3 * f, 0, S5_CUTS, [COPY, COPY, SILU])
                act.wait_ge(s5c, S5_PREP + f * S5_STEPS + S5_TABLES)
                for e in (0, 2):
                    act.wait_ge(vt5_mm, 4 * f + e + 1)
                    fn(VT[:, e // 2, 4 * (e % 2):4 * (e % 2) + 4].rearrange("p a n -> p (a n)"), X[:, e],
                       ACT.Copy).then_inc(vt5_ev, 1)
                evacs(41 + 3 * f, 1, S5_CUTS, [COPY, COPY, SILU])
                evacs(41 + 3 * f, 2, S5_CUTS, [COPY, COPY, SILU])
                evacs(41 + 3 * f, 3, S5_CUTS, [COPY, COPY, SILU])
                for bk in range(3):
                    act.wait_ge(t1_done, 3 * f + bk + 4)
                    fs = slice(432 * bk, min(432 * bk + 432, NT))
                    fn(T1[:, fs], T1[:, fs], ACT.Gelu_apprx_tanh).then_inc(g5_done, 1)
                evacs(41 + 3 * f, 4, S5_CUTS, [COPY, COPY, SILU])

            with act.Fori(0, 4) as i:
                for s in range(2):
                    c = 2 * i + s
                    evacs(53 + 2 * i, 3 * s, 6, [COPY, SILU])
                    act.wait_ge(vn_mm, c + 1)
                    fn(vn1[:, :, 0:128], X[:, 3].rearrange("p (h n) -> p h n", h=4), ACT.Copy).then_inc(vn_done, 1)
                    act.wait_ge(d_mm, c + 1)
                    fn(EM[:, :, :].rearrange("p h n -> p (h n)"), X[:, 1], ACT.Exp).then_inc(em_done, 1)
                    for u in (1, 2):
                        evacs(53 + 2 * i, 3 * s + u, 6, [COPY, SILU])

            act.wait_ge(vn_mm, 9)
            act.wait_ge(zero_done, 7)
            fn(t_vn1[:, :, 0:128], X[:, 3].rearrange("p (h n) -> p h n", h=4), ACT.Copy).then_inc(vn_done, 1)
            act.wait_ge(d_mm, 9)
            fn(t_EM[:, :, :].rearrange("p h n -> p (h n)"), X[:, 1], ACT.Exp).then_inc(em_done, 1)
            for f in range(4):
                for j in range(3):
                    act.wait_ge(gl_mm, 3 * f + j + 1)
                    if f:
                        act.wait_ge(gy_done, f)
                    fn(gsg[:, GC * j:GC * j + GC], G[:, j, 0:GC], ACT.Sigmoid, bias=bg[:, f:f + 1]).then_inc(sg_done, 1)
            for h in range(4):
                if h >= 2:
                    act.wait_ge(tp_done, h - 1)
                for hf in range(2):
                    act.wait_ge(ctt_mm, 2 * h + hf + 1)
                    fn(ct8[:, h % 2, 4 * hf:4 * hf + 4, 0:128], X[:, hf].rearrange("p (b n) -> p b n", b=4),
                       ACT.Copy).then_inc(ctt_ev, 1)

            def high_y(t, kh):
                for p in (2 * kh, 2 * kh + 1):
                    act.wait_ge(y_in[p], 16 * t + 16)
                    if p < 2:
                        act.wait_ge(ou_mm, 4 * t + 1)
                    else:
                        act.wait_ge(ob_mm, 12 * t + 1)
                    fn(yhi[:, 4 * p:4 * p + 4], yr[:, yslot(p)], ACT.Copy).then_inc(yhi_done, 1)

            def high_w(t, c, kh):
                for p in range(4 * kh, 4 * kh + 4):
                    act.wait_ge(ow_in[p % 4], 16 * (8 * t + 2 * c + kh) + 16)
                    if kh == 0:
                        act.wait_ge(ou_mm, 4 * t + c + 1)
                    else:
                        act.wait_ge(ob_mm, 12 * t + 3 * c + 1)
                    fn(ohi[:, kh, 2 * (p % 4):2 * (p % 4) + 2], orw[:, p % 4], ACT.Copy).then_inc(ohi_done, 1)

            def high(t, c):
                for kh in range(2):
                    if c == 0:
                        high_y(t, kh)
                    high_w(t, c, kh)

            high_w(0, 0, 0)
            act.wait_ge(my_done, 11)
            high_y(0, 0)
            high_w(0, 0, 1)
            high_y(0, 1)
            for t in range(3):
                for c in range(4):
                    if c < 3:
                        high(t, c + 1)
                    elif t < 2:
                        high(t + 1, 0)
                    for a in range(3):
                        act.wait_ge(xa_done, 12 * t + 3 * c + a + 7)
                        if (t, c, a) != (0, 0, 0):
                            act.wait_ge(oq_done, 12 * t + 3 * c + a)
                        fn(X[:, 4], xo[:, a, 512 * c:512 * c + 512], ACT.Square,
                           accum_out=fst[:, a, c:c + 1]).then_inc(oq_done, 1)
                act.wait_ge(ms_done, TT + 2 * t + 2)
                fn(fst[:, :, 6], fst[:, :, 5], ACT.Sqrt).then_inc(rms_done, 1)

        @block.vector
        def _(dve):
            v = nc.vector
            tt, stt, tsc, cp = v.tensor_tensor, v.scalar_tensor_tensor, v.tensor_scalar, v.tensor_copy
            MUL, ADD, SUB, MAX, MIN = ALU.mult, ALU.add, ALU.subtract, ALU.max, ALU.min

            dve.wait_ge(g_loaded, 16)

            def norm(t, s):
                dve.wait_ge(sq_done, t + 1)
                tsc(stat[:, 1, ds(t, 1)], stat[:, 0, ds(t, 1)], 1.0 / D, EPS, MUL, ADD).then_inc(ms_done, 1)
                dve.wait_ge(rms_done, t + 1)
                v.reciprocal(stat[:, 3, ds(t, 1)], stat[:, 2, ds(t, 1)]).then_inc(rstd_done, 1)
                dve.wait_ge(rstd_done, t + 1)
                stt(xin[:, s], xin[:, s], stat[:, 3, ds(t, 1)], gb[:, :], MUL, MUL).then_inc(xn_done, 1)

            def low(t):
                for qd in range(4):
                    dve.wait_ge(hhi_done, 4 * t + qd + 1)
                    sl = (slice(None), slice(4 * qd, 4 * qd + 4), ds(t * 128, 128))
                    tt(hlo[sl], X[:, qd].rearrange("p (k n) -> p k n", k=4), hhi[sl].bitcast(F), SUB).then_inc(h_done, 1)

            norm(0, 0)
            with dve.Fori(0, 2) as i:
                for s in range(4):
                    norm(4 * i + s + 1, (s + 1) % 4)
                    low(4 * i + s)
            low(8)

            g = Chain(dve, gt_dve)
            dve.wait_ge(evac_done, 6)
            dve.wait_ge(const_done, 14)
            g(v.memset(gR[:, :], 0.0))
            dve.wait_ge(gt_in, 64)
            g(tsc(gF[:, :], gF[:, :], gbi[:, 1:2], None, ADD))
            g(tsc(gA[:, :], gF[:, :], -1.0, None, MUL))
            g(tt(gA[:, :], gA[:, :], gF[:, :], MAX))
            assert g.count == 4
            g(tsc(gI[:, :], gI[:, :], gbi[:, 0:1], None, ADD))
            g(tsc(gF[:, :], gF[:, :], 0.0, None, MIN))
            g(v.memset(gK[:, :], 1.0))
            g(v.memset(gK[:, 0:NP:128], 0.0))
            g(v.memset(gK[:, NP:NT:DT], 0.0))
            dve.wait_ge(gt_act, 2)
            g(tt(gF[:, :], gF[:, :], gB[:, :], SUB))
            g(v.tensor_tensor_scan(gB[:, :], gK[:, :], gF[:, :], 0.0, MUL, ADD))
            g(tt(gsm[:, 3, 8:16], gF[:, NP:NT:DT], gsm[:, 0, 8:16], ADD))
            g(tt(gsm[:, 4, 8:16], gsm[:, 3, 8:16], gI[:, NP:NT:DT], MAX))
            g(tt(gA[:, :], gI[:, :], gB[:, :], SUB))
            g(cp(gI[:, NP:NT:DT], gsm[:, 4, 8:16]))
            g(v.memset(gF[:, NP:NT:DT], NEG))
            g(v.tensor_tensor_scan(gM[:, :], gF[:, :], gI[:, :], 0.0, ADD, MAX))
            g(v.memset(gsm[:, 0, 0:1], 0.0))
            g(cp(gsm[:, 0, 1:8], gM[:, 127:NP - 128:128]))
            g(cp(gsm[:, 2, 0:8], gM[:, 127:NP:128]))
            g(cp(gsm[:, 2, 8:16], gM[:, NP + DT - 1:NT:DT]))
            g(cp(gsm[:, 1, 0:8], gB[:, 127:NP:128]))
            g(cp(gsm[:, 1, 8:16], gB[:, NP + DT - 1:NT:DT]))
            g(tt(gB[:, :], gB[:, :], gM[:, :], SUB))
            assert g.count == GATE_ROWS, g.count

            def per_chunk(out, a, small):
                for sl, n, so in ((slice(0, NP), 128, slice(0, 8)), (slice(NP, NT), DT, slice(8, 16))):
                    g(tt(out[:, sl].rearrange("p (c n) -> p c n", n=n), a[:, sl].rearrange("p (c n) -> p c n", n=n),
                         small[:, so].unsqueeze(2).broadcast_to([4, 8, n]), ADD))

            per_chunk(gF, gB, gsm[:, 0])
            g(tt(gsm[:, 3], gsm[:, 1], gsm[:, 2], SUB))
            per_chunk(gK, gA, gsm[:, 3])
            g(tt(gsm[:, 4], gsm[:, 3], gsm[:, 0], ADD))
            assert g.count == GATE_ARGS, g.count
            dve.wait_ge(gt_act, GATE_R + 1)
            g(tt(dsel[:, :, :], sel[:, :, 0:16], gsm[:, 5:6, :].broadcast_to([4, 4, 16]), MUL))
            assert g.count == GATE_DSEL, g.count

            c5 = Chain(dve, s5c)
            C1, C2 = 6.28125, 0.0019350051879882812
            C3 = TWO_PI - C1 - C2

            def reduce_angle(dst, src, whole):
                c5(tsc(smi[:, :], src, 1.0 / TWO_PI, None, MUL))
                c5(cp(whole, smi[:, :]))
                c5(stt(dst, whole, -C1, src, MUL, ADD))
                c5(stt(dst, whole, -C2, dst, MUL, ADD))
                c5(stt(dst, whole, -C3, dst, MUL, ADD))
                c5(tsc(dst, dst, -PI_LO, PI_LO, MAX, MIN))

            def quarter_turn(dst, src):
                c5(tsc(dst, src, -1.0, None, MUL))
                c5(tt(dst, dst, src, MAX))
                return tsc(dst, dst, -1.0, TWO_PI / 4, MUL, ADD)

            dve.wait_ge(s5a, 1)
            c5(tt(sm[:, 2], par[:, 1], sm[:, 0], MUL))
            tt(sm[:, 1], par[:, 0], sm[:, 0], MUL).then_inc(s5v, 1)
            reduce_angle(sm[:, 5], sm[:, 2], sm[:, 12])
            c5(tsc(sm[:, 2], sm[:, 5], float(LC), None, MUL))
            reduce_angle(sm[:, 7], sm[:, 2], sm[:, 12])
            c5(quarter_turn(sm[:, 6], sm[:, 5]))
            quarter_turn(sm[:, 2], sm[:, 7]).then_inc(s5v, 1)
            dve.wait_ge(s5a, 7)
            c5(v.memset(PW[:, 0, 0], 1.0))
            c5(v.memset(PW[:, 1, 0], 0.0))
            c5(tt(PW[:, 0, 1], sm[:, 3], sm[:, 9], MUL))
            c5(tt(PW[:, 1, 1], sm[:, 3], sm[:, 8], MUL))
            c5(cp(E1[:, 0], sm[:, 11]))
            c5(tsc(E1[:, 1], sm[:, 10], -1.0, None, MUL))
            for m in (1, 2, 4):
                a, b = slice(1, m + 1), slice(m + 1, 2 * m + 1)
                top_re, top_im = (PW[:, n, m:m + 1].broadcast_to([128, m, 16]) for n in range(2))
                w = sm[:, 12:12 + m]
                c5(tt(PW[:, 0, b], PW[:, 0, a], top_re, MUL))
                c5(tt(w, PW[:, 1, a], top_im, MUL))
                c5(tt(PW[:, 0, b], PW[:, 0, b], w, SUB))
                c5(tt(PW[:, 1, b], PW[:, 0, a], top_im, MUL))
                c5(tt(w, PW[:, 1, a], top_re, MUL))
                c5(tt(PW[:, 1, b], PW[:, 1, b], w, ADD))
            c5(tt(sm[:, 12], par[:, 0], par[:, 0], MUL))
            c5(tt(sm[:, 13], par[:, 1], par[:, 1], MUL))
            c5(tt(sm[:, 12], sm[:, 12], sm[:, 13], ADD))
            c5(v.reciprocal(sm[:, 13], sm[:, 12]))
            c5(tsc(sm[:, 14], PW[:, 0, 1], -1.0, None, ADD))
            c5(tt(sm[:, 5], sm[:, 14], par[:, 0], MUL))
            c5(tt(sm[:, 12], PW[:, 1, 1], par[:, 1], MUL))
            c5(tt(sm[:, 5], sm[:, 5], sm[:, 12], ADD))
            c5(tt(s5k[:, 1], sm[:, 5], sm[:, 13], MUL))
            c5(tt(sm[:, 6], PW[:, 1, 1], par[:, 0], MUL))
            c5(tt(sm[:, 12], sm[:, 14], par[:, 1], MUL))
            c5(tt(sm[:, 6], sm[:, 6], sm[:, 12], SUB))
            c5(tt(s5k[:, 2], sm[:, 6], sm[:, 13], MUL))
            assert c5.count == S5_PREP, c5.count

            dve.wait_ge(gt_mm, 2)
            g(cp(col[:, 0:5, :].rearrange("p a n -> p (a n)"), X[:, 0, 0:480]))
            g(cp(col[:, 5:9, :].rearrange("p a n -> p (a n)"), X[:, 1, 0:384]))
            g(cp(dec[:, :, :].rearrange("p a n -> p (a n)"), X[:, 2, 0:64]))
            assert g.count == GATE_END, g.count


            with dve.Fori(0, 4) as i:
                def add_max(u):
                    n = 128 * min(u % 8 + 1, 5)
                    if u == 0:
                        dve.wait_ge(ab_in, 16 * i + 16)
                    dve.wait_ge(s_mm, 16 * i + u + 2)
                    dve.wait_ge(tp_mm, 17 * i + u + 1)
                    stt(aS[:, u % 2, 0:n], X2[:, 0:n], 0.125, abias[:, u // 8, BAND_KEYS - n:], MUL, ADD).then_inc(s_add, 1)
                    dve.wait_ge(s_add, 16 * i + u + 2)
                    v.reduce_max(ast[:, u % 2, 0:1], aS[:, u % 2, 0:n], AX, negate=True).then_inc(s_max, 1)

                add_max(0)
                for u in range(16):
                    n = 128 * min(u % 8 + 1, 5)
                    qs = slice(128 * (u % 8), 128 * (u % 8) + 128)
                    ps = slice(64 * (u // 8), 64 * (u // 8) + 64)
                    dve.wait_ge(e_done, 16 * i + u + 1)
                    v.reciprocal(ast[:, u % 2, 2:3], ast[:, u % 2, 1:2]).then_inc(r_done, 1)
                    dve.wait_ge(r_done, 16 * i + u + 1)
                    tsc(aS[:, u % 2, 0:n], aS[:, u % 2, 0:n], ast[:, u % 2, 2:3], None, MUL).then_inc(p_done, 1)
                    if u < 15:
                        add_max(u + 1)
                    if u == 0:
                        dve.wait_ge(z_in, 16 * i + 16)
                    dve.wait_ge(o_mm, 16 * i + u + 1)
                    tt(az[ps, qs], X[ps, 4, 0:128], az[ps, qs], MUL).then_inc(y_done, 1)

            dve.wait_ge(ss_in, 16 * 17)
            v.memset(qblk[:, :, :], 0.0).then_inc(zero_done, 1)
            dve.wait_ge(zero_done, 1)
            with dve.Fori(0, 4) as i:
                for s in range(2):
                    b = 2 * i + s
                    bs = ds(b * DT, DT)
                    cp(svb[:, :, :], sv[:, :, bs]).then_inc(kq_done, 1)
                    for t in (1, 3):
                        dve.wait_ge(kt_mm, 4 * b + t + 5)
                        cp(sKT[:, :, 128 * t:128 * t + 128], X[:, t].rearrange("p (h n) -> p h n", h=4)).then_inc(kt_ev, 1)
                    cp(sKT[:, :, 512:SK], sk[:, :, bs]).then_inc(kq_done, 1)
                    cp(qblk[0:64, :, 0:DT], sq[0:64, :, bs]).then_inc(kq_done, 1)
                    cp(qblk[64:128, :, DT:2 * DT], sq[64:128, :, bs]).then_inc(kq_done, 1)
                    dve.wait_ge(ss_mm, b + 1)
                    stt(sS[:, :], X2[:, 0:SK], 0.125, sbias[:, :], MUL, ADD).then_inc(ss_add, 1)
                    dve.wait_ge(ss_add, b + 1)
                    v.reduce_max(sst[:, 0:1], sS[:, :], AX, negate=True).then_inc(ss_max, 1)
                    dve.wait_ge(ss_e, b + 1)
                    v.reciprocal(sst[:, 2:3], sst[:, 1:2]).then_inc(ss_r, 1)
                    dve.wait_ge(ss_r, b + 1)
                    tsc(sS[:, :], sS[:, :], sst[:, 2:3], None, MUL).then_inc(ss_p, 1)
                    dve.wait_ge(so_mm, b + 2)
                    o = X[:, 4, 0:128].rearrange("p (h n) -> p h n", h=4)
                    tt(sz[0:64, :, bs], o[0:64, :, 0:DT], sz[0:64, :, bs], MUL)
                    tt(sz[64:128, :, bs], o[64:128, :, DT:2 * DT], sz[64:128, :, bs], MUL).then_inc(sy_done, 1)

            dve.wait_ge(s5_in, 32)
            v.memset(Kbd[:, :, :], 0.0).then_inc(zero_done, 1)
            dve.wait_ge(zero_done, 2)

            Va = VT[:, 0].rearrange("p (a b) n -> p a b n", a=2)
            Vb = VT[:, 1].rearrange("p (a b) n -> p a b n", a=2)
            T1f = T1[:, 0:1024]
            with dve.Fori(0, 4) as f:
                c5 = Chain(dve, s5c, S5_PREP + f * S5_STEPS)
                st4s = ds(4 * f, 4)
                dve.wait_ge(bc_in, 48 * f + 48)
                dve.wait_ge(g5_stored, 32 * f + 16)
                c5(tsc(BC[:, 1, 1], BC[:, 1, 1], -1.0, None, MUL))
                Bb = [VT[:, 1, n].rearrange("p (s c) -> p s c", s=4) for n in range(2)]
                w = VT[:, 1, 2].rearrange("p (s c) -> p s c", s=4)
                co_re, co_im = (s5k[:, n, st4s].unsqueeze(2).broadcast_to([128, 4, 32]) for n in (1, 2))
                c5(tt(Bb[0], BC[:, 0, 0], co_re, MUL))
                c5(tt(w, BC[:, 0, 1], co_im, MUL))
                c5(tt(Bb[0], Bb[0], w, SUB))
                c5(tt(Bb[1], BC[:, 0, 1], co_re, MUL))
                c5(tt(w, BC[:, 0, 0], co_im, MUL))
                c5(tt(Bb[1], Bb[1], w, ADD))
                ACv = [AC[:, n].rearrange("p s t c -> p t s c") for n in range(2)]
                full = [128, LC, 4, 32]
                pw = [[PW[:, n, o:o + LC, st4s].unsqueeze(3).broadcast_to(full) for n in range(2)] for o in range(2)]
                Bx = [x.unsqueeze(1).broadcast_to(full) for x in Bb]
                w = VT[:, 0].rearrange("p t (s c) -> p t s c", s=4)
                c5(tt(ACv[0], pw[0][0], Bx[0], MUL))
                c5(tt(w, pw[0][1], Bx[1], MUL))
                c5(tt(ACv[0], ACv[0], w, SUB))
                c5(tt(ACv[1], pw[0][0], Bx[1], MUL))
                c5(tt(w, pw[0][1], Bx[0], MUL))
                tt(ACv[1], ACv[1], w, ADD).then_inc(ab_done, 1)
                dve.wait_ge(ab_done, f + 1)
                c5(v.memset(E5[:, 0, :, 0:1], 1.0))
                c5(v.memset(E5[:, 1, :, 0:1], 0.0))
                c5(cp(E5[:, :, :, 1], E1[:, :, st4s]))
                m = 1
                while m < NCP:
                    a, b = slice(1, m + 1), slice(m + 1, 2 * m + 1)
                    mul = [E5[:, n:n + 1, :, m:m + 1].broadcast_to([128, 2, 4, m]) for n in range(2)]
                    w = Va[:, :, :, 0:m]
                    c5(tt(E5[:, :, :, b], E5[:, :, :, a], mul[0], MUL))
                    c5(tt(w, E5[:, :, :, a], mul[1], MUL))
                    c5(tt(E5[:, 0, :, b], E5[:, 0, :, b], w[:, 1], SUB))
                    c5(tt(E5[:, 1, :, b], E5[:, 1, :, b], w[:, 0], ADD))
                    m *= 2
                assert c5.count == S5_TABLES, c5.count
                for e in (1, 3):
                    dve.wait_ge(vt5_mm, 4 * f + e + 1)
                    cp(VT[:, e // 2, 4 * (e % 2):4 * (e % 2) + 4].rearrange("p a n -> p (a n)"), X[:, e]).then_inc(vt5_ev, 1)
                dve.wait_ge(k5_mm, f + 1)
                for st in range(4):
                    ps = slice(32 * st, 32 * st + 32)
                    last = cp(Kbd[ps, :, ps], X[ps, 4, 0:256].rearrange("p (t c) -> p t c", t=LC))
                last.then_inc(k5_ev, 1)
                Cx = [BC[:, 1, n] for n in range(2)]

                def add_product(out, m, op):
                    for t in range(0, LC, 2):
                        im = PW[:, 1, 1 + t:3 + t, st4s].unsqueeze(3).broadcast_to([128, 2, 4, 32])
                        c5(tt(wq[:, :, :, :], im, Cx[m].unsqueeze(1).broadcast_to([128, 2, 4, 32]), MUL))
                        last = tt(out[:, t:t + 2], out[:, t:t + 2], wq[:, :, :, :], op)
                        if t < LC - 2:
                            c5(last)
                    return last

                c5(tt(ACv[0], pw[1][0], Cx[0].unsqueeze(1).broadcast_to(full), MUL))
                c5(tt(ACv[1], pw[1][0], Cx[1].unsqueeze(1).broadcast_to(full), MUL))
                c5(add_product(ACv[0], 1, ADD))
                add_product(ACv[1], 0, SUB).then_inc(ca_done, 1)
                dve.wait_ge(ca_done, f + 2)
                dve.wait_ge(x5_mm, 4 * f + 4)
                c5(v.memset(XS[:, :, :, NCS:NCS + 1], 0.0))
                Xp = X[:, 0:4, 0:2 * NC].rearrange("p s (r n) -> p r s n", r=2)
                Ex = [E5[:, n:n + 1, :, 0:NCP].broadcast_to([128, 2, 4, NCP]) for n in range(2)]
                c5(tt(Va, Xp[:, :, :, NCS:NC], Ex[0], MUL))
                c5(tt(Vb, Xp[:, :, :, NCS:NC], Ex[1], MUL))
                c5(tt(Va[:, 0], Va[:, 0], Vb[:, 1], SUB))
                c5(tt(Va[:, 1], Va[:, 1], Vb[:, 0], ADD))
                for n in range(2):
                    for st in range(4):
                        r8 = s5k[:, 0, ds(4 * f + st, 1)]
                        c5(v.tensor_tensor_scan(Vb[:, n, st], r8.broadcast_to([128, NCP]), Va[:, n, st], 0.0, MUL, ADD))
                w = T1f.rearrange("p (r s n) -> p r s n", r=2, s=4)
                c5(tt(Va, Vb, Ex[0], MUL))
                c5(tt(w, Vb, Ex[1], MUL))
                c5(tt(XS[:, 0, :, NCS + 1:], Va[:, 0], w[:, 1], ADD))
                c5(tt(XS[:, 1, :, NCS + 1:], Va[:, 1], w[:, 0], SUB))
                A8 = [PW[:, n:n + 1, LC, st4s].unsqueeze(3).broadcast_to([128, 2, 4, 8]) for n in range(2)]
                c5(cp(XS[:, :, :, 0:NCS:2], s0[:, :, :, :]))
                for step in range(2):
                    src = XS[:, :, :, step:NCS:2]
                    c5(tt(SX[:, 0], src, A8[0], MUL))
                    c5(tt(SX[:, 1], src, A8[1], MUL))
                    c5(tt(SX[:, 0, 0], SX[:, 0, 0], SX[:, 1, 1], SUB))
                    c5(tt(SX[:, 0, 1], SX[:, 0, 1], SX[:, 1, 0], ADD))
                    dst = XS[:, :, :, 1:NCS:2] if step == 0 else FO[:, :, :, 0:8]
                    c5(tt(dst, SX[:, 0], Xp[:, :, :, step:NCS:2], ADD))
                cp(FO[:, :, :, 8], XS[:, :, :, NC]).then_inc(xs_done, 1)
                for bk in range(3):
                    i0, i1 = 3 * bk, min(3 * bk + 3, LC)
                    dve.wait_ge(y5_mm, 3 * f + bk + 1)
                    stt(T1[:, NC * i0:NC * i1], suP[:, i0:i1].rearrange("p a n -> p (a n)"), dD[:, ds(f, 1)],
                        X[:, bk, 0:NC * (i1 - i0)], MUL, ADD).then_inc(t1_done, 1)
                assert c5.count == S5_STEPS, c5.count

            for z in (v.memset(CT[:, :, :], 0.0), v.memset(vn1[:, :, 128:129], 1.0)):
                z.then_inc(zero_done, 1)
            dve.wait_ge(zero_done, 4)

            def ml_gates(c, row, g2):
                tt(g2[:, :, :, :], sel[:, :, :].unsqueeze(1).broadcast_to([4, 2, 4, 128]),
                   row[:, 0:2].unsqueeze(2).broadcast_to([4, 2, 4, 128]), MUL).then_inc(gs_done, 1)

            def ml_mid(c, q, k_scaled, q_out, wt_out, em):
                dve.wait_ge(wb_mm, c + 1)
                tt(q_out, q, X[:, 2].rearrange("p (h n) -> p h n", h=4), MUL).then_inc(q2_done, 1)
                dve.wait_ge(kn_mm, c + 1)
                kx = X[:, 4].rearrange("p (h n) -> p h n", h=4)
                k_scaled(kx).then_inc(wk_done, 1)
                dve.wait_ge(em_done, c + 1)
                dve.wait_ge(st_mm, c + 1)
                tt(wt_out, em, X[:, 0].rearrange("p (h n) -> p h n", h=4), MUL).then_inc(wt_done, 1)

            def ml_norm(c, d2, h_out):
                P = X[:, 2:4, 0:258].rearrange("p a (h n) -> p a h n", h=2)
                den = d2[:, 0].rearrange("p (a h) -> p a h", a=2)
                inv = d2[:, 1].rearrange("p (a h) -> p a h", a=2)
                floor = col[:, ds(c, 1), 32:36].rearrange("p o (a h) -> p (o a) h", a=2)
                k = Chain(dve, den_c, 4 * c)
                k(tsc(den, P[:, :, :, 128], -1.0, None, MUL))
                k(tt(den, P[:, :, :, 128], den, MAX))
                k(tt(den, den, floor, MAX))
                k(v.reciprocal(inv, den))
                tt(h_out.rearrange("p (a h) n -> p a h n", a=2), P[:, :, :, 0:128],
                   inv.unsqueeze(3).broadcast_to([128, 2, 2, 128]), MUL).then_inc(hn_done, 1)

            with dve.Fori(0, 4) as i:
                for s in range(2):
                    c = 2 * i + s
                    dve.wait_ge(mq_in[s], 64 * i + 64)
                    ml_gates(c, mrow[:, s], gs)
                    dve.wait_ge(mo_in, 32 * c + 32)
                    tt(moz[:, 0], moz[:, 0], moz[:, 1], MUL).then_inc(oz_done, 1)
                    ml_mid(c, mqkv[:, s, 0],
                           lambda kx: tt(wsk[:, :, :], kx, col[:, ds(c, 1), 64:68].rearrange("p o h -> p (o h)").unsqueeze(2).broadcast_to([128, 4, 128]), MUL),
                           q2[:, :, :], WT[:, :, :], EM[:, :, :])
                    dve.wait_ge(u_mm, c + 1)
                    for h in range(4):
                        last = stt(CT[:, h], CT[:, h], dec[:, h, ds(c, 1)],
                                   X[:, 4 * (h // 2), 129 * (h % 2):129 * (h % 2) + 129], MUL, ADD)
                    last.then_inc(ct_done, 1)
                    ml_norm(c, md, hn[:, :, :])
                    dve.wait_ge(ht_mm, c + 1)
                    dve.wait_ge(oz_done, c + 1)
                    dve.wait_ge(my_stored, 16 * c + 16)
                    tt(yb[:, :, :], X[:, 1].rearrange("p (h n) -> p h n", h=4), moz[:, 0], MUL).then_inc(my_done, 1)

            dve.wait_ge(mq_in[0], 64 * 5)
            ml_gates(8, mrow[:, 0], gs)
            dve.wait_ge(bank_full, 3 * NTILES + 3)
            dve.wait_ge(w_split, 2 * NTILES + 2)
            k = Chain(dve, zero_done, 4)
            k(v.memset(t_vn1[:, :, 128:129], 1.0))
            k(v.memset(qm[:, :, :], 0.0))
            k(tt(wsm[:, :, :], col[:, 8, 64:68].unsqueeze(2).broadcast_to([128, 4, NSTR]),
                 bmask[:, :].unsqueeze(1).broadcast_to([128, 4, NSTR]), MUL))
            dve.wait_ge(tq_in, 16 * 3)
            tt(t_oz[:, 0], t_oz[:, 0], t_oz[:, 1], MUL).then_inc(oz_done, 1)

            dve.wait_ge(cp_in, 16)
            dve.wait_ge(gl_in, 48)
            own = Chain(dve, zero_done, 7)

            def glu(f):
                dve.wait_ge(sg_done, 3 * f + 6)
                tt(gsg[:, :], gsg[:, :], gl[:, f], MUL).then_inc(gm_done, 1)
                dve.wait_ge(gm_done, f + 1)
                dve.wait_ge(gz_in, 16 * f + 16)
                st_major = gsg[:, :].rearrange("p (i n) -> p n i", i=LC)
                p_ = gsz[:, 0:NP].rearrange("p (n i) -> p n i", i=LC)
                s_ = gsz[:, NP:NT].rearrange("p (n i) -> p n i", i=LC)
                tt(p_, p_, st_major[:, NCS:NC], MUL)
                tt(s_, s_, st_major[:, 0:NCS], MUL).then_inc(gy_done, 1)

            ml_mid(8, mqkv[:, 0, 0], lambda kx: cp(t_wsk[:, :, :], kx), t_q2[:, :, :], t_WT[:, :, :], t_EM[:, :, :])
            glu(0)
            conv_in(dve, v, own, 0)
            glu(1)
            conv_taps(v, own, 0)
            glu(2)

            def spread_head(h):
                s = h % 2
                if h >= 2:
                    dve.wait_ge(cn_mm, h - 1)
                    dve.wait_ge(tp_done, h - 1)
                cp(ct8[:, s, :, 128], nin[:, h]).then_inc(ctt_ev, 1)
                cp(qm[:, s].rearrange("p (b n) -> p b n", b=NSTR)[:, :, 0:DT],
                   t_q2[:, h].rearrange("p (b n) -> p b n", b=NSTR)).then_inc(qm_done, 1)
                tt(wkm[:, s], t_wsk[:, h:h + 1].broadcast_to([128, NSTR, 128]),
                   wsm[:, h].unsqueeze(2).broadcast_to([128, NSTR, 128]), MUL).then_inc(wkm_done, 1)

            dve.wait_ge(q2_done, 9)
            dve.wait_ge(wk_done, 9)
            spread_head(0)
            glu(3)
            for h in range(4):
                s = h % 2
                if h:
                    spread_head(h)
                dve.wait_ge(ctt_mm, 2 * h + 2)
                tt(cnat[:, s], cnat[:, s], dec[:, h, 8:16].unsqueeze(2).broadcast_to([128, NSTR, 128]), MUL).then_inc(cdec, 1)
                tt(nout[:, h], nin[:, h], dec[:, h, 8:16], MUL).then_inc(cdec, 1)
                dve.wait_ge(cdec, 2 * h + 2)
                dve.wait_ge(cu_mm, h + 1)
                for hf in range(2):
                    cs = cnat[:, s, 4 * hf:4 * hf + 4].rearrange("p b k -> p (b k)")
                    last = tt(cs, cs, X[:, hf], ADD)
                last.then_inc(cu_done, 1)
                dve.wait_ge(cn_mm, h + 1)
                tt(nout[:, h], nout[:, h], X[:, 4, 0:NSTR], ADD).then_inc(n_done, 1)
                if h == 0:
                    conv_out(v, own, 0)
                if h == 3:
                    conv_in(dve, v, own, 2)
            dve.wait_ge(tp_done, 4)
            ml_norm(8, t_md, t_hn[:, :, :])
            dve.wait_ge(ht_mm, 9)
            dve.wait_ge(oz_done, 9)
            tt(t_hn[:, :, :], X[:, 1].rearrange("p (h n) -> p h n", h=4), t_oz[:, 0], MUL).then_inc(my_done, 1)

            def low_y(t, kh):
                for p in (2 * kh, 2 * kh + 1):
                    dve.wait_ge(yhi_done, 4 * t + p + 1)
                    tt(ylo[:, 4 * p:4 * p + 4], yr[:, yslot(p)], yhi[:, 4 * p:4 * p + 4].bitcast(F), SUB).then_inc(ylo_done, 1)

            def low_w(t, c, kh):
                for p in range(4 * kh, 4 * kh + 4):
                    dve.wait_ge(ohi_done, 32 * t + 8 * c + p + 1)
                    sl = (slice(None), kh, slice(2 * (p % 4), 2 * (p % 4) + 2))
                    tt(olo[sl], orw[:, p % 4], ohi[sl].bitcast(F), SUB).then_inc(olo_done, 1)

            def low(t, c):
                for kh in range(2):
                    if c == 0:
                        low_y(t, kh)
                    low_w(t, c, kh)

            low_w(0, 0, 0)
            low_y(0, 0)
            conv_taps(v, own, 2)
            conv_out(v, own, 2)
            low_w(0, 0, 1)
            low_y(0, 1)
            dve.wait_ge(g_loaded, 32)
            for t in range(3):
                for c in range(4):
                    if c < 3:
                        low(t, c + 1)
                    elif t < 2:
                        low(t + 1, 0)
                    dve.wait_ge(xo_in, 16 * t + 16)
                    for a in range(3):
                        dve.wait_ge(ob_mm, 12 * t + 3 * c + a + 2)
                        cs = slice(512 * c, 512 * c + 512)
                        tt(xo[:, a, cs], outbank(c, a), xo[:, a, cs], ADD).then_inc(xa_done, 1)
                dve.wait_ge(oq_done, 12 * t + 12)
                v.reduce_sum(fst[:, :, 4], fst[:, :, 0:4], AX).then_inc(ms_done, 1)
                dve.wait_ge(ms_done, TT + 2 * t + 1)
                tsc(fst[:, :, 5], fst[:, :, 4], 1.0 / D, EPS, MUL, ADD).then_inc(ms_done, 1)
                dve.wait_ge(rms_done, TT + t + 1)
                v.reciprocal(fst[:, :, 7], fst[:, :, 6]).then_inc(rstd_done, 1)
                dve.wait_ge(rstd_done, TT + t + 1)
                dve.wait_ge(f_stored, 48 * t + 16)
                for a in range(3):
                    stt(fo[:, a], xo[:, a], fst[:, a, 7:8], go[:, :], MUL, MUL).then_inc(f_done, 1)

GATE_ROWS, GATE_ARGS, GATE_DSEL, GATE_END = 24, 30, 31, 34
GATE_WINT, GATE_R = 3, 5
S5_CUTS = (0, 5, 7, 10, 14, 18)
S5_PREP, S5_TABLES, S5_STEPS = 56, 43, 88

_OUTS = [("y_all", (NT, D)), ("kv_new", (4, 2, 128, 640)), ("k_shift", (NSTR, 512 - DT, 512)),
         ("v_shift", (NSTR, 512 - DT, 512)), ("c_prompt", (4, 128, 128)), ("n_prompt", (128, 4)),
         ("m_last", (4, 16)), ("c_stream", (4, 128, NSTR, 128)), ("n_stream", (128, 4, NSTR)),
         ("conv_p", (4, 128, 2)), ("conv_s", (4, 128, NSTR, 2)), ("s5_last", (128, 2, 16, 9))]

def kernel(**inputs):
    import numpy as np
    import concourse.bacc as bacc
    from concourse.bass_utils import run_bass_kernel_spmd

    a = {k: np.asarray(v) for k, v in inputs.items()}
    x_all = np.concatenate([a["x_prompt"][0], a["x_sample"].reshape(NS, D)], axis=0)
    w = a["w_in"][0].reshape(KT, 128, -1)
    start = {"aq": 0, "ak": 512, "av": 1024, "az": 1536, "mq": 2048, "mk": 2560, "mv": 3072, "mo": 3584, "mz": 4096,
             "cb": 4616, "cc": 5128, "cx": 5640, "cz": 6152, "su": 6664, "sz": 7176}
    w_in_t = np.zeros((NTILES, 128, KT, 128), np.float32)
    w_in_t[T_GATE, :, :, 0:4] = w[:, :, 4608:4612].transpose(1, 0, 2)
    w_in_t[T_GATE, :, :, 32:36] = w[:, :, 4612:4616].transpose(1, 0, 2)
    for names, tile in ((("aq", "ak", "av", "az"), T_ATT), (("mq", "mk", "mv", "su"), T_ML), (("mo", "mz"), T_MG),
                        (("cb", "cc", "sz"), T_S5), (("cx", "cz"), T_CV)):
        for kind, n in enumerate(names):
            for i in range(4):
                c0 = start[n] + 128 * i
                w_in_t[tile(i, kind)] = w[:, :, c0:c0 + 128].transpose(1, 0, 2)
    w_out_t = a["w_out"][0].reshape(KT, 128, 4, 512).transpose(2, 1, 0, 3)
    rb = a["attn_rel_bias"][0]
    q, j = np.arange(128)[:, None], np.arange(BAND_KEYS)[None, :]
    idx = np.clip(q + 512 - j, -128, 128) + 128
    hidden = ((q < 64) & (j >= 576)) | ((q >= 64) & (j < 64))
    bias_p = np.where(hidden[None], np.float32(NEG), rb[:, idx]).astype(np.float32)
    q, j = np.arange(DT)[:, None], np.arange(SK)[None, :]
    bias_s = rb[:, np.clip(q + 512 - j, -128, 128) + 128].reshape(128, SK)

    def states(x):
        return x.reshape((16, 2, 64) + x.shape[2:]).transpose((1, 2, 0) + tuple(range(3, x.ndim + 1))).reshape((128, 16) + x.shape[2:])

    def spread(x):
        x = x.reshape(16, 2, 64, 16)
        out = np.zeros((2, 64, 16, 32), np.float32)
        out[0, :, :, 0:16] = x[:, 0].transpose(1, 0, 2)
        out[1, :, :, 16:32] = x[:, 1].transpose(1, 0, 2)
        return out.reshape(128, 16, 32)

    arrays = {
        "x_all": x_all, "w_in_t": w_in_t, "w_out_t": w_out_t,
        "g_in": np.broadcast_to(a["norm_g"][0], (128, D)), "g_out": np.broadcast_to(a["final_norm_g"], (128, D)),
        "bias_p": bias_p, "bias_s": bias_s,
        "b_if": a["mlstm_b_if"][0].reshape(2, 4).T, "m_init": a["state_mlstm_m"][0].T,
        "k_cache": a["cache_attn_k"][0].reshape(NSTR, 512, 512), "v_cache": a["cache_attn_v"][0].reshape(NSTR, 512, 512),
        "c_init": a["state_mlstm_C"][0].transpose(1, 2, 0, 3), "n_init": a["state_mlstm_n"][0].transpose(2, 1, 0),
        "conv_w": a["conv_w"][0].reshape(3, 4, 128).transpose(2, 0, 1),
        "conv_buf": a["state_conv"][0].reshape(NSTR, 2, 4, 128).transpose(2, 3, 0, 1),
        "s5_par": np.stack([states(a["s5_A_re"][0]), states(a["s5_A_im"][0]),
                            states(np.broadcast_to(a["s5_log_dt"][0][:, None], (32, 64)))], axis=1),
        "s5_b": np.stack([spread(a["s5_B_re"][0]), spread(a["s5_B_im"][0])], axis=1),
        "s5_c": np.stack([spread(a["s5_C_re"][0].transpose(0, 2, 1)), spread(a["s5_C_im"][0].transpose(0, 2, 1))], axis=1),
        "s5_s0": np.stack([states(a["state_s5_re"][0].transpose(1, 2, 0)), states(a["state_s5_im"][0].transpose(1, 2, 0))], axis=1),
        "s5_d": a["s5_D"][0].reshape(4, 128).T,
        "w_glu": a["s5_w_glu"][0].reshape(4, 128, 512).transpose(1, 0, 2), "b_glu": a["s5_b_glu"][0].reshape(4, 128).T,
    }
    nc = bacc.Bacc("TRN2", target_bir_lowering=False, num_devices=1, dynamic_dma_scratch_size=256)
    arrays = {k: np.ascontiguousarray(v) for k, v in arrays.items()}
    args = [nc.dram_tensor(k, v.shape, mybir.dt.from_np(v.dtype), kind="ExternalInput").ap() for k, v in arrays.items()]
    args += [nc.dram_tensor(k, s, mybir.dt.float32, kind="ExternalOutput").ap() for k, s in _OUTS]
    encoder_program(nc, *args)
    r = run_bass_kernel_spmd(nc, [arrays], core_ids=[0]).results[0]

    y, kv, m, s5 = r["y_all"], r["kv_new"], r["m_last"], r["s5_last"]
    kv = kv.transpose(1, 3, 0, 2).reshape(2, 640, 8, 64)
    caches = [np.concatenate([r[n].reshape(NSTR, 512 - DT, 8, 64), kv[i, 512:].reshape(NSTR, DT, 8, 64)], axis=1)[None]
              for i, n in enumerate(("k_shift", "v_shift"))]
    s5 = s5.reshape(2, 64, 2, 16, 9).transpose(2, 4, 3, 0, 1).reshape(2, 9, 32, 64)
    return (y[None, :NP], y[NP:].reshape(NSTR, DT, D),
            kv[0, :512][None, None], kv[1, :512][None, None],
            r["c_prompt"].transpose(0, 2, 1)[None, None], r["n_prompt"].T[None, None], m[:, 7][None, None],
            r["conv_p"].transpose(2, 0, 1).reshape(2, 512)[None, None],
            s5[0, 8][None, None], s5[1, 8][None, None],
            caches[0], caches[1],
            r["c_stream"].transpose(2, 0, 1, 3)[None], r["n_stream"].transpose(2, 1, 0)[None], m[:, 8:16].T[None],
            r["conv_s"].transpose(2, 3, 0, 1).reshape(NSTR, 2, 512)[None],
            s5[0, 0:8][None], s5[1, 0:8][None])
```
